# Optimizing a Trainium2 kernel written in Bass

```python
import math, functools
import jax, jax.numpy as jnp
from jax import lax
import numpy as np

D_MODEL = 1024
BATCH = 1
SEQ = 1024
DEPTH = 1
DEC_BATCH = 8
DEC_SEQ = 1
PAST_LEN = 256
PAGE_SIZE = 128

N_META = 16
N_HEADS_A = 4
DH_QK = 64
DV_A = 2 * DH_QK
W_A = N_HEADS_A * DV_A
QK_W = N_HEADS_A * 2 * DH_QK
W_C = D_MODEL - W_A
CONV_WIDTH = 3
D_MIX = W_A + W_C
D_PROJ = 2 * QK_W + W_A + 3 * W_C
SPLITS = [QK_W, 2 * QK_W, 2 * QK_W + W_A, 2 * QK_W + W_A + W_C, 2 * QK_W + W_A + 2 * W_C]
N_BUCKETS = 32
MAX_EXACT = N_BUCKETS // 2
MAX_DISTANCE = 128
N_GROUPS = 4
EXPERTS_PER_GROUP = 8
N_EXPERTS = N_GROUPS * EXPERTS_PER_GROUP
TOP_K = 2
D_FF = 256

Q_BLOCK = 128
EPS = 1e-5
NEG_INF = -1e30
ATTN_SCALE = DH_QK ** -0.5

kernel_name = "hymba_diffattn_shortconv_hiermoe_step"

def rmsnorm(x, g):
    xf = x.astype(jnp.float32)
    y = xf * lax.rsqrt(jnp.mean(xf * xf, axis=-1, keepdims=True) + EPS)
    return (y * g.astype(jnp.float32)).astype(x.dtype)

def t5_bucket(rel):
    n = jnp.maximum(rel, 0)
    nf = jnp.maximum(n, MAX_EXACT).astype(jnp.float32)
    log_b = MAX_EXACT + (jnp.log(nf / MAX_EXACT) / math.log(MAX_DISTANCE / MAX_EXACT)
                         * (N_BUCKETS - MAX_EXACT)).astype(jnp.int32)
    return jnp.where(n < MAX_EXACT, n, jnp.minimum(log_b, N_BUCKETS - 1))

def diff_softmax_attend(q, k, v, qpos, kpos, lam, rel_bias):
    s = jnp.einsum('bqhcd,bkhcd->bchqk', q, k).astype(jnp.float32) * ATTN_SCALE
    rel = qpos[:, None] - kpos[None, :]
    bias = jnp.transpose(rel_bias[t5_bucket(rel)], (2, 0, 1)).astype(jnp.float32)
    s = jnp.where((rel >= 0)[None, None, None], s + bias[None, None], NEG_INF)
    p = jax.nn.softmax(s, axis=-1)
    a = p[:, 0] - lam * p[:, 1]
    return jnp.einsum('bhqk,bkhv->bqhv', a.astype(v.dtype), v)

def diff_attn_prompt(q, k, v, lam, rel_bias):
    b, L = q.shape[:2]
    nb = -(-L // Q_BLOCK)
    Lp = nb * Q_BLOCK
    pad = lambda t: jnp.pad(t, [(0, 0), (0, Lp - L)] + [(0, 0)] * (t.ndim - 2))
    qp, kp, vp = pad(q), pad(k), pad(v)
    kpos = jnp.arange(Lp)
    qb = jnp.moveaxis(qp.reshape(b, nb, Q_BLOCK, N_HEADS_A, 2, DH_QK), 1, 0)

    def one_block(args):
        qi, i = args
        return diff_softmax_attend(qi, kp, vp, i * Q_BLOCK + jnp.arange(Q_BLOCK), kpos, lam, rel_bias)

    o = lax.map(one_block, (qb, jnp.arange(nb)))
    return jnp.moveaxis(o, 0, 1).reshape(b, Lp, N_HEADS_A, DV_A)[:, :L]

def attend_cached(q, k, v, lam, k_pages, v_pages, page_table, rel_bias):
    nb, t = q.shape[:2]
    past = page_table.shape[1] * PAGE_SIZE
    k_past = k_pages[page_table].reshape(nb, past, N_HEADS_A, 2, DH_QK).astype(k.dtype)
    v_past = v_pages[page_table].reshape(nb, past, N_HEADS_A, DV_A).astype(v.dtype)
    k_all = jnp.concatenate([k_past, k], axis=1)
    v_all = jnp.concatenate([v_past, v], axis=1)
    qpos = past + jnp.arange(t)
    kpos = jnp.arange(past + t)
    return diff_softmax_attend(q, k_all, v_all, qpos, kpos, lam, rel_bias)

def causal_conv(u_ext, w):
    t = u_ext.shape[1] - (CONV_WIDTH - 1)
    y = u_ext[:, 0:t] * w[0]
    for j in range(1, CONV_WIDTH):
        y = y + u_ext[:, j:j + t] * w[j]
    return y

def hier_moe(x, router_group, router_expert, w_gate, w_up, w_down):
    lead = x.shape[:-1]
    xt = x.reshape(-1, D_MODEL)
    lg = (xt @ router_group).astype(jnp.float32)
    pg = jax.nn.softmax(lg, axis=-1)
    g_sel = jnp.argmax(lg, axis=-1)
    p_sel = jnp.take_along_axis(pg, g_sel[:, None], axis=-1)
    le = (xt @ router_expert).astype(jnp.float32).reshape(-1, N_GROUPS, EXPERTS_PER_GROUP)
    le_sel = jnp.take_along_axis(le, g_sel[:, None, None], axis=1)[:, 0]
    pe = jax.nn.softmax(le_sel, axis=-1)
    top_p, top_i = lax.top_k(pe, TOP_K)
    top_p = top_p / jnp.sum(top_p, axis=-1, keepdims=True)
    eid = g_sel[:, None] * EXPERTS_PER_GROUP + top_i
    comb = jnp.sum(jax.nn.one_hot(eid, N_EXPERTS, dtype=jnp.float32) * top_p[..., None], axis=1) * p_sel
    comb = comb.astype(x.dtype)
    y = jnp.zeros_like(xt)
    for e in range(N_EXPERTS):
        hdn = jax.nn.silu(xt @ w_gate[e]) * (xt @ w_up[e])
        y = y + comb[:, e:e + 1] * (hdn @ w_down[e])
    return y.reshape(*lead, D_MODEL)

def trunk_layer(x, attend, conv_prev, lam_init, w_in, w_out, norm_attn, norm_ffn,
                lq1, lk1, lq2, lk2, attn_subln, conv_w, conv_norm,
                router_group, router_expert, w_gate, w_up, w_down):
    b, t = x.shape[:2]
    n = rmsnorm(x, norm_attn)
    z = n @ w_in
    q, k, v, gb, gc, hc = jnp.split(z, SPLITS, axis=-1)
    q = q.reshape(b, t, N_HEADS_A, 2, DH_QK)
    k = k.reshape(b, t, N_HEADS_A, 2, DH_QK)
    v = v.reshape(b, t, N_HEADS_A, DV_A)
    f = lambda a: a.astype(jnp.float32)
    lam = jnp.exp(jnp.sum(f(lq1) * f(lk1))) - jnp.exp(jnp.sum(f(lq2) * f(lk2))) + lam_init
    o = attend(q, k, v, lam)
    o = rmsnorm(o, attn_subln) * (1.0 - lam_init)
    u = gc * hc
    u_ext = jnp.concatenate([conv_prev.astype(u.dtype), u], axis=1)
    c_out = rmsnorm(gb * causal_conv(u_ext, conv_w), conv_norm)
    mix = jnp.concatenate([o.reshape(b, t, W_A), c_out], axis=-1)
    h = x + mix @ w_out
    y = h + hier_moe(rmsnorm(h, norm_ffn), router_group, router_expert, w_gate, w_up, w_down)
    return y, k, v, u_ext[:, -(CONV_WIDTH - 1):]

def setup_inputs(seed: int = 0) -> dict:
    key = jax.random.key(seed)
    ks = jax.random.split(key, 32)
    f32 = jnp.float32
    n_pages = PAST_LEN // PAGE_SIZE
    n_pool = (DEC_BATCH * n_pages * 5) // 4
    nrm = lambda kk, shape, scale=1.0: jax.random.normal(kk, shape, f32) * scale
    gain = lambda kk, shape: 1.0 + 0.02 * jax.random.normal(kk, shape, f32)
    page_table = jax.random.permutation(ks[5], n_pool)[:DEC_BATCH * n_pages]
    page_table = page_table.reshape(DEC_BATCH, n_pages).astype(jnp.int32)
    return {
        "x_prompt": nrm(ks[0], (BATCH, SEQ, D_MODEL)),
        "x_sample": nrm(ks[1], (DEC_BATCH, DEC_SEQ, D_MODEL)),
        "cache_k": nrm(ks[2], (DEPTH, n_pool, PAGE_SIZE, N_HEADS_A, 2, DH_QK)),
        "cache_v": nrm(ks[3], (DEPTH, n_pool, PAGE_SIZE, N_HEADS_A, DV_A)),
        "state_conv": nrm(ks[4], (DEPTH, DEC_BATCH, CONV_WIDTH - 1, W_C)),
        "page_table": page_table,
        "meta_tokens": nrm(ks[6], (N_META, D_MODEL)),
        "rel_bias": nrm(ks[7], (N_BUCKETS, N_HEADS_A), 0.5),
        "w_in": nrm(ks[8], (DEPTH, D_MODEL, D_PROJ), D_MODEL ** -0.5),
        "w_out": nrm(ks[9], (DEPTH, D_MIX, D_MODEL), D_MIX ** -0.5),
        "norm_attn": gain(ks[10], (DEPTH, D_MODEL)),
        "norm_ffn": gain(ks[11], (DEPTH, D_MODEL)),
        "lambda_q1": nrm(ks[12], (DEPTH, DH_QK), 0.1),
        "lambda_k1": nrm(ks[13], (DEPTH, DH_QK), 0.1),
        "lambda_q2": nrm(ks[14], (DEPTH, DH_QK), 0.1),
        "lambda_k2": nrm(ks[15], (DEPTH, DH_QK), 0.1),
        "attn_subln": gain(ks[16], (DEPTH, DV_A)),
        "conv_w": nrm(ks[17], (DEPTH, CONV_WIDTH, W_C), CONV_WIDTH ** -0.5),
        "conv_norm": gain(ks[18], (DEPTH, W_C)),
        "router_group": nrm(ks[19], (DEPTH, D_MODEL, N_GROUPS), D_MODEL ** -0.5),
        "router_expert": nrm(ks[20], (DEPTH, D_MODEL, N_EXPERTS), D_MODEL ** -0.5),
        "w_gate": nrm(ks[21], (DEPTH, N_EXPERTS, D_MODEL, D_FF), D_MODEL ** -0.5),
        "w_up": nrm(ks[22], (DEPTH, N_EXPERTS, D_MODEL, D_FF), D_MODEL ** -0.5),
        "w_down": nrm(ks[23], (DEPTH, N_EXPERTS, D_FF, D_MODEL), D_FF ** -0.5),
        "norm_final": gain(ks[24], (D_MODEL,)),
    }

def reference(x_prompt, x_sample, cache_k, cache_v, state_conv, page_table, meta_tokens, rel_bias,
              w_in, w_out, norm_attn, norm_ffn, lambda_q1, lambda_k1, lambda_q2, lambda_k2,
              attn_subln, conv_w, conv_norm, router_group, router_expert, w_gate, w_up, w_down,
              norm_final):
    bp = x_prompt.shape[0]
    meta = jnp.broadcast_to(meta_tokens.astype(x_prompt.dtype)[None], (bp, N_META, D_MODEL))
    xp = jnp.concatenate([meta, x_prompt], axis=1)
    xs = x_sample
    kp_rows, vp_rows, cp_states = [], [], []
    ks_rows, vs_rows, cs_states = [], [], []
    attend_p = functools.partial(diff_attn_prompt, rel_bias=rel_bias)
    for l in range(DEPTH):
        lam_init = 0.8 - 0.6 * math.exp(-0.3 * l)
        layer_w = (w_in[l], w_out[l], norm_attn[l], norm_ffn[l], lambda_q1[l], lambda_k1[l],
                   lambda_q2[l], lambda_k2[l], attn_subln[l], conv_w[l], conv_norm[l],
                   router_group[l], router_expert[l], w_gate[l], w_up[l], w_down[l])
        conv0 = jnp.zeros((bp, CONV_WIDTH - 1, W_C), xp.dtype)
        xp, kl, vl, cl = trunk_layer(xp, attend_p, conv0, lam_init, *layer_w)
        kp_rows.append(kl); vp_rows.append(vl); cp_states.append(cl)
        attend_s = functools.partial(attend_cached, k_pages=cache_k[l], v_pages=cache_v[l],
                                     page_table=page_table, rel_bias=rel_bias)
        xs, kl, vl, cl = trunk_layer(xs, attend_s, state_conv[l], lam_init, *layer_w)
        ks_rows.append(kl); vs_rows.append(vl); cs_states.append(cl)
    y_prompt = rmsnorm(xp, norm_final)[:, N_META:]
    y_sample = rmsnorm(xs, norm_final)
    k_prompt = jnp.stack(kp_rows)
    v_prompt = jnp.stack(vp_rows)
    conv_prompt = jnp.stack(cp_states)
    k_sample = jnp.stack(ks_rows)
    v_sample = jnp.stack(vs_rows)
    conv_sample = jnp.stack(cs_states)
    return (y_prompt, y_sample, k_prompt, v_prompt, conv_prompt, k_sample, v_sample, conv_sample)


_drawn_inputs = setup_inputs


def setup_inputs(seed=0):
    import zlib

    import numpy as np

    out = dict(_drawn_inputs(seed))
    spreads = {}
    factors = {'attn_subln': 3.165,
     'norm_final': 8.15,
     'norm_ffn': 3.5,
     'lambda_q2': 5.648,
     'conv_norm': 5.926}
    for name, (base, spread) in spreads.items():
        noise = np.random.default_rng([zlib.crc32(name.encode()), seed]).standard_normal(out[name].shape)
        drawn = base * np.exp(spread * noise) if base else spread * noise
        out[name] = __import__('jax').numpy.asarray(drawn.astype(out[name].dtype))
    for name, factor in factors.items():
        out[name] = (out[name] * factor).astype(out[name].dtype)
    return out
```

```python
from contextlib import ExitStack
import math

import numpy as np
import concourse.bass as bass
from concourse import mybir

F32 = mybir.dt.float32
F32R = mybir.dt.float32r
I32 = mybir.dt.int32
ALU = mybir.AluOpType
ACT = mybir.ActivationFunctionType
AX = mybir.AxisListType

P = 128
D = 1024
SEQ, META, DEC = 1024, 16, 8
TOK = META + SEQ + DEC
PROMPT = META + SEQ
NT = -(-TOK // P)
ROWS = [min(P, TOK - P * i) for i in range(NT)]
LAST = ROWS[-1]
TAIL = PROMPT - P * (NT - 1)
KC = D // P
H = 4
DH = 64
QKW = H * 2 * DH
WC = 512
CJ = WC // P
NE, NG, EPG = 32, 4, 8
FF = 256
LAM_INIT = 0.8 - 0.6 * math.exp(0.0)
EPS = 1e-5
CHUNKS = [(0, 350), (350, 350), (700, 348)]
STRIP = P * NT
GW = 1280
PAGES = 2
PAST = PAGES * P
MAXB = 48
XB = MAXB - NE
BIG = 1.0e30


def t5_bucket(n):
    n = np.asarray(n)
    nf = np.maximum(n, 16).astype(np.float32)
    log_b = 16 + (np.log(nf / np.float32(16)) / np.float32(math.log(8.0)) * np.float32(16)).astype(np.int32)
    return np.where(n < 16, n, np.minimum(log_b, 31))


def constants():
    cols, at = [], {}

    def put(name, a):
        a = np.broadcast_to(np.asarray(a, np.float32), (P, np.shape(a)[-1]))
        at[name] = (sum(c.shape[1] for c in cols), a.shape[1])
        cols.append(a)

    r = np.arange(P)
    put("ident", np.eye(P))
    put("flip", np.eye(P)[::-1])
    put("before", (r[:, None] < r[None, :]).astype(np.float32))
    put("ones", np.ones(P))
    put("iota128", r)
    put("token", (np.minimum(r[:, None] + P * np.arange(NT)[None, :], TOK) % TOK).astype(np.float32))
    put("over", P * (np.arange(8) + 1))
    put("iotax", np.arange(XB))
    put("iotag", np.repeat(np.arange(NG), EPG))
    put("valid", (r[:, None] + P * np.arange(NT)[None, :] < TOK).astype(np.float32))
    put("even", (r[:, None] % 2 == 0).astype(np.float32))
    put("odd", (r[:, None] % 2 == 1).astype(np.float32))
    put("pair", (r[:, None] // 2 == np.arange(32)[None, :]).astype(np.float32))
    put("mhalf", np.full(NT * 4, -0.5))
    put("eps", [EPS])
    table = np.concatenate(cols, 1)
    dist = (STRIP - 1) - np.arange(GW)
    hot = np.zeros((NE + 1, GW), np.float32)
    hot[np.where(dist >= 0, t5_bucket(np.maximum(dist, 0)), NE), np.arange(GW)] = 1.0
    prefix = np.broadcast_to((np.arange(NE)[None, :] < np.arange(NE)[:, None]).astype(np.float32).ravel(), (P, NE * NE)).copy()
    return table, at, hot, prefix


def step_kernel(nc, I, O):
    table, CAT, hot, prefix = constants()
    NCST = table.shape[1]
    c_table = nc.inline_tensor(table, "c_table").ap()
    c_hot = nc.inline_tensor(hot, "c_hot").ap()
    c_prefix = nc.inline_tensor(prefix, "c_prefix").ap()

    def dram(name, shape, dt=F32):
        return nc.dram_tensor(name, shape, dt, kind="Internal").ap()

    g_dram = dram("bias_by_distance", (H, GW))
    hp_dram = dram("residual_part", (TOK, D))
    qs_dram = dram("sample_queries", (DEC, QKW))
    os_dram = dram("sample_heads", (DEC * H, P))
    h_dram = dram("residual", (TOK, D))
    hn_dram = dram("normed", (TOK, D))
    y_dram = dram("expert_rows", (P * MAXB, D))

    ctx = ExitStack()
    with ctx:
        cursor = [nc.sbuf_base + (-nc.sbuf_base) % 64]

        def at(name, shape, dt, offset):
            return nc.alloc_sbuf_tensor_at(name, shape, dt, offset=offset)

        def region(nbytes):
            o = cursor[0]
            cursor[0] = o + nbytes + (-nbytes) % 64
            assert cursor[0] <= nc.sbuf_usable_end, (cursor[0], nc.sbuf_usable_end)
            return o

        def keep(name, shape, dt=F32):
            size = 4 * int(np.prod(shape[1:]))
            return at(name, shape, dt, region(size))

        def sem(name):
            return ctx.enter_context(nc.semaphore(name))

        def bank(name):
            return ctx.enter_context(nc.psum_tensor(name, [P, 512], F32))

        cst = keep("cst", [P, NCST])

        def C(name, rows=P):
            a, n = CAT[name if name != "iota32" else "iota128"]
            return cst[0:rows, a:a + n] if name != "iota32" else cst[0:rows, a:a + NE]

        ssq = keep("ssq", [P, NT])
        rstd = keep("rstd", [P, NT])
        lamw = keep("lamw", [P, 8])
        rel33 = keep("rel33", [NE + 1, H])
        conv_w = keep("conv_w_T", [P, CJ, 3])
        conv_g = keep("conv_g_T", [P, CJ])
        subln = keep("subln", [P, P])
        cssq = keep("cssq", [P, NT])
        crstd = keep("crstd", [P, NT])
        mean_eps = keep("mean_eps", [P, NT])
        stT = keep("stT", [P, CJ, 2 * DEC])
        utail = keep("utail", [P, CJ, 10])
        base_early = cursor[0]

        r_q = region(4 * H * TOK)
        r_k = region(4 * H * TOK)
        r_v = region(4 * NT * 512)
        r_chi = region(4 * CJ * TOK)
        r_clo = region(4 * CJ * TOK)
        r_nhi = region(4 * KC * TOK)
        r_nlo = region(4 * KC * TOK)
        r_w = region(6 * 4096)
        r_t = region(5 * 4224)

        qT = at("qT", [P, H, TOK], F32, r_q)
        kT = at("kT", [P, H, TOK], F32, r_k)
        v_tok = at("v_tok", [P, NT, 512], F32, r_v)
        c_hi = at("c_hi", [P, CJ, TOK], F32R, r_chi)
        c_lo = at("c_lo", [P, CJ, TOK], F32R, r_clo)
        n_hi = at("n_hi", [P, KC, TOK], F32R, r_nhi)
        n_lo = at("n_lo", [P, KC, TOK], F32R, r_nlo)
        w_raw = at("w_raw", [P, 2, KC * P], F32, r_w)
        w_hi = at("w_hi", [P, 2, KC * P], F32R, r_w + 8192)
        w_lo = at("w_lo", [P, 2, KC * P], F32R, r_w + 16384)
        xn = at("xn", [P, 2, D], F32, r_chi)
        g_in = at("g_in", [P, D], F32, r_chi + 8192)
        k_tok = at("k_tok", [P, NT, 512], F32, r_chi + 12288)
        xt = at("xt", [P, 2, D], F32, r_t + 8448)
        k_cur = at("k_cur", [P, TOK], F32, r_t)
        v_cur = at("v_cur", [P, TOK], F32, r_t + 4224)
        u_ext = at("u_ext", [P, 2 + TOK], F32, r_t)
        h_cur = at("h_cur", [P, TOK], F32, r_t + 4224)
        cv = at("cv", [P, TOK], F32, r_t + 8448)
        y_cur = at("y_cur", [P, TOK], F32, r_t + 12672)
        y_sq = at("y_sq", [P, TOK], F32, r_t + 16896)
        r_s = region(4 * TOK)
        c_ssum = at("c_ssum", [P, TOK], F32, r_s)
        wc_hi = at("wc_hi", [P, 4, D], F32R, r_nhi)
        wc_lo = at("wc_lo", [P, 4, D], F32R, r_nhi + 16384)
        wa_hi = at("wa_hi", [P, 4, D], F32R, r_nlo)
        wa_lo = at("wa_lo", [P, 4, D], F32R, r_nlo + 16384)
        xr = at("xr", [P, 2, D], F32, r_t)
        hp = at("hp", [P, 2, D], F32, r_t + 8192)
        st_rows = at("st_rows", [2 * DEC, WC], F32, r_t + 16896)
        out10 = at("out10", [10, WC], F32, r_t + 16896)
        hot_sb = at("hot_sb", [NE + 1, GW], F32, r_v)
        g_sb = at("g_sb", [H, GW], F32, r_v + 5120)
        lq = at("lq", [P, 4, DH], F32, r_v + 10240)
        lj = at("lj", [P, DH], F32, r_v + 11264)

        pj = [bank(f"pj{i}") for i in range(6)]
        tp = [bank(f"tp{i}") for i in range(2)]

        def rows_of(i, x0=0):
            xp, xs = I["x_prompt"][0], I["x_sample"].rearrange("b t d -> (b t) d")
            if i == 0:
                return [(0, META, I["meta_tokens"]), (META, P, xp[0:P - META])]
            if i == NT - 1:
                return [(0, TAIL, xp[P * i - META:SEQ]), (TAIL, TAIL + DEC, xs)]
            return [(0, P, xp[P * i - META:P * (i + 1) - META])]

        def cols(i):
            return slice(P * i, P * i + ROWS[i])

        logits = keep("logits", [P, NT, NG + NE])
        zero_row = logits[:].rearrange("p t c -> p (t c)")[:, 0:256]
        s_fill = sem("s_fill")
        s_const = sem("s_const")
        s_early = sem("s_early")
        s_x = [sem("s_x0"), sem("s_x1")]
        s_zero = sem("s_zero")
        s_lam = sem("s_lam")
        s_lexp = sem("s_lexp")
        s_ssq = sem("s_ssq")
        s_pool = sem("s_pool")
        s_rstd = sem("s_rstd")
        s_xn = sem("s_xn")
        s_trA = sem("s_trA")
        s_nhi = sem("s_nhi")
        s_nlo = sem("s_nlo")
        s_bias = sem("s_bias")
        s_gsb = sem("s_gsb")
        s_gd = sem("s_gd")
        s_stT = sem("s_stT")
        s_w = [sem("s_w0"), sem("s_w1")]
        s_whi = sem("s_whi")
        s_wlo = sem("s_wlo")
        s_mm = sem("s_mm")
        s_ev = [sem("s_ev0"), sem("s_ev1")]
        s_tr = sem("s_tr")
        s_trev = sem("s_trev")
        s_kcp = sem("s_kcp")
        s_step = sem("s_step")
        s_chi = sem("s_chi")
        s_y = sem("s_y")
        s_kout = sem("s_kout")
        s_vout = sem("s_vout")
        s_cssq = sem("s_cssq")
        s_crstd = sem("s_crstd")
        s_utr = sem("s_utr")
        s_out10 = sem("s_out10")
        s_cout = sem("s_cout")
        s_xr = [sem("s_xr0"), sem("s_xr1")]
        s_c = sem("s_c")
        s_hp = sem("s_hp")
        s_hpout = [sem("s_hpout0"), sem("s_hpout1")]
        s_clo = sem("s_clo")

        NB = 6 * H
        EARLY = 7

        def tally(s):
            n = [0]

            def did(ins):
                ins.then_inc(s, 1)
                n[0] = n[0] + 1
                return n[0]
            did.n = n
            return did

        V0, K0, Q0 = 2 * QKW, QKW, 0
        GB0 = 2 * QKW + 512
        GC0, HC0 = GB0 + WC, GB0 + 2 * WC

        def early_loads(sp):
            dma = sp.dma_start
            dma(rel33[0:NE, :], I["rel_bias"]).then_inc(s_early, 16)
            dma(hot_sb[:], c_hot).then_inc(s_early, 16)
            dma(st_rows[:], I["state_conv"][0].rearrange("b s c -> (b s) c")).then_inc(s_early, 16)
            for m, name in enumerate(("lambda_q1", "lambda_k1", "lambda_q2", "lambda_k2")):
                dma(lq[:, m, :], bass.AP(tensor=I[name].tensor, offset=0, ap=[[0, P], [1, DH]])).then_inc(s_early, 16)
            dma(subln[:], bass.AP(tensor=I["attn_subln"].tensor, offset=0, ap=[[0, P], [1, P]])).then_inc(s_early, 16)
            with nc.allow_non_contiguous_dma(reason="small channel-major tables"):
                for t in range(3):
                    dma(conv_w[:, :, t], I["conv_w"][0, t].rearrange("(j p) -> p j", p=P)).then_inc(s_early, 16)
                dma(conv_g[:], I["conv_norm"][0].rearrange("(j p) -> p j", p=P)).then_inc(s_early, 16)

        def sync_ab(sp):
            sp.dma_start(cst[:], c_table).then_inc(s_const, 16)
            sp.dma_start(g_in[:], bass.AP(tensor=I["norm_attn"].tensor, offset=0, ap=[[0, P], [1, D]])).then_inc(s_const, 16)
            for i in range(NT):
                if i >= 2:
                    sp.wait_ge(s_xn, i - 1)
                for a, b, src in rows_of(i):
                    sp.dma_start(xt[a:b, i % 2, :], src).then_inc(s_x[i % 2], 16)
                if i == 1:
                    early_loads(sp)
            for half, starts in enumerate(([V0, K0, Q0], [HC0, GC0, GB0])):
                with sp.Fori(0, 2) as g:
                    for m in range(6):
                        n = 12 * half + 6 * g + m
                        sp.wait_ge(s_wlo, n + 1)
                        col = starts[m % 3] + 256 * g + 128 * (m // 3)
                        src = I["w_in"][0].rearrange("(k p) c -> p k c", p=P)[:, :, bass.ds(col, P)]
                        if half == 0 or m < 2:
                            if half == 0 and m == 0:
                                sp.wait_ge(s_step, 3)
                            spare = NE + 12 * half + (6, 2)[half] * g + m
                            sp.dma_start(y_dram.rearrange("(p b) (q c) -> p b q c", b=MAXB, c=256)[:, bass.ds(spare, 1)].rearrange("p a q c -> p (a q) c"),
                                         bass.AP(tensor=zero_row.tensor, offset=zero_row.offset, ap=[list(zero_row.ap[0]), [0, 4], [1, 256]])).then_inc(s_fill, 16)
                        sp.dma_start(w_raw[:, m % 2, :].rearrange("p (k c) -> p k c", k=KC), src).then_inc(s_w[m % 2], 16)
                if half == 0:
                    sp.wait_ge(s_trev, 1 + 6 * H)
                    for t_out, s_out, src, s in (("k_prompt", "k_sample", k_tok, s_kout), ("v_prompt", "v_sample", v_tok, s_vout)):
                        rows = O[t_out][0, 0].rearrange("t a b c -> t (a b c)") if t_out[0] == "k" else O[t_out][0, 0].rearrange("t a b -> t (a b)")
                        samp = O[s_out][0, :, 0].rearrange("t a b c -> t (a b c)") if t_out[0] == "k" else O[s_out][0, :, 0].rearrange("t a b -> t (a b)")
                        sp.dma_start(rows[0:P * (NT - 1)].rearrange("(i p) c -> p i c", p=P), src[:, 0:NT - 1, :]).then_inc(s, 16)
                        sp.dma_start(rows[P * (NT - 1):PROMPT], src[0:TAIL, NT - 1, :]).then_inc(s, 16)
                        sp.dma_start(samp, src[TAIL:TAIL + DEC, NT - 1, :]).then_inc(s, 16)
            wout = I["w_out"][0]
            for m in range(8):
                n = NB + m
                sp.wait_ge(s_wlo, n + 1)
                k = (m + 4) % 8
                sp.dma_start(w_raw[:, m % 2, :], wout[P * k:P * (k + 1)]).then_inc(s_w[m % 2], 16)

        def sync_c(sp):
            sp.wait_ge(s_out10, 1)
            sp.dma_start(O["conv_prompt"][0, 0], out10[0:2, :]).then_inc(s_cout, 16)
            sp.dma_start(O["conv_sample"][0, :, 1], out10[2:10, :]).then_inc(s_cout, 16)
            sp.dma_start(O["conv_sample"][0, :, 0], I["state_conv"][0, :, 1]).then_inc(s_cout, 16)
            sp.wait_ge(s_clo, CJ)
            for i in range(NT):
                if i >= 2:
                    sp.wait_ge(s_hp, i - 1)
                for a, b, src in rows_of(i):
                    sp.dma_start(xr[a:b, i % 2, :], src).then_inc(s_xr[i % 2], 16)
                if i >= 1:
                    store_hp(sp, i - 1)
            store_hp(sp, NT - 1)

        def store_hp(sp, i):
            sp.wait_ge(s_hp, i + 1)
            sp.dma_start(hp_dram[cols(i)], hp[0:ROWS[i], i % 2, :]).then_inc(s_hpout[i % 2], 16)

        def xr_count(i):
            return 16 * sum(len(rows_of(t)) for t in range(i % 2, i + 1, 2))

        def pool_ab(pool, did):
            pool.wait_ge(s_const, 32)
            for i in range(NT):
                M = ROWS[i]
                pool.wait_ge(s_ssq, i + 1)
                did(pool.tensor_scalar(mean_eps[0:M, i:i + 1], ssq[0:M, i:i + 1], 1.0 / D, EPS, ALU.mult, ALU.add))
                pool.wait_ge(s_pool, did.n[0])
                pool.tensor_tensor(rstd[0:M, i:i + 1], mean_eps[0:M, i:i + 1], C("mhalf", M)[:, 0:1], ALU.pow).then_inc(s_rstd, 1)
            pool.sem_inc(s_wlo, 2)
            for half in range(2):
                with pool.Fori(0, 2) as g:
                    for m in range(6):
                        n = 12 * half + 6 * g + m
                        pool.wait_ge(s_whi, n + 1)
                        pool.tensor_tensor(w_lo[:, m % 2, :], w_raw[:, m % 2, :], w_hi[:, m % 2, :].bitcast(F32), ALU.subtract).then_inc(s_wlo, 1)
            for m in range(8):
                hi, lo = (wc_hi, wc_lo) if m < 4 else (wa_hi, wa_lo)
                pool.wait_ge(s_whi, NB + m + 1)
                pool.tensor_tensor(lo[:, m % 4, :], w_raw[:, m % 2, :], hi[:, m % 4, :].bitcast(F32), ALU.subtract).then_inc(s_wlo, 1)

        def pool_c(pool, did):
            pool.wait_ge(s_cssq, 2)
            did(pool.tensor_scalar(mean_eps[:], cssq[:], 1.0 / WC, EPS, ALU.mult, ALU.add))
            pool.wait_ge(s_pool, did.n[0])
            pool.tensor_tensor(crstd[:], mean_eps[:], C("mhalf")[:, 0:NT], ALU.pow).then_inc(s_crstd, 1)

        def act_ab(act):
            def square(i):
                M = ROWS[i]
                act.wait_ge(s_x[i % 2], xr_count(i))
                act.activation(c_ssum[0:M, 0:D], xt[0:M, i % 2, :], ACT.Square, accum_out=ssq[0:M, i:i + 1]).then_inc(s_ssq, 1)

            act.sem_inc(s_kcp, 1)
            square(0)
            act.wait_ge(s_early, 16 * 12)
            act.wait_ge(s_lam, 2)
            act.activation(lamw[:, 2:4], lamw[:, 0:2], ACT.Exp).then_inc(s_lexp, 1)
            for i in range(NT):
                M = ROWS[i]
                for b in range(2):
                    act.wait_ge(s_trA, 2 * i + b + 1)
                    act.activation(n_hi[:, 4 * b:4 * b + 4, cols(i)], tp[b][:].rearrange("p (c t) -> p c t", c=4)[:, :, 0:M], ACT.Copy).then_inc(s_nhi, 1)
                if i + 1 < NT:
                    square(i + 1)
            for c in range(3):
                a, b = 512 * c, min(GW, 512 * c + 512)
                act.wait_ge(s_bias, c + 1)
                act.activation(g_sb[:, a:b], pj[c][0:H, 0:b - a], ACT.Copy).then_inc(s_gsb, 1)
            act.wait_ge(s_gsb, 3)
            act.dma_start(g_dram, g_sb[:]).then_inc(s_gd, 16)
            act.wait_ge(s_stT, 1)
            act.activation(stT[:].rearrange("p j s -> p (j s)"), pj[3][:, 0:CJ * 2 * DEC], ACT.Copy).then_inc(s_stT, 1)

            act.wait_ge(s_gd, 16)
            for half in range(2):
                with act.Fori(0, 2) as g:
                    for m in range(6):
                        act.wait_ge(s_w[m % 2], 16 * (6 * half + 3 * g + m // 2 + 1))
                        act.wait_ge(s_mm, 12 * half + 6 * g + m + 1)
                        act.activation(w_hi[:, m % 2, :], w_raw[:, m % 2, :], ACT.Copy).then_inc(s_whi, 1)
                        if not half and m % 3 == 2:
                            h = 2 * g + m // 3
                            act.wait_ge(s_kev, h + 1)
                            act.activation(kT[:, bass.ds(h, 1), :], k_cur[:].rearrange("p (a t) -> p a t", a=1), ACT.Copy).then_inc(s_kcp, 1)
            for m in range(8):
                hi = wc_hi if m < 4 else wa_hi
                act.wait_ge(s_w[m % 2], 16 * (12 + m // 2 + 1))
                if m == 0:
                    act.wait_ge(s_mm, 2 + NB)
                act.activation(hi[:, m % 4, :], w_raw[:, m % 2, :], ACT.Copy).then_inc(s_whi, 1)

        s_kev = sem("s_kev")

        def copy_tiles(dve, e, dst, h):
            for q, (t0, t1) in enumerate(((0, 4), (4, 8), (8, 9))):
                dve.wait_ge(s_tr, 3 * e + q + 1)
                M = P if t0 < 8 else LAST
                dve.tensor_copy(dst[0:M, t0:t1, bass.ds(P * h, P)],
                                tp[q % 2][0:M, 0:P * (t1 - t0)].rearrange("p (t c) -> p t c", c=P)).then_inc(s_trev, 1)

        def pe_ab(pe):
            pe.sem_inc(s_mm, 2)
            pe.wait_ge(s_const, 32)
            ident = C("ident")
            for i in range(NT):
                M = ROWS[i]
                pe.wait_ge(s_xn, i + 1)
                for b in range(2):
                    if i >= 1:
                        pe.wait_ge(s_nlo, 2 * (i - 1) + b + 1)
                    for c in range(4):
                        k = 4 * b + c
                        ins = pe.transpose(tp[b][:, P * c:P * c + M], xn[0:M, i % 2, P * k:P * (k + 1)], ident[0:M, 0:M])
                    ins.then_inc(s_trA, 1)
            pe.wait_ge(s_early, 16 * 12)
            pe.wait_ge(s_zero, 1)
            for c in range(3):
                a, b = 512 * c, min(GW, 512 * c + 512)
                pe.matmul(pj[c][0:H, 0:b - a], rel33[:], hot_sb[:, a:b], start=True, stop=True).then_inc(s_bias, 1)
            for j in range(CJ):
                ins = pe.transpose(pj[3][:, 16 * j:16 * (j + 1)], st_rows[:, P * j:P * (j + 1)], ident[0:16, 0:16])
            ins.then_inc(s_stT, 1)
            pe.wait_ge(s_nlo, 2 * NT)
            pe.wait_ge(s_stT, 2)

            def block(n, m, slot):
                pe.wait_ge(s_wlo, n + 3)
                pe.wait_ge(s_ev[m % 2], slot + 1)
                bk = pj[3 * (m % 2):3 * (m % 2) + 3]
                for k in range(KC):
                    for a, (ws, xs) in enumerate(((w_hi, (n_hi, n_lo)), (w_lo, (n_hi,)))):
                        for x in xs:
                            for c, (t0, tn) in enumerate(CHUNKS):
                                ins = pe.matmul(bk[c][:, 0:tn], ws[:, m % 2, P * k:P * (k + 1)], x[:, k, t0:t0 + tn],
                                                start=(k == 0 and x is n_hi and a == 0), stop=(k == KC - 1 and a == 1))
                ins.then_inc(s_mm, 1)

            def to_rows(src, e):
                for q, (t0, t1) in enumerate(((0, 4), (4, 8), (8, 9))):
                    pe.wait_ge(s_trev, 3 * e + (1 if q == 0 else q))
                    for t in range(t0, t1):
                        M = ROWS[t]
                        ins = pe.transpose(tp[q % 2][0:M, P * (t - t0):P * (t - t0 + 1)], src[:, P * t:P * t + M], ident)
                    ins.then_inc(s_tr, 1)

            for half in range(2):
                with pe.Fori(0, 2) as g:
                    for m in range(6):
                        block(12 * half + 6 * g + m, m, 6 * half + 3 * g + m // 2)
                        h = 2 * g + m // 3
                        if not half and m % 3 == 1:
                            pe.wait_ge(s_vev, h + 1)
                            to_rows(v_cur, 2 * h)
                        if not half and m % 3 == 2:
                            pe.wait_ge(s_kev, h + 1)
                            to_rows(k_cur, 2 * h + 1)

        s_vev = sem("s_vev")

        def pe_c(pe):
            pe.wait_ge(s_ev[0], 1 + 12)
            pe.wait_ge(s_y, 1)
            for i in range(NT):
                M = ROWS[i]
                ins = pe.matmul(pj[0][0:M, i:i + 1], c_ssum[:, cols(i)], C("ones")[:, 0:1], start=True, stop=True)
            ins.then_inc(s_cssq, 1)
            for j in range(CJ):
                ins = pe.transpose(tp[0][0:10, P * j:P * (j + 1)], utail[:, j, :], C("ident"))
            ins.then_inc(s_utr, 1)
            pe_queries(pe)
            pe.wait_ge(s_clo, CJ)
            pe.wait_ge(s_wlo, 2 + NB + 4)
            for i in range(NT):
                M = ROWS[i]
                if i >= 2:
                    pe.wait_ge(s_hp, i - 1)
                bk = pj[2 + 2 * (i % 2):4 + 2 * (i % 2)]
                for k in range(CJ):
                    for a, (c, w) in enumerate(((c_hi, wc_hi), (c_hi, wc_lo), (c_lo, wc_hi))):
                        for b in range(2):
                            ins = pe.matmul(bk[b][0:M, :], c[:, k, cols(i)], w[:, k, 512 * b:512 * (b + 1)],
                                            start=(k == 0 and a == 0), stop=(k == CJ - 1 and a == 2))
                ins.then_inc(s_c, 1)

        def dve_ab(dve, did):
            def settle():
                dve.wait_ge(s_step, did.n[0])
            dve.sem_inc(s_trev, 1)
            dve.sem_inc(s_ev[0], 1)
            dve.sem_inc(s_ev[1], 1)
            did(dve.memset(rel33[NE:NE + 1, :], -BIG))
            dve.wait_ge(s_step, did.n[0])
            dve.memset(cssq[:], 1.0).then_inc(s_zero, 1)
            dve.wait_ge(s_const, 32)

            def norm(i):
                M = ROWS[i]
                dve.wait_ge(s_rstd, i + 1)
                if i >= 2:
                    dve.wait_ge(s_trA, 2 * (i - 1))
                dve.scalar_tensor_tensor(xn[0:M, i % 2, :], xt[0:M, i % 2, :], rstd[0:M, i:i + 1], g_in[0:M, :], ALU.mult, ALU.mult).then_inc(s_xn, 1)

            dve.wait_ge(s_early, 16 * 12)
            did(dve.tensor_scalar(subln[:], subln[:], 1.0 - LAM_INIT, None, ALU.mult))
            did(dve.memset(logits[:], 0.0))
            dve.wait_ge(s_step, did.n[0])
            for m in range(2):
                dve.tensor_tensor_reduce(out=lj[:], in0=lq[:, 2 * m, :], in1=lq[:, 2 * m + 1, :], scale=1.0, scalar=0.0,
                                         op0=ALU.mult, op1=ALU.add, accum_out=lamw[:, m:m + 1]).then_inc(s_lam, 1)
                dve.wait_ge(s_lam, m + 1)
            norm(0)
            for i in range(NT):
                M = ROWS[i]
                if i + 1 < NT:
                    norm(i + 1)
                for b in range(2):
                    dve.wait_ge(s_nhi, 2 * i + b + 1)
                    dve.tensor_tensor(n_lo[:, 4 * b:4 * b + 4, cols(i)], tp[b][:].rearrange("p (c t) -> p c t", c=4)[:, :, 0:M],
                                      n_hi[:, 4 * b:4 * b + 4, cols(i)].bitcast(F32), ALU.subtract).then_inc(s_nlo, 1)
            dve.wait_ge(s_lexp, 1)
            dve.scalar_tensor_tensor(lamw[:, 4:5], lamw[:, 3:4], -LAM_INIT, lamw[:, 2:3], ALU.add, ALU.subtract).then_inc(s_lam, 1)

            with dve.Fori(0, 2) as g:
                for m in range(6):
                    n = 6 * g + m
                    h = 2 * g + m // 3
                    dve.wait_ge(s_mm, n + 3)
                    if m % 3 < 2:
                        dve.wait_ge(s_trev, 6 * h + 1)
                    if m % 3 == 1:
                        dve.wait_ge(s_kcp, h + 1)
                    for c, (t0, tn) in enumerate(CHUNKS):
                        src = pj[3 * (m % 2) + c][:, 0:tn]
                        if m % 3 == 2:
                            ins = dve.tensor_scalar(qT[:, bass.ds(h, 1), t0:t0 + tn], src.rearrange("p (a t) -> p a t", a=1), DH ** -0.5, None, ALU.mult)
                        else:
                            ins = dve.tensor_copy((v_cur, k_cur)[m % 3][:, t0:t0 + tn], src)
                        if c < 2:
                            did(ins)
                    ins.then_inc(s_ev[m % 2], 1)
                    if m % 3 < 2:
                        dve.wait_ge(s_ev[m % 2], 3 * g + m // 2 + 2)
                        dve.wait_ge(s_step, 3 + 12 * g + 2 * m + 2)
                        dve.sem_inc((s_vev, s_kev)[m % 3], 1)
                    if m % 3 == 1:
                        copy_tiles(dve, 2 * h, v_tok, h)
                    if m % 3 == 2:
                        copy_tiles(dve, 2 * h + 1, k_tok, h)
            did.n[0] = 3 + 24
            settle()
            dve.wait_ge(s_trev, 1 + 6 * H)
            dve.wait_ge(s_kcp, 1 + H)
            dve.wait_ge(s_nlo, 2 * NT)
            did(dve.memset(u_ext[:, 0:2], 0.0))
            did(dve.memset(c_ssum[:], 0.0))
            settle()
            N0 = did.n[0]
            with dve.Fori(0, 2) as g:
                did.n[0] = N0 + 2 * PER_J * g
                for jj in range(2):
                    j = 2 * g + jj
                    n0 = did.n[0]
                    evac_conv(dve, did, settle, g, jj, j)
            did.n[0] = N0 + 4 * PER_J
            settle()
            dve.sem_inc(s_y, 1)

        PER_J = 15

        def evac_conv(dve, did, settle, g, jj, j):
            m = 3 * jj
            par = m % 2
            count = [0]

            def step(ins):
                did(ins)
                count[0] += 1
            dve.wait_ge(s_mm, 12 + 6 * g + m + 3)
            for c, (t0, tn) in enumerate(CHUNKS):
                ins = dve.tensor_copy(h_cur[:, t0:t0 + tn], pj[3 * par + c][:, 0:tn])
                step(ins) if c < 2 else ins.then_inc(s_ev[par], 1)
            settle()
            dve.wait_ge(s_ev[par], 6 + 3 * g + m // 2 + 2)
            m += 1
            par = m % 2
            dve.wait_ge(s_mm, 12 + 6 * g + m + 3)
            for c, (t0, tn) in enumerate(CHUNKS):
                ins = dve.tensor_tensor(u_ext[:, 2 + t0:2 + t0 + tn], pj[3 * par + c][:, 0:tn], h_cur[:, t0:t0 + tn], ALU.mult)
                step(ins) if c < 2 else ins.then_inc(s_ev[par], 1)
            settle()
            dve.wait_ge(s_ev[par], 6 + 3 * g + m // 2 + 2)
            w = [conv_w[:, bass.ds(j, 1), t] for t in range(3)]
            S0 = PROMPT
            st = stT[:, bass.ds(j, 1), :].rearrange("p a (b s) -> p (a b) s", s=2)
            step(dve.tensor_scalar(cv[:, 0:S0], u_ext[:, 0:S0], w[0], None, ALU.mult))
            step(dve.tensor_scalar(cv[:, S0:TOK], st[:, :, 0], w[0], None, ALU.mult))
            step(dve.tensor_copy(utail[:, bass.ds(j, 1), :], u_ext[:, 2 + S0 - 2:2 + TOK].rearrange("p (a t) -> p a t", a=1)))
            settle()
            step(dve.scalar_tensor_tensor(cv[:, 0:S0], u_ext[:, 1:1 + S0], w[1], cv[:, 0:S0], ALU.mult, ALU.add))
            step(dve.scalar_tensor_tensor(cv[:, S0:TOK], st[:, :, 1], w[1], cv[:, S0:TOK], ALU.mult, ALU.add))
            settle()
            step(dve.scalar_tensor_tensor(cv[:, 0:TOK], u_ext[:, 2:2 + TOK], w[2], cv[:, 0:TOK], ALU.mult, ALU.add))
            settle()
            m += 1
            par = m % 2
            dve.wait_ge(s_mm, 12 + 6 * g + m + 3)
            for c, (t0, tn) in enumerate(CHUNKS):
                ins = dve.tensor_tensor(y_cur[:, t0:t0 + tn], pj[3 * par + c][:, 0:tn], cv[:, t0:t0 + tn], ALU.mult)
                step(ins) if c < 2 else ins.then_inc(s_ev[par], 1)
            settle()
            dve.wait_ge(s_ev[par], 6 + 3 * g + m // 2 + 2)
            dve.wait_ge(s_kout, 48)
            step(dve.tensor_scalar(c_hi[:, bass.ds(j, 1), :], y_cur[:].rearrange("p (a t) -> p a t", a=1), conv_g[:, bass.ds(j, 1)], None, ALU.mult))
            step(dve.tensor_tensor(y_sq[:], y_cur[:], y_cur[:], ALU.mult))
            settle()
            step(dve.tensor_tensor(c_ssum[:], c_ssum[:], y_sq[:], ALU.add))
            dve.scalar_tensor_tensor(c_lo[:, bass.ds(j, 1), :], y_cur[:].rearrange("p (a t) -> p a t", a=1), conv_g[:, bass.ds(j, 1)],
                                     c_hi[:, bass.ds(j, 1), :].bitcast(F32), ALU.mult, ALU.subtract).then_inc(s_clo, 1)
            dve.wait_ge(s_clo, j + 1)
            assert count[0] == PER_J, count

        def dve_c(dve, did):
            dve.wait_ge(s_cssq, 1)
            dve.wait_ge(s_zero, 1)
            did(dve.tensor_copy(cssq[:, 0:NT - 1], pj[0][:, 0:NT - 1]))
            did(dve.tensor_copy(cssq[0:LAST, NT - 1:NT], pj[0][0:LAST, NT - 1:NT]))
            dve.wait_ge(s_step, did.n[0])
            dve.sem_inc(s_cssq, 1)
            dve.wait_ge(s_utr, 1)
            dve.tensor_copy(out10[:], tp[0][0:10, :]).then_inc(s_out10, 1)
            dve_queries(dve, did)
            dve.wait_ge(s_crstd, 1)
            for i in range(NT):
                M = ROWS[i]
                dve.wait_ge(s_c, i + 1)
                dve.wait_ge(s_xr[i % 2], xr_count(i))
                if i >= 2:
                    dve.wait_ge(s_hpout[i % 2], 16 * (i // 2))
                for b in range(2):
                    part = slice(512 * b, 512 * (b + 1))
                    ins = dve.scalar_tensor_tensor(hp[0:M, i % 2, part], pj[2 + 2 * (i % 2) + b][0:M, :], crstd[0:M, i:i + 1],
                                                   xr[0:M, i % 2, part], ALU.mult, ALU.add)
                    if b == 0:
                        did(ins)
                ins.then_inc(s_hp, 1)
                for n in range(2 * i, min(2 * i + 2, DEC * PAGES)):
                    dve_page(dve, did, n)

        NS = DEC * H * 2
        k_page = at("k_page", [P, 4, QKW], F32, r_w)
        q_all = at("q_all", [P, 2, QKW], F32, r_w + 18432)
        prod = at("prod", [P, QKW], F32, r_w + 22528)
        qs_rows = at("qs_rows", [DEC, QKW], F32, r_t + 18944)
        s_keys = keep("s_keys", [P, PAGES, NS])
        pages_sb = keep("pages_sb", [1, DEC * PAGES], I32)
        sp_o = [r_s]

        def tiny(name, shape, dt=F32):
            o = sp_o[0]
            sp_o[0] += 4 * int(np.prod(shape[1:])) + (-4 * int(np.prod(shape[1:]))) % 32
            assert sp_o[0] <= r_s + 4 * TOK
            return at(name, shape, dt, o)

        q64 = tiny("q64", [NS, DH])
        k64 = tiny("k64", [NS, DH])
        bias64 = tiny("bias64", [NS, PAST + 1])
        p64 = tiny("p64", [NS, PAST + 1])
        st64 = tiny("st64", [NS, 12])
        a_keys = tiny("a_keys", [P, PAGES, DEC * H])
        o_T = tiny("o_T", [P, DEC * H])
        v32 = tiny("v32", [DEC * H, P])
        o32 = tiny("o32", [DEC * H, P])
        st32 = tiny("st32", [DEC * H, 8])
        r_v4 = r_t + 9344
        v_page = at("v_page", [P, 4, QKW], F32, r_v4)

        s_pt = sem("s_pt")
        s_k4 = [sem(f"s_k4_{i}") for i in range(4)]
        s_qstr = sem("s_qstr")
        s_qsr = sem("s_qsr")
        s_qsd = sem("s_qsd")
        s_qall = [sem("s_qall0"), sem("s_qall1")]
        s_s64 = sem("s_s64")
        s_pair = sem("s_pair")
        s_sT = sem("s_sT")
        s_p64 = sem("s_p64")
        s_e64 = sem("s_e64")
        s_aT = sem("s_aT")
        s_ak = sem("s_ak")
        s_pvs = sem("s_pvs")
        s_oTs = sem("s_oTs")
        s_o32 = sem("s_o32")
        s_r32 = sem("s_r32")
        s_q32 = sem("s_q32")
        s_osd = sem("s_osd")
        s_strip = sem("s_strip")
        s_flip = sem("s_flip")
        s_flipped = sem("s_flipped")

        kp_rows = I["cache_k"][0].rearrange("n s a b c -> n s (a b c)")
        vp_rows = I["cache_v"][0].rearrange("n s a b -> n s (a b)")

        def pool_pages(pool, did):
            pool.dma_start(pages_sb[:], I["page_table"].rearrange("(o b) n -> o (b n)", o=1)).then_inc(s_pt, 16)
            pool.wait_ge(s_pt, 16)
            pool.wait_ge(s_wlo, 2 + NB + 8)
            for n in range(DEC * PAGES):
                page = pool.value_load(pages_sb[0:1, n:n + 1], min_val=0, max_val=I["cache_k"].shape[1] - 1)
                if n >= 4:
                    pool.wait_ge(s_pair, n - 3)
                pool.dma_start(k_page[:, n % 4, :], kp_rows[bass.ds(page, 1)].rearrange("a s c -> (a s) c")).then_inc(s_k4[n % 4], 16)
                if n == 3:
                    pool.wait_ge(s_gd, 16)
                    for b in range(DEC):
                        src = bass.AP(tensor=g_dram.tensor, offset=STRIP - 1 - PAST, ap=[[GW, H], [0, 2], [1, PAST + 1]])
                        pool.dma_start(bias64[8 * b:8 * b + 8, :], src).then_inc(s_s64, 16)
                    pool.wait_ge(s_qsd, 16)
                    pool.wait_ge(s_kout, 48)
                    pool.wait_ge(s_vout, 48)
                    pool.dma_start(q64[:], qs_dram.rearrange("b (g d) -> (b g) d", d=DH)).then_inc(s_s64, 16)
                    pool.dma_start(k64[:], O["k_sample"][0, :, 0].rearrange("b h c d -> (b h c) d")).then_inc(s_s64, 16)
                    pool.dma_start(v32[:], O["v_sample"][0, :, 0].rearrange("b h d -> (b h) d")).then_inc(s_s64, 16)

        S64 = 16 * (DEC + 3)
        KEY_LOADS = DEC * PAGES // 4

        def pool_values(pool, did):
            pool.wait_ge(s_cout, 48)
            pool.wait_ge(s_hp, NT)
            pool.wait_ge(s_hpout[0], 16 * 5)
            pool.wait_ge(s_hpout[1], 16 * 4)
            for n in range(DEC * PAGES):
                page = pool.value_load(pages_sb[0:1, n:n + 1], min_val=0, max_val=I["cache_v"].shape[1] - 1)
                if n >= 4:
                    pool.wait_ge(s_pvs, n - 3)
                pool.dma_start(v_page[:, n % 4, :], vp_rows[bass.ds(page, 1)].rearrange("a s c -> (a s) c")).then_inc(s_k4[n % 4], 16)

        def act_queries(act):
            act.wait_ge(s_qsr, 1)
            act.dma_start(qs_dram, qs_rows[:]).then_inc(s_qsd, 16)
            act.wait_ge(s_qsd, 16)
            act.wait_ge(s_wlo, 2 + NB + 8)
            for b in range(DEC):
                if b >= 2:
                    act.wait_ge(s_pair, 2 * (b - 1))
                act.dma_start(q_all[:, b % 2, :], bass.AP(tensor=qs_dram.tensor, offset=QKW * b, ap=[[0, P], [1, QKW]])).then_inc(s_qall[b % 2], 16)

        def pe_queries(pe):
            for h in range(H):
                ins = pe.transpose(tp[1][0:DEC, P * h:P * (h + 1)], qT[:, h, PROMPT:TOK], C("ident"))
            ins.then_inc(s_qstr, 1)

        def dve_queries(dve, did):
            dve.wait_ge(s_qstr, 1)
            dve.tensor_copy(qs_rows[:], tp[1][0:DEC, :]).then_inc(s_qsr, 1)

        def dve_page(dve, did, n):
            b, g = n // PAGES, n % PAGES
            dve.wait_ge(s_k4[n % 4], 16 * (n // 4 + 1))
            dve.wait_ge(s_qall[b % 2], 16 * (b // 2 + 1))
            did(dve.tensor_tensor(prod[:], k_page[:, n % 4, :], q_all[:, b % 2, :], ALU.mult))
            dve.wait_ge(s_step, did.n[0])
            dve.tensor_reduce(s_keys[:, g, 8 * b:8 * b + 8], prod[:].rearrange("p (g d) -> p g d", d=DH), AX.X, ALU.add).then_inc(s_pair, 1)
            dve.wait_ge(s_pair, n + 1)

        def pe_sample_scores(pe):
            pe.wait_ge(s_pair, DEC * PAGES)
            for g in range(PAGES):
                ins = pe.transpose(tp[0][0:NS, P * g:P * (g + 1)], s_keys[:, g, :], C("ident"))
            ins.then_inc(s_sT, 1)

        def dve_sample_softmax(dve, did):
            def settle():
                dve.wait_ge(s_step, did.n[0])
            dve.wait_ge(s_s64, S64)
            did(dve.tensor_tensor_reduce(out=q64[:], in0=q64[:], in1=k64[:], scale=1.0, scalar=0.0, op0=ALU.mult, op1=ALU.add, accum_out=st64[:, 0:1]))
            dve.wait_ge(s_sT, 1)
            did(dve.tensor_tensor_reduce(out=p64[:, 0:PAST], in0=tp[0][0:NS, 0:PAST], in1=bias64[:, 0:PAST], scale=1.0, scalar=-3.0e38,
                                         op0=ALU.add, op1=ALU.max, accum_out=st64[:, 1:2]))
            settle()
            did(dve.tensor_tensor(p64[:, PAST:PAST + 1], st64[:, 0:1], bias64[:, PAST:PAST + 1], ALU.add))
            settle()
            did(dve.tensor_tensor(st64[:, 2:3], p64[:, PAST:PAST + 1], st64[:, 1:2], ALU.max))
            settle()
            dve.tensor_scalar(st64[:, 3:4], st64[:, 2:3], -1.0, None, ALU.mult).then_inc(s_p64, 1)
            dve.wait_ge(s_e64, 1)
            did(dve.reciprocal(st64[:, 5:6], st64[:, 4:5]))
            did(dve.scalar_tensor_tensor(st64[:, 6:7], C("odd", NS), lamw[0:NS, 4:5], C("even", NS), ALU.mult, ALU.add))
            settle()
            did(dve.tensor_tensor(st64[:, 7:8], st64[:, 5:6], st64[:, 6:7], ALU.mult))
            settle()
            dve.tensor_scalar(p64[:], p64[:], st64[:, 7:8], None, ALU.mult).then_inc(s_p64, 1)
            dve.wait_ge(s_aT, 1)
            did(dve.tensor_reduce(a_keys[:].rearrange("p g r -> p (g r)"), tp[1][:, 0:2 * NS].rearrange("p (r c) -> p r c", c=2), AX.X, ALU.add))
            dve.tensor_copy(st32[:, 0:1], tp[1][0:DEC * H, 256:257]).then_inc(s_ak, 1)
            dve.wait_ge(s_ak, 1)

        def act_sample(act):
            act.wait_ge(s_p64, 1)
            act.activation(p64[:], p64[:], ACT.Exp, bias=st64[:, 3:4], accum_out=st64[:, 4:5]).then_inc(s_e64, 1)

        def pe_sample_weights(pe):
            pe.wait_ge(s_p64, 2)
            for g in range(PAGES):
                pe.transpose(tp[1][:, NS * g:NS * (g + 1)], p64[:, P * g:P * (g + 1)], C("ident", NS)[:, 0:NS])
            pe.matmul(tp[1][0:DEC * H, 256:257], C("pair", NS), p64[:, PAST:PAST + 1], start=True, stop=True).then_inc(s_aT, 1)

        def pe_sample_values(pe, b):
            if b == 0:
                pe.wait_ge(s_ak, 1)
            for g in range(PAGES):
                n = PAGES * b + g
                pe.wait_ge(s_k4[n % 4], 16 * (KEY_LOADS + n // 4 + 1))
            for h in range(H):
                for g in range(PAGES):
                    c = H * b + h
                    ins = pe.matmul(tp[1][:, c:c + 1], v_page[:, (PAGES * b + g) % 4, P * h:P * (h + 1)], a_keys[:, g, c:c + 1],
                                    start=(g == 0), stop=(g == PAGES - 1))
            ins.then_inc(s_pvs, 2)

        def dve_sample_out(dve, did):
            def settle():
                dve.wait_ge(s_step, did.n[0])
            dve.wait_ge(s_pvs, DEC * PAGES)
            dve.tensor_copy(o_T[:], tp[1][:, 0:DEC * H]).then_inc(s_oTs, 1)
            dve.wait_ge(s_oTs, 2)
            did(dve.scalar_tensor_tensor(o32[:], v32[:], st32[:, 0:1], tp[0][0:DEC * H, 0:P], ALU.mult, ALU.add))
            settle()
            dve.tensor_tensor_reduce(out=v32[:], in0=o32[:], in1=o32[:], scale=1.0, scalar=0.0, op0=ALU.mult, op1=ALU.add,
                                     accum_out=st32[:, 1:2]).then_inc(s_q32, 1)
            dve.wait_ge(s_r32, 1)
            dve.scalar_tensor_tensor(o32[:], o32[:], st32[:, 3:4], subln[0:DEC * H, :], ALU.mult, ALU.mult).then_inc(s_o32, 1)

        def pe_sample_out(pe):
            pe.wait_ge(s_oTs, 1)
            pe.transpose(tp[0][0:DEC * H, 0:P], o_T[:], C("ident")).then_inc(s_oTs, 1)

        def pool_sample_out(pool, did):
            pool.wait_ge(s_q32, 1)
            did(pool.tensor_scalar(st32[:, 2:3], st32[:, 1:2], 1.0 / P, EPS, ALU.mult, ALU.add))
            pool.wait_ge(s_pool, did.n[0])
            pool.tensor_tensor(st32[:, 3:4], st32[:, 2:3], C("mhalf", DEC * H)[:, 0:1], ALU.pow).then_inc(s_r32, 1)
            pool.wait_ge(s_o32, 1)
            pool.dma_start(os_dram, o32[:]).then_inc(s_osd, 16)

        strip = at("strip", [P, H, STRIP], F32, r_w)
        SW = PROMPT
        sc = at("sc", [P, 2, 2, SW], F32, r_nhi)
        aT = at("aT", [P, 2, NT, P], F32, r_nhi + 16 * SW)
        o_sb = at("o_sb", [P, 2, H * P], F32, r_nhi + 16 * SW + 8 * NT * P)
        hp_in = at("hp_in", [P, 2, D], F32, r_chi)
        h_sb = at("h_sb", [P, 2, D], F32, r_chi + 8192)
        hn = at("hn", [P, 2, D], F32, r_chi + 16384)
        oT_hi = at("oT_hi", [P, H, P], F32R, r_chi + 24576)
        oT_lo = at("oT_lo", [P, H, P], F32R, r_chi + 26624)
        hnT = at("hnT", [P, KC, P], F32, r_chi + 28672)
        g_ffn = at("g_ffn", [P, D], F32, r_t)
        router = at("router", [P, KC, NG + NE], F32, r_t + 4096)
        junk = at("junk", [P, D], F32, r_t + 5248)
        junk_o = at("junk_o", [P, P], F32, r_t + 17536)
        ust = keep("ust", [P, 2, 16])
        ost = keep("ost", [P, 2, 12])
        hst = keep("hst", [P, 2, 4])

        UNITS = [(i, h) for i in range(NT) for h in range(H)]
        NU = len(UNITS)

        def keys(i):
            return min(P * (i + 1), PROMPT)

        def q_rows(i):
            return TAIL if i == NT - 1 else P

        def pieces(i):
            n = keys(i)
            return [(c, k0, min(512, n - k0)) for c in range(2) for k0 in range(0, n, 512)]

        def groups(i):
            return [(b, min(b + 4, i + 1)) for b in range(0, i + 1, 4)]

        piece0 = [sum(len(pieces(i)) for i, _ in UNITS[:u]) for u in range(NU + 1)]

        bank_uses = []

        s_sc = sem("s_sc")
        s_sb = sem("s_sb")
        s_nmx = sem("s_nmx")
        s_exp = sem("s_exp")
        s_a = sem("s_a")
        s_b = sem("s_b")
        s_be = sem("s_be")
        s_blo = sem("s_blo")
        s_o = sem("s_o")
        s_oe = sem("s_oe")
        s_ossq = sem("s_ossq")
        s_orstd = sem("s_orstd")
        s_on = sem("s_on")
        s_osin = sem("s_osin")
        s_hpi = [sem("s_hpi0"), sem("s_hpi1")]
        s_h = sem("s_h")
        s_hsq = sem("s_hsq")
        s_hrstd = sem("s_hrstd")
        s_hn = sem("s_hn")
        s_hst = [sem("s_hst0"), sem("s_hst1")]
        s_hnst = [sem("s_hnst0"), sem("s_hnst1")]
        s_lg = sem("s_lg")
        s_lge = sem("s_lge")
        s_dconst = sem("s_dconst")
        s_subln = sem("s_subln")

        def tile_at(s, lag):
            i = (s - lag - 3) // H
            return i if (s - lag - 3) % H == 0 and 0 <= i < NT else None

        SLOTS = NU + 8
        L_ON, L_OT, L_H, L_HT, L_LG = 2, 3, 4, 5, 6

        for s in range(SLOTS):
            if 0 <= s - 1 < NU:
                for q in range(len(groups(UNITS[s - 1][0]))):
                    bank_uses.append(("a", s - 1, q))
            if (i := tile_at(s, L_OT)) is not None:
                bank_uses.append(("o", i, 0))
            if (i := tile_at(s, L_HT)) is not None:
                bank_uses += [("h", i, 0), ("h", i, 1)]
        USE = {u: n for n, u in enumerate(bank_uses)}
        SC_USES = []
        for s in range(SLOTS):
            if s < NU:
                SC_USES += [("s", s, n) for n in range(len(pieces(UNITS[s][0])))]
            if (i := tile_at(s, L_H)) is not None:
                SC_USES += [("w", i, 0), ("w", i, 1)]
            if (i := tile_at(s, L_LG)) is not None:
                SC_USES.append(("r", i, 0))
        SCU = {u: n for n, u in enumerate(SC_USES)}
        NR = 4
        ring = [pj[0], pj[1], pj[2], pj[5]]
        o_bank = [pj[3], pj[4]]

        strip_flat = strip[:].rearrange("p h c -> p (h c)")
        NF = H * STRIP // 512

        def pe_flip(pe):
            for f in range(NF):
                if f == 0:
                    pe.wait_ge(s_strip, 16 * H)
                if f >= 4:
                    pe.wait_ge(s_flipped, f - 3)
                pe.matmul(pj[f % 4][:], C("flip"), strip_flat[:, 512 * f:512 * (f + 1)], start=True, stop=True).then_inc(s_flip, 1)

        def act_flip(act):
            for f in range(NF):
                act.wait_ge(s_flip, f + 1)
                act.activation(strip_flat[:, 512 * f:512 * (f + 1)], pj[f % 4][:], ACT.Copy).then_inc(s_flipped, 1)

        def sync_d(sp):
            sp.wait_ge(s_wlo, 2 + NB + 8)
            sp.wait_ge(s_gd, 16)
            sp.wait_ge(s_pair, DEC * PAGES)
            for h in range(H):
                sp.dma_start(strip[:, h, :], bass.AP(tensor=g_dram.tensor, offset=GW * h, ap=[[1, P], [1, STRIP]])).then_inc(s_strip, 16)
            sp.wait_ge(s_hp, NT)
            sp.wait_ge(s_hpout[0], 16 * 5)
            sp.wait_ge(s_hpout[1], 16 * 4)
            sp.dma_start(g_ffn[:], bass.AP(tensor=I["norm_ffn"].tensor, offset=0, ap=[[0, P], [1, D]])).then_inc(s_dconst, 16)
            sp.dma_start(router[:, :, 0:NG], I["router_group"][0].rearrange("(k p) c -> p k c", p=P)).then_inc(s_dconst, 16)
            sp.dma_start(router[:, :, NG:NG + NE], I["router_expert"][0].rearrange("(k p) c -> p k c", p=P)).then_inc(s_dconst, 16)
            for i in range(NT):
                M = ROWS[i]
                if i >= 2:
                    sp.wait_ge(s_h, i - 1)
                sp.dma_start(hp_in[0:M, i % 2, :], hp_dram[cols(i)]).then_inc(s_hpi[i % 2], 16)
                if i >= 1:
                    store_tile(sp, i - 1)
            sp.wait_ge(s_fill, 16 * XB)
            sp.wait_ge(s_osd, 16)
            sp.wait_ge(s_b, USE[("o", NT - 3, 0)] + 1)
            sp.dma_start(o_sb[TAIL:TAIL + DEC, (NT - 1) % 2, :], os_dram.rearrange("(b h) d -> b (h d)", h=H)).then_inc(s_osin, 16)
            store_tile(sp, NT - 1)
            sp.wait_ge(s_lge, NT)
            sp.dma_start(c_pre[:], c_prefix.rearrange("p (a b) -> p a b", a=NE)).then_inc(s_pre, 16)
            for w in range(2):
                sp.wait_ge(s_hst[w], 16 * (5 - w))
                sp.wait_ge(s_hnst[w], 16 * (5 - w))
            sp.sem_inc(s_dfree, 1)

        def store_tile(sp, i):
            M = ROWS[i]
            sp.wait_ge(s_h, i + 1)
            sp.dma_start(h_dram[cols(i)], h_sb[0:M, i % 2, :]).then_inc(s_hst[i % 2], 16)
            sp.wait_ge(s_hn, i + 1)
            sp.dma_start(hn_dram[cols(i)], hn[0:M, i % 2, :]).then_inc(s_hnst[i % 2], 16)

        def pe_d(pe):
            ident = C("ident")
            pe.wait_ge(s_be, 1)
            for s in range(SLOTS):
                if s < NU:
                    i, h = UNITS[s]
                    M = q_rows(i)
                    for n, (c, k0, kn) in enumerate(pieces(i)):
                        u = SCU[("s", s, n)]
                        if u == 0:
                            pe.wait_ge(s_flipped, NF)
                        if u >= NR:
                            pe.wait_ge(s_sb, u - NR + 1)
                        pe.matmul(ring[u % NR][0:M, 0:kn], qT[DH * c:DH * (c + 1), h, P * i:P * i + M],
                                  kT[DH * c:DH * (c + 1), h, k0:k0 + kn], start=True, stop=True).then_inc(s_sc, 1)
                if 0 <= s - 1 < NU:
                    i, h = UNITS[s - 1]
                    M = q_rows(i)
                    for q, (b0, b1) in enumerate(groups(i)):
                        u = USE[("a", s - 1, q)]
                        if q == 0:
                            pe.wait_ge(s_a, s)
                        if u >= 2:
                            pe.wait_ge(s_be, u)
                        for b in range(b0, b1):
                            kw = min(P, PROMPT - P * b)
                            ins = pe.transpose(tp[u % 2][0:kw, P * (b - b0):P * (b - b0) + M], sc[0:M, (s - 1) % 2, 0, P * b:P * b + kw], ident[0:M, 0:M])
                        ins.then_inc(s_b, 1)
                if 0 <= s - 2 < NU:
                    i, h = UNITS[s - 2]
                    M = q_rows(i)
                    pe.wait_ge(s_be, USE[("a", s - 2, len(groups(i)) - 1)] + 2)
                    if s - 2 >= 2:
                        pe.wait_ge(s_oe, s - 3)
                    for b in range(i + 1):
                        kw = min(P, PROMPT - P * b)
                        ins = pe.matmul(o_bank[s % 2][0:M, 0:P], aT[0:kw, (s - 2) % 2, b, 0:M], v_tok[0:kw, b, P * h:P * (h + 1)],
                                        start=(b == 0), stop=(b == i))
                    ins.then_inc(s_o, 1)
                if (i := tile_at(s, L_OT)) is not None:
                    M = ROWS[i]
                    u = USE[("o", i, 0)]
                    pe.wait_ge(s_on, i + 1)
                    if i == NT - 1:
                        pe.wait_ge(s_osin, 16)
                    pe.wait_ge(s_be, u)
                    for h in range(H):
                        ins = pe.transpose(tp[u % 2][:, P * h:P * h + M], o_sb[0:M, i % 2, P * h:P * (h + 1)], ident[0:M, 0:M])
                    ins.then_inc(s_b, 1)
                if (i := tile_at(s, L_H)) is not None:
                    M = ROWS[i]
                    pe.wait_ge(s_blo, i + 1)
                    u0 = SCU[("w", i, 0)]
                    pe.wait_ge(s_sb, u0 + 1 - NR + 1)
                    for k in range(H):
                        for a, (c, w) in enumerate(((oT_hi, wa_hi), (oT_hi, wa_lo), (oT_lo, wa_hi))):
                            for b in range(2):
                                ins = pe.matmul(ring[(u0 + b) % NR][0:M, :], c[:, k, 0:M], w[:, k, 512 * b:512 * (b + 1)],
                                                start=(k == 0 and a == 0), stop=(k == H - 1 and a == 2))
                                if k == H - 1 and a == 2:
                                    ins.then_inc(s_sc, 1)
                if (i := tile_at(s, L_HT)) is not None:
                    M = ROWS[i]
                    pe.wait_ge(s_hn, i + 1)
                    for q in range(2):
                        u = USE[("h", i, q)]
                        pe.wait_ge(s_be, u)
                        for c in range(4):
                            k = 4 * q + c
                            ins = pe.transpose(tp[u % 2][:, P * c:P * c + M], hn[0:M, i % 2, P * k:P * (k + 1)], ident[0:M, 0:M])
                        ins.then_inc(s_b, 1)
                if (i := tile_at(s, L_LG)) is not None:
                    M = ROWS[i]
                    u = SCU[("r", i, 0)]
                    pe.wait_ge(s_be, USE[("h", i, 1)] + 2)
                    pe.wait_ge(s_sb, u - NR + 1)
                    for k in range(KC):
                        ins = pe.matmul(ring[u % NR][0:M, 0:NG + NE], hnT[:, k, 0:M], router[:, k, :], start=(k == 0), stop=(k == KC - 1))
                    ins.then_inc(s_sc, 1)

        def act_d(act):
            for s in range(SLOTS):
                if s < NU:
                    i, h = UNITS[s]
                    M = q_rows(i)
                    act.wait_ge(s_nmx, s + 1)
                    for c in range(2):
                        act.activation(sc[0:M, s % 2, c, 0:keys(i)], sc[0:M, s % 2, c, 0:keys(i)], ACT.Exp, bias=ust[0:M, s % 2, 8 + c:9 + c],
                                       accum_out=ust[0:M, s % 2, 10 + c:11 + c]).then_inc(s_exp, 1)
                if 0 <= s - 1 < NU:
                    i, h = UNITS[s - 1]
                    M = q_rows(i)
                    if s - 1 >= 2:
                        act.wait_ge(s_o, s - 2)
                    for q, (b0, b1) in enumerate(groups(i)):
                        u = USE[("a", s - 1, q)]
                        act.wait_ge(s_b, u + 1)
                        kw = min(P, PROMPT - P * (b1 - 1))
                        act.activation(aT[0:kw, (s - 1) % 2, b0:b1, 0:M], tp[u % 2][0:kw, :].rearrange("p (b t) -> p b t", t=P)[:, 0:b1 - b0, 0:M], ACT.Copy).then_inc(s_be, 1)
                        assert kw == P or b1 == b0 + 1
                if (i := tile_at(s, L_OT)) is not None:
                    M = ROWS[i]
                    u = USE[("o", i, 0)]
                    act.wait_ge(s_b, u + 1)
                    if i >= 1:
                        act.wait_ge(s_sc, SCU[("w", i - 1, 1)] + 1)
                    act.activation(oT_hi[:, :, 0:M], tp[u % 2][:].rearrange("p (h t) -> p h t", h=H)[:, :, 0:M], ACT.Copy).then_inc(s_othi, 1)
                    act.wait_ge(s_blo, i + 1)
                    act.sem_inc(s_be, 1)
                if (i := tile_at(s, L_H)) is not None:
                    M = ROWS[i]
                    act.wait_ge(s_h, i + 1)
                    act.activation(junk[0:M, :], h_sb[0:M, i % 2, :], ACT.Square, accum_out=hst[0:M, i % 2, 0:1]).then_inc(s_hsq, 1)
                if (i := tile_at(s, L_HT)) is not None:
                    M = ROWS[i]
                    if i >= 1:
                        act.wait_ge(s_lge, i)
                    for q in range(2):
                        u = USE[("h", i, q)]
                        act.wait_ge(s_b, u + 1)
                        act.activation(hnT[:, 4 * q:4 * q + 4, 0:M], tp[u % 2][:].rearrange("p (c t) -> p c t", c=4)[:, :, 0:M], ACT.Copy).then_inc(s_be, 1)

        s_othi = sem("s_othi")

        def pool_d(pool, did):
            for s in range(SLOTS):
                if (i := tile_at(s, L_ON)) is not None:
                    M = q_rows(i)
                    pool.wait_ge(s_ossq, H * (i + 1))
                    did(pool.tensor_scalar(ost[0:M, i % 2, 4:8], ost[0:M, i % 2, 0:4], 1.0 / P, EPS, ALU.mult, ALU.add))
                    pool.wait_ge(s_pool, did.n[0])
                    pool.tensor_tensor(ost[0:M, i % 2, 8:12], ost[0:M, i % 2, 4:8], C("mhalf", M)[:, 0:4], ALU.pow).then_inc(s_orstd, 1)
                if (i := tile_at(s, L_H)) is not None:
                    M = ROWS[i]
                    pool.wait_ge(s_hsq, i + 1)
                    did(pool.tensor_scalar(hst[0:M, i % 2, 1:2], hst[0:M, i % 2, 0:1], 1.0 / D, EPS, ALU.mult, ALU.add))
                    pool.wait_ge(s_pool, did.n[0])
                    pool.tensor_tensor(hst[0:M, i % 2, 2:3], hst[0:M, i % 2, 1:2], C("mhalf", M)[:, 0:1], ALU.pow).then_inc(s_hrstd, 1)

        def dve_d(dve, did):
            def settle():
                dve.wait_ge(s_step, did.n[0])
            dve.wait_ge(s_flipped, NF)
            dve.wait_ge(s_dconst, 48)
            dve.wait_ge(s_fill, 16 * XB)
            for s in range(SLOTS):
                if s < NU:
                    i, h = UNITS[s]
                    M = q_rows(i)
                    ps = pieces(i)
                    half = len(ps) // 2
                    if s >= 2:
                        i2 = UNITS[s - 2][0]
                        dve.wait_ge(s_b, USE[("a", s - 2, len(groups(i2)) - 1)] + 1)
                    for n, (c, k0, kn) in enumerate(ps):
                        u = SCU[("s", s, n)]
                        dve.wait_ge(s_sc, u + 1)
                        m0 = P * (NT - 1) - P * i + k0
                        col = c * half + (n - c * half)
                        dve.tensor_tensor_reduce(out=sc[0:M, s % 2, c, k0:k0 + kn], in0=ring[u % NR][0:M, 0:kn], in1=strip[0:M, h, m0:m0 + kn],
                                                 scale=1.0, scalar=-3.0e38, op0=ALU.add, op1=ALU.max, accum_out=ust[0:M, s % 2, col:col + 1]).then_inc(s_sb, 1)
                    dve.wait_ge(s_sb, SCU[("s", s, len(ps) - 1)] + 1)
                    did(dve.tensor_reduce(ust[0:M, s % 2, 6:8], ust[0:M, s % 2, 0:2 * half].rearrange("p (c n) -> p c n", c=2), AX.X, ALU.max))
                    settle()
                    dve.tensor_scalar(ust[0:M, s % 2, 8:10], ust[0:M, s % 2, 6:8], -1.0, None, ALU.mult).then_inc(s_nmx, 1)
                if 0 <= s - 1 < NU:
                    i, h = UNITS[s - 1]
                    M, x = q_rows(i), (s - 1) % 2
                    dve.wait_ge(s_exp, 2 * s)
                    if s - 1 >= 2:
                        dve.wait_ge(s_oe, s - 2)
                    did(dve.reciprocal(ust[0:M, x, 12:14], ust[0:M, x, 10:12]))
                    settle()
                    did(dve.scalar_tensor_tensor(ust[0:M, x, 14:15], ust[0:M, x, 10:11], lamw[0:M, 4:5], ust[0:M, x, 13:14], ALU.mult, ALU.mult))
                    settle()
                    dve.scalar_tensor_tensor(sc[0:M, x, 0, 0:keys(i)], sc[0:M, x, 1, 0:keys(i)], ust[0:M, x, 14:15], sc[0:M, x, 0, 0:keys(i)],
                                             ALU.mult, ALU.add).then_inc(s_a, 1)
                if 0 <= s - 2 < NU:
                    i, h = UNITS[s - 2]
                    M, x = q_rows(i), (s - 2) % 2
                    if h == 0 and i >= 2:
                        dve.wait_ge(s_b, USE[("o", i - 2, 0)] + 1)
                    dve.wait_ge(s_o, s - 1)
                    dve.tensor_scalar(o_sb[0:M, i % 2, P * h:P * (h + 1)], o_bank[s % 2][0:M, 0:P], ust[0:M, x, 12:13], None, ALU.mult).then_inc(s_oe, 1)
                    dve.wait_ge(s_oe, s - 1)
                    dve.tensor_tensor_reduce(out=junk_o[0:M, :], in0=o_sb[0:M, i % 2, P * h:P * (h + 1)], in1=o_sb[0:M, i % 2, P * h:P * (h + 1)],
                                             scale=1.0, scalar=0.0, op0=ALU.mult, op1=ALU.add, accum_out=ost[0:M, i % 2, h:h + 1]).then_inc(s_ossq, 1)
                if (i := tile_at(s, L_ON)) is not None:
                    M = q_rows(i)
                    dve.wait_ge(s_orstd, i + 1)
                    for h in range(H):
                        ins = dve.scalar_tensor_tensor(o_sb[0:M, i % 2, P * h:P * (h + 1)], o_sb[0:M, i % 2, P * h:P * (h + 1)], ost[0:M, i % 2, 8 + h:9 + h],
                                                       subln[0:M, :], ALU.mult, ALU.mult)
                        did(ins)
                    settle()
                    dve.sem_inc(s_on, 1)
                if (i := tile_at(s, L_OT)) is not None:
                    M = ROWS[i]
                    u = USE[("o", i, 0)]
                    dve.wait_ge(s_othi, i + 1)
                    dve.tensor_tensor(oT_lo[:, :, 0:M], tp[u % 2][:].rearrange("p (h t) -> p h t", h=H)[:, :, 0:M], oT_hi[:, :, 0:M].bitcast(F32), ALU.subtract).then_inc(s_blo, 1)
                if (i := tile_at(s, L_H)) is not None:
                    M = ROWS[i]
                    u0 = SCU[("w", i, 0)]
                    dve.wait_ge(s_sc, u0 + 2)
                    dve.wait_ge(s_hpi[i % 2], 16 * (i // 2 + 1))
                    if i >= 2:
                        dve.wait_ge(s_hst[i % 2], 16 * (i // 2))
                    for b in range(2):
                        part = slice(512 * b, 512 * (b + 1))
                        dve.tensor_tensor(h_sb[0:M, i % 2, part], ring[(u0 + b) % NR][0:M, :], hp_in[0:M, i % 2, part], ALU.add).then_inc(s_sb, 1)
                    dve.wait_ge(s_sb, u0 + 2)
                    dve.sem_inc(s_h, 1)
                    dve.wait_ge(s_hrstd, i + 1)
                    if i >= 2:
                        dve.wait_ge(s_hnst[i % 2], 16 * (i // 2))
                    dve.scalar_tensor_tensor(hn[0:M, i % 2, :], h_sb[0:M, i % 2, :], hst[0:M, i % 2, 2:3], g_ffn[0:M, :], ALU.mult, ALU.mult).then_inc(s_hn, 1)
                if (i := tile_at(s, L_LG)) is not None:
                    M = ROWS[i]
                    u = SCU[("r", i, 0)]
                    dve.wait_ge(s_sc, u + 1)
                    dve.tensor_copy(logits[0:M, i, :], ring[u % NR][0:M, 0:NG + NE]).then_inc(s_sb, 1)
                    dve.wait_ge(s_sb, u + 1)
                    dve.sem_inc(s_lge, 1)

        XMEM = r_chi + 4 * 4 * 6144
        SZ = 4 * 6144
        e_raw = at("e_raw", [P, 6, 2048], F32, r_q)
        e_hi = at("e_hi", [P, 2, 3, 2048], F32R, r_chi)
        e_lo = at("e_lo", [P, 2, 3, 2048], F32R, r_chi + 2 * SZ)
        xg = at("xg", [P, 2, D], F32, XMEM)
        xT_hi = at("xT_hi", [P, KC, P], F32R, XMEM + 8192)
        xT_lo = at("xT_lo", [P, KC, P], F32R, XMEM + 12288)
        yo = at("yo", [P, 2, D], F32, XMEM + 16384)
        sg = at("sg", [P, FF], F32, XMEM + 24576)
        hh = at("hh", [P, FF], F32, XMEM + 25600)
        hT_hi = at("hT_hi", [P, 2, P], F32R, XMEM + 26624)
        hT_lo = at("hT_lo", [P, 2, P], F32R, XMEM + 27648)
        rcur = [XMEM + 16384]

        def rt(name, shape, dt=F32):
            o = rcur[0]
            n = 4 * int(np.prod(shape[1:]))
            rcur[0] = o + n + (-n) % 32
            assert rcur[0] <= r_s + 4 * TOK, rcur[0] - r_s
            return at(name, shape, dt, o)

        A = NE * NT
        c_pre = rt("c_pre", [P, NE, NE])
        pre_nx = rt("pre_nx", [P, NE, NE])
        lem = rt("lem", [P, NT, NE])
        eq = rt("eq", [P, NT, NE])
        hot2 = rt("hot2", [P, 2, NT, NE])
        mark = rt("mark", [P, NT + 2, NE])
        grp = rt("grp", [P, 4, NT, NG])
        gs = rt("gs", [P, 8, NT])
        ms = rt("ms", [P, 2, NT])
        ei = rt("ei", [P, 2, NT])
        rk = rt("rk", [P, 8, 2, NT])
        big2 = at("big2", [P, 2, NT, NE], F32, XMEM + 8192)
        over2 = at("over2", [P, 2 * NT, 8], F32, XMEM + 12288)
        ranks = at("ranks", [P, NT + 1, NE], F32, XMEM + 13312)
        place_hot = at("place_hot", [P, 2, P], F32, XMEM)
        block_tok = at("block_tok", [P, 2, MAXB], F32, XMEM + 1024)
        nxs = at("nxs", [P, 4, NE], F32, XMEM + 2048)
        xl = at("xl", [P, XB, NE], F32, XMEM + 4096)
        xlf = at("xlf", [P, XB + 1], F32, XMEM + 6400)
        gate_w = keep("gate_w", [P, 2, NT])
        addr = keep("addr", [P, 2 * NT], I32)
        slot_tok = keep("slot_tok", [P, MAXB], I32)
        xlist = keep("xlist", [P, XB + 1], I32)
        idx_cur = keep("idx_cur", [P, 2], I32)

        s_pre = sem("s_pre")
        s_rx = sem("s_rx")
        s_re = sem("s_re")
        s_mark = sem("s_mark")
        s_rank = sem("s_rank")
        s_ph = sem("s_ph")
        s_pm = sem("s_pm")
        s_slots = sem("s_slots")
        s_dfree = sem("s_dfree")

        def spread(ap, dims):
            return bass.AP(tensor=ap.tensor, offset=ap.offset, ap=[list(ap.ap[0])] + dims)

        def each(ap, n, inner):
            return spread(ap, [[1, n], [0, inner]])

        def over_rows(ap, outer, n):
            return spread(ap, [[0, outer], [1, n]])

        def dve_r(dve, did):
            def settle():
                dve.wait_ge(s_step, did.n[0])

            def do(ins):
                did(ins)
                settle()
            dve.wait_ge(s_pre, 16)
            dve.wait_ge(s_dfree, 1)
            g, e = logits[:, :, 0:NG], logits[:, :, NG:NG + NE]
            iota32 = C("iota32")

            def first_max(vals, n, m, idx, tmp):
                do(dve.tensor_reduce(m, vals, AX.X, ALU.max))
                do(dve.tensor_tensor(tmp, vals, each(m, NT, n), ALU.is_equal))
                do(dve.scalar_tensor_tensor(tmp, tmp, -64.0, over_rows(iota32, NT, n), ALU.mult, ALU.add))
                do(dve.tensor_reduce(idx, tmp, AX.X, ALU.min))
                do(dve.tensor_scalar(idx, idx, 64.0, None, ALU.add))

            first_max(g, NG, gs[:, 0, :], gs[:, 1, :], grp[:, 0])
            dve.tensor_tensor(grp[:, 1], g, each(gs[:, 0, :], NT, NG), ALU.subtract).then_inc(s_rx, 1)
            do(dve.tensor_tensor(eq[:], over_rows(C("iotag"), NT, NE), each(gs[:, 1, :], NT, NE), ALU.is_equal))
            do(dve.tensor_scalar(eq[:], eq[:], -1.0, BIG, ALU.add, ALU.mult))
            do(dve.tensor_tensor(lem[:], eq[:], e, ALU.add))
            for c in range(2):
                first_max(lem[:], NE, ms[:, c, :], ei[:, c, :], eq[:])
                do(dve.tensor_tensor(hot2[:, c], over_rows(iota32, NT, NE), each(ei[:, c, :], NT, NE), ALU.is_equal))
                if c == 0:
                    do(dve.scalar_tensor_tensor(lem[:], hot2[:, 0], -3.0 * BIG, lem[:], ALU.mult, ALU.add))
            dve.tensor_tensor(gs[:, 2, :], ms[:, 1, :], ms[:, 0, :], ALU.subtract).then_inc(s_rx, 1)
            did(dve.memset(mark[:], 0.0))
            do(dve.tensor_tensor(eq[:], hot2[:, 0], hot2[:, 1], ALU.add))
            dve.tensor_tensor(mark[:, 1:NT + 1, :], eq[:], each(C("valid"), NT, NE), ALU.mult).then_inc(s_mark, 1)
            dve.wait_ge(s_re, 2)
            do(dve.tensor_reduce(gs[:, 3, :], grp[:, 2], AX.X, ALU.add))
            do(dve.tensor_scalar(gs[:, 5, :], gs[:, 4, :], 1.0, None, ALU.add))
            do(dve.tensor_tensor(gs[:, 3, :], gs[:, 3, :], gs[:, 5, :], ALU.mult))
            do(dve.reciprocal(gate_w[:, 0, :], gs[:, 3, :]))
            do(dve.tensor_tensor(gate_w[:, 1, :], gate_w[:, 0, :], gs[:, 4, :], ALU.mult))
            dve.wait_ge(s_rank, 1)
            do(dve.tensor_copy(ranks[:], pj[0][:, 0:(NT + 1) * NE].rearrange("p (t e) -> p t e", e=NE)))
            ov = C("over")
            do(dve.tensor_tensor(big2[:, 0, 0:8, :].rearrange("p a b -> p (a b)").rearrange("p (e j) -> p e j", j=8), each(ranks[:, NT, :], NE, 8), over_rows(ov, NE, 8), ALU.is_gt))
            do(dve.tensor_reduce(nxs[:, 0, :], big2[:, 0, 0:8, :].rearrange("p a b -> p (a b)").rearrange("p (e j) -> p e j", j=8), AX.X, ALU.add))
            do(dve.tensor_tensor(pre_nx[:], c_pre[:], over_rows(nxs[:, 0, :], NE, NE), ALU.mult))
            do(dve.tensor_reduce(nxs[:, 1, :], pre_nx[:], AX.X, ALU.add))
            do(dve.tensor_tensor(nxs[:, 2, :], nxs[:, 0, :], nxs[:, 1, :], ALU.add))
            do(dve.tensor_tensor(xl[:], each(C("iotax"), XB, NE), over_rows(nxs[:, 2, :], XB, NE), ALU.is_ge))
            do(dve.tensor_reduce(xlf[:, 0:XB], xl[:], AX.X, ALU.add))
            do(dve.tensor_scalar(xlf[:, 0:XB], xlf[:, 0:XB], float(NE - 1), None, ALU.min))
            do(dve.tensor_copy(xlf[:, XB:XB + 1], nxs[:, 2, NE - 1:NE]))
            did(dve.tensor_copy(xlist[:], xlf[:]))
            for c in range(2):
                did(dve.tensor_tensor(big2[:, c], hot2[:, c], ranks[:, 0:NT, :], ALU.mult))
            settle()
            do(dve.tensor_reduce(rk[:, 0], big2[:], AX.X, ALU.add))
            for c in range(2):
                did(dve.tensor_tensor(big2[:, c], hot2[:, c], over_rows(nxs[:, 1, :], NT, NE), ALU.mult))
            settle()
            do(dve.tensor_reduce(rk[:, 1], big2[:], AX.X, ALU.add))
            flat = [rk[:, i].rearrange("p a b -> p (a b)") for i in range(8)]
            eif = ei[:].rearrange("p a b -> p (a b)")
            N2 = 2 * NT
            do(dve.tensor_tensor(over2[:], each(flat[0], N2, 8), over_rows(ov, N2, 8), ALU.is_ge))
            do(dve.tensor_reduce(flat[2], over2[:], AX.X, ALU.add))
            do(dve.scalar_tensor_tensor(flat[3], flat[2], -float(P), flat[0], ALU.mult, ALU.add))
            do(dve.tensor_tensor(flat[4], flat[1], flat[2], ALU.add))
            do(dve.scalar_tensor_tensor(flat[4], flat[4], float(NE - 1), eif, ALU.add, ALU.subtract))
            do(dve.tensor_scalar(flat[5], flat[2], 1.0, None, ALU.min))
            do(dve.tensor_tensor(flat[4], flat[4], flat[5], ALU.mult))
            do(dve.tensor_tensor(flat[6], flat[4], eif, ALU.add))
            do(dve.scalar_tensor_tensor(flat[7], flat[3], float(MAXB), flat[6], ALU.mult, ALU.add))
            did(dve.tensor_copy(addr[:], flat[7]))
            for u in range(N2):
                if u >= 2:
                    dve.wait_ge(s_pm, u - 1)
                did(dve.tensor_scalar(place_hot[:, u % 2, :], C("iota128"), flat[3][:, u:u + 1], None, ALU.is_equal))
                dve.tensor_scalar(block_tok[:, u % 2, :], C("iota128")[:, 0:MAXB], flat[6][:, u:u + 1], C("token")[:, u % NT:u % NT + 1],
                                  ALU.is_equal, ALU.mult).then_inc(s_ph, 1)
                settle()
            dve.wait_ge(s_pm, N2)
            did(dve.tensor_copy(slot_tok[:], pj[1][:, 0:MAXB]))
            settle()
            dve.sem_inc(s_slots, 1)

        def act_r(act):
            act.wait_ge(s_rx, 1)
            act.activation(grp[:, 2], grp[:, 1], ACT.Exp).then_inc(s_re, 1)
            act.wait_ge(s_rx, 2)
            act.activation(gs[:, 4, :], gs[:, 2, :], ACT.Exp).then_inc(s_re, 1)

        def pe_r(pe):
            pe.wait_ge(s_mark, 1)
            pe.wait_ge(s_lge, NT)
            out = pj[0][:, 0:(NT + 1) * NE]
            pe.matmul(out, C("ones"), mark[:, 0:NT + 1, :].rearrange("p t e -> p (t e)"), start=True, stop=False)
            for t in range(NT - 1):
                pe.matmul(out[:, NE * (t + 2):], C("ones"), spread(mark[:, t + 1, :], [[0, NT - 1 - t], [1, NE]]),
                          start=False, stop=False, skip_group_check=True)
            pe.matmul(out, C("before"), mark[:, 1:NT + 2, :].rearrange("p t e -> p (t e)"), start=False, stop=True).then_inc(s_rank, 1)
            for u in range(2 * NT):
                pe.wait_ge(s_ph, u + 1)
                pe.matmul(pj[1][:, 0:MAXB], place_hot[:, u % 2, :], block_tok[:, u % 2, :], start=(u == 0), stop=(u == 2 * NT - 1)).then_inc(s_pm, 1)

        s_er = [sem(f"s_er{i}") for i in range(6)]
        s_hi = [sem(f"s_hi{q}") for q in range(3)]
        s_lo = [sem(f"s_lo{q}") for q in range(3)]
        s_idx = sem("s_idx")
        s_xg = [sem("s_xg0"), sem("s_xg1")]
        s_xt = sem("s_xt")
        s_xthi = sem("s_xthi")
        s_xtlo = sem("s_xtlo")
        s_gu = sem("s_gu")
        s_silu = sem("s_silu")
        s_hh = sem("s_hh")
        s_ht = sem("s_ht")
        s_hthi = sem("s_hthi")
        s_htlo = sem("s_htlo")
        s_dn = sem("s_dn")
        s_y0 = sem("s_y0")
        s_y1 = sem("s_y1")
        s_yst = [sem("s_yst0"), sem("s_yst1")]
        s_ally = sem("s_ally")
        s_turn = sem("s_turn")

        xb = [tp[0], tp[1]]
        gu_bank, ht_bank, dn = pj[2], pj[3], [pj[4], pj[5]]
        y_rows = y_dram.rearrange("(p b) c -> p b c", b=MAXB)

        def later(n, lag):
            return not isinstance(n, int) or n >= lag

        def half(n, par):
            return n // 2 if isinstance(n, int) else n[1]

        def load_piece(sp, n, m, par, q, expert):
            if later(n, 2):
                sp.wait_ge(s_lo[q], n - 1)
            w = I[("w_gate", "w_up", "w_down")[q]][0]
            if q < 2:
                src = w[bass.ds(expert, 1)].rearrange("a (p k) f -> p (a k f)", p=P)
                dst = e_raw[:, 3 * par + q, :]
            else:
                src = w[bass.ds(expert, 1)].rearrange("a (f p) c -> p (a f) c", p=P)
                dst = e_raw[:, 3 * par + q, :].rearrange("p (f c) -> p f c", f=2)
            sp.dma_start(dst, src).then_inc(s_er[3 * par + q], 16)

        def store_block(sp, n, m, par):
            sp.wait_ge(s_y0, n + 1)
            sp.wait_ge(s_y1, n + 1)
            sp.dma_start(y_rows[:, bass.ds(n, 1), :], yo[:, par:par + 1, :]).then_inc(s_yst[par], 16)

        def gather(pool, n, m, par):
            if later(n, 2):
                pool.wait_ge(s_xt, 2 * n - 2)
            pool.tensor_copy(idx_cur[:, par:par + 1], slot_tok[:, bass.ds(n, 1)]).then_inc(s_idx, 1)
            pool.wait_ge(s_idx, n + 1)
            pool.sem_inc(s_turn, 1)
            pool.indirect_dma_start(xg[:, par, :], None, hn_dram, bass.IndirectOffsetOnAxis(ap=idx_cur[:, par:par + 1], axis=0)).then_inc(s_xg[par], 16)

        def high(act, n, m, par, q):
            act.wait_ge(s_er[3 * par + q], 16 * (m + 1))
            if later(n, 2):
                act.wait_ge(s_dn if q == 2 else s_gu, n - 1)
            act.activation(e_hi[:, par, q, :], e_raw[:, 3 * par + q, :], ACT.Copy).then_inc(s_hi[q], 1)

        def low(eng, n, m, par, q):
            eng.wait_ge(s_hi[q], n + 1)
            eng.tensor_tensor(e_lo[:, par, q, :], e_raw[:, 3 * par + q, :], e_hi[:, par, q, :].bitcast(F32), ALU.subtract).then_inc(s_lo[q], 1)

        def pe_xt(pe, n, m, par):
            pe.wait_ge(s_xg[par], 16 * (m + 1))
            rows = xg[:, par, :].rearrange("s (p k) -> s k p", k=KC)
            for q in range(2):
                if later(n, 1):
                    pe.wait_ge(s_xtlo, 2 * n + q - 1)
                for c in range(4):
                    ins = pe.transpose(xb[q][:, P * c:P * (c + 1)], rows[:, 4 * q + c, :], C("ident"))
                ins.then_inc(s_xt, 1)

        def act_xt(act, n, m, par):
            for q in range(2):
                act.wait_ge(s_xt, 2 * n + q + 1)
                if later(n, 1) and q == 0:
                    act.wait_ge(s_gu, n)
                act.activation(xT_hi[:, 4 * q:4 * q + 4, :].rearrange("p c t -> p (c t)"), xb[q][:], ACT.Copy).then_inc(s_xthi, 1)

        def dve_xt(dve, n, m, par):
            for q in range(2):
                dve.wait_ge(s_xthi, 2 * n + q + 1)
                dve.tensor_tensor(xT_lo[:, 4 * q:4 * q + 4, :].rearrange("p c t -> p (c t)"), xb[q][:],
                                  xT_hi[:, 4 * q:4 * q + 4, :].rearrange("p c t -> p (c t)").bitcast(F32), ALU.subtract).then_inc(s_xtlo, 1)

        def pe_gu(pe, n, m, par):
            pe.wait_ge(s_xtlo, 2 * n + 2)
            pe.wait_ge(s_lo[0], n + 1)
            pe.wait_ge(s_lo[1], n + 1)
            if later(n, 1):
                pe.wait_ge(s_hh, n)
            for k in range(KC):
                for a, (x, w) in enumerate(((xT_hi, e_hi), (xT_hi, e_lo), (xT_lo, e_hi))):
                    ins = pe.matmul(gu_bank[:].rearrange("p (q f) -> p q f", q=2), x[:, k, :], w[:, par, 0:2, FF * k:FF * (k + 1)],
                                    start=(k == 0 and a == 0), stop=(k == KC - 1 and a == 2))
            ins.then_inc(s_gu, 1)

        def act_silu(act, n, m, par):
            act.wait_ge(s_gu, n + 1)
            if later(n, 1):
                act.wait_ge(s_hh, n)
            act.activation(sg[:], gu_bank[:, 0:FF], ACT.Silu).then_inc(s_silu, 1)

        def dve_mult(dve, n, m, par):
            dve.wait_ge(s_silu, n + 1)
            if later(n, 1):
                dve.wait_ge(s_ht, n)
            dve.tensor_tensor(hh[:], gu_bank[:, FF:2 * FF], sg[:], ALU.mult).then_inc(s_hh, 1)

        def pe_ht(pe, n, m, par):
            pe.wait_ge(s_hh, n + 1)
            if later(n, 1):
                pe.wait_ge(s_htlo, n)
            for f in range(2):
                ins = pe.transpose(ht_bank[:, P * f:P * (f + 1)], hh[:, P * f:P * (f + 1)], C("ident"))
            ins.then_inc(s_ht, 1)

        def act_ht(act, n, m, par):
            act.wait_ge(s_ht, n + 1)
            if later(n, 1):
                act.wait_ge(s_dn, n)
            act.activation(hT_hi[:].rearrange("p f t -> p (f t)"), ht_bank[:, 0:2 * P], ACT.Copy).then_inc(s_hthi, 1)

        def dve_ht(dve, n, m, par):
            dve.wait_ge(s_hthi, n + 1)
            dve.tensor_tensor(hT_lo[:].rearrange("p f t -> p (f t)"), ht_bank[:, 0:2 * P], hT_hi[:].rearrange("p f t -> p (f t)").bitcast(F32),
                              ALU.subtract).then_inc(s_htlo, 1)

        def pe_dn(pe, n, m, par):
            pe.wait_ge(s_htlo, n + 1)
            pe.wait_ge(s_lo[2], n + 1)
            if later(n, 1):
                pe.wait_ge(s_y0, n)
                pe.wait_ge(s_y1, n)
            for f in range(2):
                for a, (x, w) in enumerate(((hT_hi, e_hi), (hT_hi, e_lo), (hT_lo, e_hi))):
                    for b in range(2):
                        o = D * f + 512 * b
                        ins = pe.matmul(dn[b][:], x[:, f, :], w[:, par, 2, o:o + 512], start=(f == 0 and a == 0), stop=(f == 1 and a == 2))
            ins.then_inc(s_dn, 1)

        def y_half(eng, n, m, par, b):
            eng.wait_ge(s_dn, n + 1)
            eng.wait_ge(s_yst[par], 16 * m + 16)
            part = slice(512 * b, 512 * (b + 1))
            if b == 0:
                eng.activation(yo[:, par, part], dn[b][:], ACT.Copy).then_inc(s_y0, 1)
            else:
                eng.tensor_copy(yo[:, par, part], dn[b][:]).then_inc(s_y1, 1)

        def sp_step(sp, B):
            if (b := B(2)):
                load_piece(sp, *b, 0, b[0])
                load_piece(sp, *b, 1, b[0])
            if (b := B(-2)):
                store_block(sp, *b)
            if (b := B(2)):
                load_piece(sp, *b, 2, b[0])

        def pool_step(pool, B):
            if (b := B(1)):
                low(pool, *b, 1)
            if (b := B(2)):
                gather(pool, *b)

        def act_step(act, B):
            if (b := B(-1)):
                act_ht(act, *b)
            if (b := B(-2)):
                y_half(act, *b, 0)
            if (b := B(0)):
                high(act, *b, 2)
            if (b := B(1)):
                high(act, *b, 0)
                high(act, *b, 1)
            if (b := B(0)):
                act_silu(act, *b)
            if (b := B(1)):
                act_xt(act, *b)

        def dve_step(dve, B):
            if (b := B(-1)):
                dve_ht(dve, *b)
            if (b := B(-2)):
                y_half(dve, *b, 1)
            if (b := B(0)):
                low(dve, *b, 2)
            if (b := B(1)):
                low(dve, *b, 0)
            if (b := B(0)):
                dve_mult(dve, *b)
            if (b := B(1)):
                dve_xt(dve, *b)

        def pe_step(pe, B):
            if (b := B(0)):
                pe_gu(pe, *b)
            if (b := B(1)):
                pe_xt(pe, *b)
            if (b := B(-1)):
                pe_dn(pe, *b)
            if (b := B(0)):
                pe_ht(pe, *b)

        def run_blocks(eng, step, first):
            def at_block(n):
                return lambda d: (n + d, (n + d) // 2, (n + d) % 2) if 0 <= n + d < NE else None
            for n in range(first, 2):
                step(eng, at_block(n))
            with eng.Fori(1, NE // 2 - 1) as g:
                for par in range(2):
                    step(eng, lambda d: (2 * g + (par + d), g + (par + d) // 2, (par + d) % 2))
            for n in range(NE - 2, NE + 2):
                step(eng, at_block(n))

        def overflow(eng, body):
            extra = eng.value_load(xlist[0:1, XB:XB + 1], min_val=0, max_val=XB)
            with eng.Fori(0, XB // 2) as g:
                for par in range(2):
                    with eng.If(2 * g + par < extra):
                        body((NE + 2 * g + par, NE // 2 + g, par), g)

        def sp_m(sp):
            sp.wait_ge(s_o, NU)
            for w in range(2):
                sp.sem_inc(s_yst[w], 16)
            run_blocks(sp, sp_step, -2)
            sp.wait_ge(s_slots, 1)

            def body(b, g):
                n, m, par = b
                expert = sp.value_load(xlist[0:1, bass.ds(2 * g + par, 1)], min_val=0, max_val=NE - 1)
                for q in range(3):
                    load_piece(sp, n, m, par, q, expert)
                store_block(sp, n, m, par)
                sp.wait_ge(s_yst[par], 16 * (m + 2))
                sp.sem_inc(s_turn, 1)
            overflow(sp, body)
            for w in range(2):
                sp.wait_ge(s_yst[w], 16 * (NE // 2 + 1))
            sp.sem_inc(s_ally, 1)

        def pool_m(pool):
            pool.wait_ge(s_slots, 1)
            for w in range(2):
                pool.wait_ge(s_hnst[w], 16 * (5 - w))
            run_blocks(pool, pool_step, -2)

            def body(b, g):
                gather(pool, *b)
                low(pool, *b, 1)
            overflow(pool, body)

        def act_m(act):
            for w in range(2):
                act.wait_ge(s_hst[w], 16 * (5 - w))
                act.wait_ge(s_hnst[w], 16 * (5 - w))
            act.wait_ge(s_lge, NT)
            run_blocks(act, act_step, -1)
            act.wait_ge(s_slots, 1)

            def body(b, g):
                for q in range(3):
                    high(act, *b, q)
                act_xt(act, *b)
                act_silu(act, *b)
                act_ht(act, *b)
                y_half(act, *b, 0)
            overflow(act, body)

        def dve_m(dve):
            run_blocks(dve, dve_step, -1)

            def body(b, g):
                low(dve, *b, 0)
                low(dve, *b, 2)
                dve_xt(dve, *b)
                dve_mult(dve, *b)
                dve_ht(dve, *b)
                y_half(dve, *b, 1)
            overflow(dve, body)

        def pe_m(pe):
            run_blocks(pe, pe_step, -1)
            pe.wait_ge(s_slots, 1)

            def body(b, g):
                pe_xt(pe, *b)
                pe_gu(pe, *b)
                pe_ht(pe, *b)
                pe_dn(pe, *b)
            overflow(pe, body)

        RF = 3
        f_h = at("f_h", [P, RF, D], F32, r_chi)
        f_y = at("f_y", [P, RF, 2, D], F32, r_chi + 4096 * RF)
        f_o = at("f_o", [P, RF, D], F32, r_chi + 4096 * 3 * RF)
        f_junk = at("f_junk", [P, D], F32, r_chi + 4096 * 4 * RF)
        g_fin = at("g_fin", [P, D], F32, r_chi + 4096 * (4 * RF + 1))
        fst = keep("fst", [P, RF, 4])
        s_gfin = sem("s_gfin")
        s_fh = [sem(f"s_fh{i}") for i in range(RF)]
        s_fy = [sem(f"s_fy{i}") for i in range(RF)]
        s_fs = sem("s_fs")
        s_fq = sem("s_fq")
        s_fr = sem("s_fr")
        s_fn = sem("s_fn")
        s_fout = sem("s_fout")

        def sp_f(sp):
            sp.dma_start(g_fin[:], bass.AP(tensor=I["norm_final"].tensor, offset=0, ap=[[0, P], [1, D]])).then_inc(s_gfin, 16)

            def out(i):
                sp.wait_ge(s_fn, i + 1)
                r = i % RF
                y = O["y_prompt"][0]
                if i == 0:
                    sp.dma_start(y[0:P - META], f_o[META:P, r, :]).then_inc(s_fout, 16)
                elif i < NT - 1:
                    sp.dma_start(y[P * i - META:P * (i + 1) - META], f_o[:, r, :]).then_inc(s_fout, 16)
                else:
                    sp.dma_start(y[P * i - META:SEQ], f_o[0:TAIL, r, :]).then_inc(s_fout, 16)
                    sp.dma_start(O["y_sample"].rearrange("b t d -> (b t) d"), f_o[TAIL:TAIL + DEC, r, :]).then_inc(s_fout, 16)

            for i in range(NT):
                if i >= RF:
                    sp.wait_ge(s_fs, 2 * (i - RF + 1))
                sp.dma_start(f_h[0:ROWS[i], i % RF, :], h_dram[cols(i)]).then_inc(s_fh[i % RF], 16)
                if i >= 1:
                    out(i - 1)
            out(NT - 1)
            sp.wait_ge(s_fout, 16 * (NT + 1))
            for s, v in ((s_kout, 48), (s_vout, 48), (s_cout, 48)):
                sp.wait_ge(s, v)

        def pool_f(pool, did):
            pool.wait_ge(s_ally, 1)

            def root(i):
                M = ROWS[i]
                pool.wait_ge(s_fq, i + 1)
                did(pool.tensor_scalar(fst[0:M, i % RF, 1:2], fst[0:M, i % RF, 0:1], 1.0 / D, EPS, ALU.mult, ALU.add))
                pool.wait_ge(s_pool, did.n[0])
                pool.tensor_tensor(fst[0:M, i % RF, 2:3], fst[0:M, i % RF, 1:2], C("mhalf", M)[:, 0:1], ALU.pow).then_inc(s_fr, 1)

            for i in range(NT):
                M = ROWS[i]
                if i >= RF:
                    pool.wait_ge(s_fs, 2 * (i - RF + 1))
                for c in range(2):
                    pool.indirect_dma_start(f_y[0:M, i % RF, c, :], None, y_dram,
                                            bass.IndirectOffsetOnAxis(ap=addr[0:M, NT * c + i:NT * c + i + 1], axis=0)).then_inc(s_fy[i % RF], 16)
                if i >= 2:
                    root(i - 2)
            root(NT - 2)
            root(NT - 1)

        def act_f(act):
            act.wait_ge(s_ally, 1)
            for i in range(NT):
                M = ROWS[i]
                act.wait_ge(s_fs, 2 * i + 2)
                if i >= 1:
                    act.wait_ge(s_fq, i)
                act.activation(f_junk[0:M, :], f_o[0:M, i % RF, :], ACT.Square, accum_out=fst[0:M, i % RF, 0:1]).then_inc(s_fq, 1)

        def dve_f(dve, did):
            dve.wait_ge(s_ally, 1)
            dve.wait_ge(s_gfin, 16)

            def norm(i):
                M, r = ROWS[i], i % RF
                dve.wait_ge(s_fr, i + 1)
                dve.scalar_tensor_tensor(f_o[0:M, r, :], f_o[0:M, r, :], fst[0:M, r, 2:3], g_fin[0:M, :], ALU.mult, ALU.mult).then_inc(s_fn, 1)

            for i in range(NT):
                M, r = ROWS[i], i % RF
                dve.wait_ge(s_fh[r], 16 * (i // RF + 1))
                dve.wait_ge(s_fy[r], 32 * (i // RF + 1))
                if i >= RF:
                    dve.wait_ge(s_fout, 16 * (i - RF + 1))
                for c in range(2):
                    dve.scalar_tensor_tensor(f_o[0:M, r, :], f_y[0:M, r, c, :], gate_w[0:M, c, i:i + 1], (f_h[0:M, r, :], f_o[0:M, r, :])[c],
                                             ALU.mult, ALU.add).then_inc(s_fs, 1)
                    if c == 0:
                        dve.wait_ge(s_fs, 2 * i + 1)
                if i >= 1:
                    norm(i - 1)
            norm(NT - 1)

        block = ctx.enter_context(nc.Block())

        @block.sync
        def _(sp):
            sync_ab(sp)
            sync_c(sp)
            sync_d(sp)
            sp_m(sp)
            sp_f(sp)

        @block.gpsimd
        def _(pool):
            did = tally(s_pool)
            pool_ab(pool, did)
            pool_c(pool, did)
            pool_pages(pool, did)
            pool_values(pool, did)
            pool_sample_out(pool, did)
            pool_d(pool, did)
            pool_m(pool)
            pool_f(pool, did)

        @block.scalar
        def _(act):
            act_ab(act)
            act_queries(act)
            act_flip(act)
            act_sample(act)
            act_d(act)
            act_r(act)
            act_m(act)
            act_f(act)

        @block.tensor
        def _(pe):
            pe_ab(pe)
            pe_c(pe)
            pe_sample_scores(pe)
            pe_flip(pe)
            pe_sample_weights(pe)
            for b in range(DEC):
                pe_sample_values(pe, b)
            pe_sample_out(pe)
            pe_d(pe)
            pe_r(pe)
            pe_m(pe)

        @block.vector
        def _(dve):
            did = tally(s_step)
            dve_ab(dve, did)
            dve_c(dve, did)
            dve_sample_softmax(dve, did)
            dve_sample_out(dve, did)
            dve.sem_inc(s_be, 1)
            dve_d(dve, did)
            dve_r(dve, did)
            dve_m(dve)
            dve_f(dve, did)


_OUTS = {"y_prompt": (1, SEQ, D), "y_sample": (DEC, 1, D), "k_prompt": (1, 1, PROMPT, H, 2, DH), "v_prompt": (1, 1, PROMPT, H, P),
         "conv_prompt": (1, 1, 2, WC), "k_sample": (1, DEC, 1, H, 2, DH), "v_sample": (1, DEC, 1, H, P), "conv_sample": (1, DEC, 2, WC)}


def kernel(**inputs):
    import concourse.bacc as bacc
    from concourse.bass_utils import run_bass_kernel_spmd

    nc = bacc.Bacc("TRN2", target_bir_lowering=False, num_devices=1)
    arrays = {f"in_{k}": np.ascontiguousarray(a) for k, a in inputs.items()}
    ins = {k: nc.dram_tensor(f"in_{k}", arrays[f"in_{k}"].shape, mybir.dt.from_np(arrays[f"in_{k}"].dtype), kind="ExternalInput").ap()
           for k in inputs}
    outs = {k: nc.dram_tensor(f"out_{k}", shape, F32, kind="ExternalOutput").ap() for k, shape in _OUTS.items()}
    step_kernel(nc, ins, outs)
    got = run_bass_kernel_spmd(nc, [arrays], core_ids=[0]).results[0]
    return tuple(got[f"out_{k}"] for k in _OUTS)
```

```python
from contextlib import ExitStack
import math

import numpy as np
import concourse.bass as bass
from concourse import mybir

F32 = mybir.dt.float32
F32R = mybir.dt.float32r
I32 = mybir.dt.int32
ALU = mybir.AluOpType
ACT = mybir.ActivationFunctionType
AX = mybir.AxisListType

P = 128
D = 1024
SEQ, META, DEC = 1024, 16, 8
TOK = META + SEQ + DEC
PROMPT = META + SEQ
NT = -(-TOK // P)
ROWS = [min(P, TOK - P * i) for i in range(NT)]
LAST = ROWS[-1]
TAIL = PROMPT - P * (NT - 1)
KC = D // P
H = 4
DH = 64
QKW = H * 2 * DH
WC = 512
CJ = WC // P
NE, NG, EPG = 32, 4, 8
FF = 256
LAM_INIT = 0.8 - 0.6 * math.exp(0.0)
EPS = 1e-5
CHUNKS = [(0, 350), (350, 350), (700, 348)]
STRIP = P * NT
GW = 1280
PAGES = 2
PAST = PAGES * P
MAXB = 48
XB = MAXB - NE
BIG = 1.0e30


def t5_bucket(n):
    n = np.asarray(n)
    nf = np.maximum(n, 16).astype(np.float32)
    log_b = 16 + (np.log(nf / np.float32(16)) / np.float32(math.log(8.0)) * np.float32(16)).astype(np.int32)
    return np.where(n < 16, n, np.minimum(log_b, 31))


def constants():
    cols, at = [], {}

    def put(name, a):
        a = np.broadcast_to(np.asarray(a, np.float32), (P, np.shape(a)[-1]))
        at[name] = (sum(c.shape[1] for c in cols), a.shape[1])
        cols.append(a)

    r = np.arange(P)
    put("ident", np.eye(P))
    put("flip", np.eye(P)[::-1])
    put("before", (r[:, None] < r[None, :]).astype(np.float32))
    put("ones", np.ones(P))
    put("iota128", r)
    row = r[:, None] + P * np.arange(NT)[None, :]
    put("token1", np.where(row < TOK, row + 1, 0))
    put("over", P * (np.arange(8) + 1))
    put("iotax", np.arange(XB))
    put("iotag", np.repeat(np.arange(NG), EPG))
    put("valid", (r[:, None] + P * np.arange(NT)[None, :] < TOK).astype(np.float32))
    put("even", (r[:, None] % 2 == 0).astype(np.float32))
    put("odd", (r[:, None] % 2 == 1).astype(np.float32))
    put("pair", (r[:, None] // 2 == np.arange(32)[None, :]).astype(np.float32))
    put("mhalf", np.full(NT * 4, -0.5))
    put("eps", [EPS])
    table = np.concatenate(cols, 1)
    dist = (STRIP - 1) - np.arange(GW)
    hot = np.zeros((NE + 1, GW), np.float32)
    hot[np.where(dist >= 0, t5_bucket(np.maximum(dist, 0)), NE), np.arange(GW)] = 1.0
    prefix = np.broadcast_to((np.arange(NE)[None, :] < np.arange(NE)[:, None]).astype(np.float32).ravel(), (P, NE * NE)).copy()
    return table, at, hot, prefix


def step_kernel(nc, I, O):
    table, CAT, hot, prefix = constants()
    NCST = table.shape[1]
    c_table = nc.inline_tensor(table, "c_table").ap()
    c_hot = nc.inline_tensor(hot, "c_hot").ap()
    c_prefix = nc.inline_tensor(prefix, "c_prefix").ap()

    def dram(name, shape, dt=F32):
        return nc.dram_tensor(name, shape, dt, kind="Internal").ap()

    g_dram = dram("bias_by_distance", (H, GW))
    hp_dram = dram("residual_part", (TOK, D))
    qs_dram = dram("sample_queries", (DEC, QKW))
    os_dram = dram("sample_heads", (DEC * H, P))
    h_dram = dram("residual", (TOK, D))
    hn_dram = dram("normed", (TOK, D))
    strip_dram = dram("bias_strips", (P, H * STRIP))
    y_dram = dram("expert_rows", (P * MAXB, D))

    ctx = ExitStack()
    with ctx:
        cursor = [nc.sbuf_base + (-nc.sbuf_base) % 64]

        def at(name, shape, dt, offset):
            return nc.alloc_sbuf_tensor_at(name, shape, dt, offset=offset)

        def region(nbytes):
            o = cursor[0]
            cursor[0] = o + nbytes + (-nbytes) % 64
            assert cursor[0] <= nc.sbuf_usable_end, (cursor[0], nc.sbuf_usable_end)
            return o

        def keep(name, shape, dt=F32):
            size = 4 * int(np.prod(shape[1:]))
            return at(name, shape, dt, region(size))

        def sem(name):
            return ctx.enter_context(nc.semaphore(name))

        def bank(name):
            return ctx.enter_context(nc.psum_tensor(name, [P, 512], F32))

        cst = keep("cst", [P, NCST])

        def C(name, rows=P):
            a, n = CAT[name if name != "iota32" else "iota128"]
            return cst[0:rows, a:a + n] if name != "iota32" else cst[0:rows, a:a + NE]

        ssq = keep("ssq", [P, NT])
        rstd = keep("rstd", [P, NT])
        lamw = keep("lamw", [P, 8])
        rel33 = keep("rel33", [NE + 1, H])
        conv_w = keep("conv_w_T", [P, CJ, 3])
        conv_g = keep("conv_g_T", [P, CJ])
        subln = keep("subln", [P, P])
        cssq = keep("cssq", [P, NT])
        crstd = keep("crstd", [P, NT])
        mean_eps = keep("mean_eps", [P, NT])
        stT = keep("stT", [P, CJ, 2 * DEC])
        utail = keep("utail", [P, CJ, 10])

        r_q = region(4 * H * TOK)
        r_k = region(4 * H * TOK)
        r_v = region(4 * NT * 512)
        r_chi = region(4 * CJ * TOK)
        r_clo = region(4 * CJ * TOK)
        r_nhi = region(4 * KC * TOK)
        r_nlo = region(4 * KC * TOK)
        r_w = region(6 * 4096)
        r_t = region(5 * 4224)

        qT = at("qT", [P, H, TOK], F32, r_q)
        kT = at("kT", [P, H, TOK], F32, r_k)
        v_tok = at("v_tok", [P, NT, 512], F32, r_v)
        c_hi = at("c_hi", [P, CJ, TOK], F32R, r_chi)
        c_lo = at("c_lo", [P, CJ, TOK], F32R, r_clo)
        n_hi = at("n_hi", [P, KC, TOK], F32R, r_nhi)
        n_lo = at("n_lo", [P, KC, TOK], F32R, r_nlo)
        w_raw = at("w_raw", [P, 2, KC * P], F32, r_w)
        w_hi = at("w_hi", [P, 2, KC * P], F32R, r_w + 8192)
        w_lo = at("w_lo", [P, 2, KC * P], F32R, r_w + 16384)
        xn = at("xn", [P, 2, D], F32, r_chi)
        g_in = at("g_in", [P, D], F32, r_chi + 8192)
        k_tok = at("k_tok", [P, NT, 512], F32, r_chi + 12288)
        strip_in = at("strip_in", [P, H * STRIP], F32, r_chi + 12288)
        NF = H * STRIP // 512
        xt = at("xt", [P, 3, D], F32, r_t + 8448)
        k_cur = at("k_cur", [P, TOK], F32, r_t)
        v_cur = at("v_cur", [P, TOK], F32, r_t + 4224)
        u_ext = at("u_ext", [P, 2 + TOK], F32, r_t)
        h_cur = at("h_cur", [P, TOK], F32, r_t + 4224)
        cv = at("cv", [P, TOK], F32, r_t + 8448)
        y_cur = at("y_cur", [P, TOK], F32, r_t + 12672)
        y_sq = at("y_sq", [P, TOK], F32, r_t + 16896)
        r_s = region(4 * TOK)
        c_ssum = at("c_ssum", [P, TOK], F32, r_s)
        wc_hi = at("wc_hi", [P, 4, D], F32R, r_nhi)
        wc_lo = at("wc_lo", [P, 4, D], F32R, r_nhi + 16384)
        wa_hi = at("wa_hi", [P, 4, D], F32R, r_nlo)
        wa_lo = at("wa_lo", [P, 4, D], F32R, r_nlo + 16384)
        xr = at("xr", [P, 2, D], F32, r_t)
        hp = at("hp", [P, 2, D], F32, r_t + 8192)
        st_rows = at("st_rows", [2 * DEC, WC], F32, r_k)
        out10 = at("out10", [10, WC], F32, r_t + 16896)
        hot_sb = at("hot_sb", [NE + 1, GW], F32, r_v)
        g_sb = at("g_sb", [H, GW], F32, r_v + 5120)
        lq = at("lq", [P, 4, DH], F32, r_v + 10240)
        lj = at("lj", [P, DH], F32, r_v + 11264)

        pj = [bank(f"pj{i}") for i in range(6)]
        tp = [bank(f"tp{i}") for i in range(2)]

        def rows_of(i, x0=0):
            xp, xs = I["x_prompt"][0], I["x_sample"].rearrange("b t d -> (b t) d")
            if i == 0:
                return [(0, META, I["meta_tokens"]), (META, P, xp[0:P - META])]
            if i == NT - 1:
                return [(0, TAIL, xp[P * i - META:SEQ]), (TAIL, TAIL + DEC, xs)]
            return [(0, P, xp[P * i - META:P * (i + 1) - META])]

        def cols(i):
            return slice(P * i, P * i + ROWS[i])

        logits = keep("logits", [P, NT, NG + NE])
        zero_row = logits[:].rearrange("p t c -> p (t c)")[:, 0:256]
        s_fill = sem("s_fill")
        s_const = sem("s_const")
        s_early = sem("s_early")
        s_x = [sem(f"s_x{i}") for i in range(3)]
        s_zero = sem("s_zero")
        s_lam = sem("s_lam")
        s_lexp = sem("s_lexp")
        s_ssq = sem("s_ssq")
        s_pool = sem("s_pool")
        s_rstd = sem("s_rstd")
        s_xn = sem("s_xn")
        s_trA = sem("s_trA")
        s_nhi = sem("s_nhi")
        s_nlo = sem("s_nlo")
        s_bias = sem("s_bias")
        s_gsb = sem("s_gsb")
        s_strip_in = sem("s_strip_in")
        s_flip = sem("s_flip")
        s_flipped = sem("s_flipped")
        s_stripd = sem("s_stripd")
        s_gd = sem("s_gd")
        s_stT = sem("s_stT")
        s_w = [sem("s_w0"), sem("s_w1")]
        s_whi = sem("s_whi")
        s_wlo = sem("s_wlo")
        s_mm = sem("s_mm")
        s_ev = [sem("s_ev0"), sem("s_ev1")]
        s_tr = sem("s_tr")
        s_trev = sem("s_trev")
        s_kcp = sem("s_kcp")
        s_step = sem("s_step")
        s_y = sem("s_y")
        s_kout = sem("s_kout")
        s_vout = sem("s_vout")
        s_cssq = sem("s_cssq")
        s_crstd = sem("s_crstd")
        s_utr = sem("s_utr")
        s_out10 = sem("s_out10")
        s_cout = sem("s_cout")
        s_xr = [sem("s_xr0"), sem("s_xr1")]
        s_c = sem("s_c")
        s_hp = sem("s_hp")
        s_hpout = [sem("s_hpout0"), sem("s_hpout1")]
        s_clo = sem("s_clo")

        NB = 6 * H

        def tally(s):
            n = [0]

            def did(ins):
                ins.then_inc(s, 1)
                n[0] = n[0] + 1
                return n[0]
            did.n = n
            return did

        V0, K0, Q0 = 2 * QKW, QKW, 0
        GB0 = 2 * QKW + 512
        GC0, HC0 = GB0 + WC, GB0 + 2 * WC

        def early_loads(sp):
            dma = sp.dma_start
            dma(rel33[0:NE, :], I["rel_bias"]).then_inc(s_early, 16)
            dma(hot_sb[:], c_hot).then_inc(s_early, 16)
            dma(st_rows[:], I["state_conv"][0].rearrange("b s c -> (b s) c")).then_inc(s_early, 16)
            for m, name in enumerate(("lambda_q1", "lambda_k1", "lambda_q2", "lambda_k2")):
                dma(lq[:, m, :], bass.AP(tensor=I[name].tensor, offset=0, ap=[[0, P], [1, DH]])).then_inc(s_early, 16)
            dma(subln[:], bass.AP(tensor=I["attn_subln"].tensor, offset=0, ap=[[0, P], [1, P]])).then_inc(s_early, 16)
            with nc.allow_non_contiguous_dma(reason="small channel-major tables"):
                for t in range(3):
                    dma(conv_w[:, :, t], I["conv_w"][0, t].rearrange("(j p) -> p j", p=P)).then_inc(s_early, 16)
                dma(conv_g[:], I["conv_norm"][0].rearrange("(j p) -> p j", p=P)).then_inc(s_early, 16)

        def sync_ab(sp):
            for a, b, src in rows_of(0):
                sp.dma_start(xt[a:b, 0, :], src).then_inc(s_x[0], 16)
            sp.dma_start(cst[:], c_table).then_inc(s_const, 16)
            sp.dma_start(g_in[:], bass.AP(tensor=I["norm_attn"].tensor, offset=0, ap=[[0, P], [1, D]])).then_inc(s_const, 16)
            for i in range(1, NT):
                if i >= 3:
                    sp.wait_ge(s_xn, i - 2)
                for a, b, src in rows_of(i):
                    sp.dma_start(xt[a:b, i % 3, :], src).then_inc(s_x[i % 3], 16)
                if i == 2:
                    early_loads(sp)
            sp.wait_ge(s_gd, 16)
            for h in range(H):
                sp.dma_start(strip_in[:, STRIP * h:STRIP * (h + 1)], bass.AP(tensor=g_dram.tensor, offset=GW * h, ap=[[1, P], [1, STRIP]])).then_inc(s_strip_in, 16)
            def block_load(half, g, m):
                n = 12 * half + 6 * g + m
                sp.wait_ge(s_wlo, n + 1)
                if half == 0 or m < 2:
                    if half == 0 and m == 0:
                        sp.wait_ge(s_step, 3)
                    spare = NE + 12 * half + (6, 2)[half] * g + m
                    sp.dma_start(y_dram.rearrange("(p b) (q c) -> p b q c", b=MAXB, c=256)[:, bass.ds(spare, 1)].rearrange("p a q c -> p (a q) c"),
                                 bass.AP(tensor=zero_row.tensor, offset=zero_row.offset, ap=[list(zero_row.ap[0]), [0, 4], [1, 256]])).then_inc(s_fill, 16)
                col = ([V0, K0, Q0], [HC0, GC0, GB0])[half][m % 3] + 256 * g + 128 * (m // 3)
                src = I["w_in"][0].rearrange("(k p) c -> p k c", p=P)[:, :, bass.ds(col, P)]
                sp.dma_start(w_raw[:, m % 2, :].rearrange("p (k c) -> p k c", k=KC), src).then_inc(s_w[m % 2], 16)

            with sp.Fori(0, 2) as g:
                for m in range(6):
                    block_load(0, g, m)
            for m in range(12):
                if m == 3:
                    sp.wait_ge(s_trev, 1 + 6 * H)
                    for t_out, s_out, src, s in (("k_prompt", "k_sample", k_tok, s_kout), ("v_prompt", "v_sample", v_tok, s_vout)):
                        form = "t a b c -> t (a b c)" if src is k_tok else "t a b -> t (a b)"
                        rows, samp = O[t_out][0, 0].rearrange(form), O[s_out][0, :, 0].rearrange(form)
                        sp.dma_start(rows[0:P * (NT - 1)].rearrange("(i p) c -> p i c", p=P), src[:, 0:NT - 1, :]).then_inc(s, 16)
                        sp.dma_start(rows[P * (NT - 1):PROMPT], src[0:TAIL, NT - 1, :]).then_inc(s, 16)
                        sp.dma_start(samp, src[TAIL:TAIL + DEC, NT - 1, :]).then_inc(s, 16)
                block_load(1, m // 6, m % 6)
            wout = I["w_out"][0]
            for m in range(8):
                n = NB + m
                sp.wait_ge(s_wlo, n + 1)
                k = (m + 4) % 8
                if m == 4:
                    sp.wait_ge(s_clo, CJ)
                    load_rows(sp, 0)
                    load_rows(sp, 1)
                sp.dma_start(w_raw[:, m % 2, :], wout[P * k:P * (k + 1)]).then_inc(s_w[m % 2], 16)

        def sync_c(sp):
            sp.wait_ge(s_out10, 1)
            sp.dma_start(O["conv_prompt"][0, 0], out10[0:2, :]).then_inc(s_cout, 16)
            sp.dma_start(O["conv_sample"][0, :, 1], out10[2:10, :]).then_inc(s_cout, 16)
            sp.dma_start(O["conv_sample"][0, :, 0], I["state_conv"][0, :, 1]).then_inc(s_cout, 16)
            for i in range(NT):
                if i == 3:
                    sync_sample(sp)
                if i == 4:
                    sync_values(sp, 0)
                    sync_values(sp, 1)
                if i >= 2:
                    sp.wait_ge(s_hp, i - 1)
                    load_rows(sp, i)
                if i >= 1:
                    store_hp(sp, i - 1)
            store_hp(sp, NT - 1)

        def load_rows(sp, i):
            for a, b, src in rows_of(i):
                sp.dma_start(xr[a:b, i % 2, :], src).then_inc(s_xr[i % 2], 16)

        def store_hp(sp, i):
            sp.wait_ge(s_hp, i + 1)
            sp.dma_start(hp_dram[cols(i)], hp[0:ROWS[i], i % 2, :]).then_inc(s_hpout[i % 2], 16)

        def xr_count(i, ring=2):
            return 16 * sum(len(rows_of(t)) for t in range(i % ring, i + 1, ring))

        def pool_ab(pool, did):
            pool.sem_inc(s_wlo, 2)
            pool.wait_ge(s_const, 32)
            for i in range(NT):
                M = ROWS[i]
                pool.wait_ge(s_ssq, i + 1)
                did(pool.tensor_scalar(mean_eps[0:M, i:i + 1], ssq[0:M, i:i + 1], 1.0 / D, EPS, ALU.mult, ALU.add))
                pool.wait_ge(s_pool, did.n[0])
                pool.tensor_tensor(rstd[0:M, i:i + 1], mean_eps[0:M, i:i + 1], C("mhalf", M)[:, 0:1], ALU.pow).then_inc(s_rstd, 1)
            for half in range(2):
                with pool.Fori(0, 2) as g:
                    for m in range(6):
                        n = 12 * half + 6 * g + m
                        pool.wait_ge(s_whi, n + 1)
                        pool.tensor_tensor(w_lo[:, m % 2, :], w_raw[:, m % 2, :], w_hi[:, m % 2, :].bitcast(F32), ALU.subtract).then_inc(s_wlo, 1)
            for m in range(8):
                hi, lo = (wc_hi, wc_lo) if m < 4 else (wa_hi, wa_lo)
                if m == 3:
                    pool_c(pool, did)
                pool.wait_ge(s_whi, NB + m + 1)
                pool.tensor_tensor(lo[:, m % 4, :], w_raw[:, m % 2, :], hi[:, m % 4, :].bitcast(F32), ALU.subtract).then_inc(s_wlo, 1)

        def pool_c(pool, did):
            pool.wait_ge(s_cssq, 2)
            did(pool.tensor_scalar(mean_eps[:], cssq[:], 1.0 / WC, EPS, ALU.mult, ALU.add))
            pool.wait_ge(s_pool, did.n[0])
            pool.tensor_tensor(crstd[:], mean_eps[:], C("mhalf")[:, 0:NT], ALU.pow).then_inc(s_crstd, 1)

        def act_ab(act):
            def square(i):
                M = ROWS[i]
                act.wait_ge(s_x[i % 3], xr_count(i, 3))
                if i >= 1:
                    act.wait_ge(s_ssq, i)
                act.activation(c_ssum[0:M, 0:D], xt[0:M, i % 3, :], ACT.Square, accum_out=ssq[0:M, i:i + 1]).then_inc(s_ssq, 1)

            act.sem_inc(s_kcp, 1)
            square(0)
            for i in range(NT):
                M = ROWS[i]
                if i + 1 < NT:
                    square(i + 1)
                for b in range(2):
                    act.wait_ge(s_trA, 2 * i + b + 1)
                    act.activation(n_hi[:, 4 * b:4 * b + 4, cols(i)], tp[b][:].rearrange("p (c t) -> p c t", c=4)[:, :, 0:M], ACT.Copy).then_inc(s_nhi, 1)
                if i == 2:
                    for c in range(3):
                        a, b = 512 * c, min(GW, 512 * c + 512)
                        act.wait_ge(s_bias, c + 1)
                        act.activation(g_sb[:, a:b], pj[c][0:H, 0:b - a], ACT.Copy).then_inc(s_gsb, 1)
                    act.wait_ge(s_gsb, 3)
                    act.dma_start(g_dram, g_sb[:]).then_inc(s_gd, 16)
            act.wait_ge(s_lam, 2)
            act.activation(lamw[:, 2:4], lamw[:, 0:2], ACT.Exp).then_inc(s_lexp, 1)
            act.wait_ge(s_stT, 1)
            act.activation(stT[:].rearrange("p j s -> p (j s)"), pj[3][:, 0:CJ * 2 * DEC], ACT.Copy).then_inc(s_stT, 1)

            act.sem_inc(s_trev, 1)
            for n in range(NB):
                m, (h, kind) = n % 6, divmod(n - 2, 3)
                if n == 2:
                    act.wait_ge(s_flipped, NF)
                    act.dma_start(strip_dram, strip_in[:]).then_inc(s_stripd, 16)
                if n == 3:
                    act.wait_ge(s_gd, 16)
                    act.wait_ge(s_stripd, 16)
                if 0 <= h < H and kind == 1:
                    copy_tiles(act, 2 * h, v_tok, h)
                if 0 <= h < H and kind == 2:
                    copy_tiles(act, 2 * h + 1, k_tok, h)
                act.wait_ge(s_w[m % 2], 16 * (n // 2 + 1))
                act.wait_ge(s_mm, n + 1)
                act.activation(w_hi[:, m % 2, :], w_raw[:, m % 2, :], ACT.Copy).then_inc(s_whi, 1)
                if 0 <= h < H and kind == 1:
                    act.wait_ge(s_kev, h + 1)
                    act.activation(kT[:, h, :], k_cur[:], ACT.Copy).then_inc(s_kcp, 1)
            for m in range(8):
                hi = wc_hi if m < 4 else wa_hi
                act.wait_ge(s_w[m % 2], 16 * (12 + m // 2 + 1))
                if m == 0:
                    act.wait_ge(s_mm, 2 + NB)
                act.activation(hi[:, m % 4, :], w_raw[:, m % 2, :], ACT.Copy).then_inc(s_whi, 1)

        s_kev = sem("s_kev")

        def copy_tiles(act, e, dst, h):
            for q, (t0, t1) in enumerate(((0, 4), (4, 8), (8, 9))):
                act.wait_ge(s_tr, 3 * e + q + 1)
                M = P if t0 < 8 else LAST
                act.activation(dst[0:M, t0:t1, P * h:P * (h + 1)],
                               tp[q % 2][0:M, 0:P * (t1 - t0)].rearrange("p (t c) -> p t c", c=P), ACT.Copy).then_inc(s_trev, 1)

        def pe_ab(pe):
            pe.sem_inc(s_mm, 2)
            pe.wait_ge(s_const, 32)
            ident = C("ident")
            for i in range(NT):
                M = ROWS[i]
                pe.wait_ge(s_xn, i + 1)
                for b in range(2):
                    if i >= 1:
                        pe.wait_ge(s_nlo, 2 * (i - 1) + b + 1)
                    for c in range(4):
                        k = 4 * b + c
                        ins = pe.transpose(tp[b][:, P * c:P * c + M], xn[0:M, i % 2, P * k:P * (k + 1)], ident[0:M, 0:M])
                    ins.then_inc(s_trA, 1)
                if i == 2:
                    pe.wait_ge(s_early, 16 * 12)
                    pe.wait_ge(s_zero, 1)
                    for c in range(3):
                        a, b = 512 * c, min(GW, 512 * c + 512)
                        pe.matmul(pj[c][0:H, 0:b - a], rel33[:], hot_sb[:, a:b], start=True, stop=True).then_inc(s_bias, 1)
            for j in range(CJ):
                ins = pe.transpose(pj[3][:, 16 * j:16 * (j + 1)], st_rows[:, P * j:P * (j + 1)], ident[0:16, 0:16])
            ins.then_inc(s_stT, 1)
            pe.wait_ge(s_gsb, 3)
            pe.wait_ge(s_strip_in, 16 * H)
            for f in range(NF):
                if f >= 3:
                    pe.wait_ge(s_flipped, f - 2)
                pe.matmul(pj[f % 3][:], C("flip"), strip_in[:, 512 * f:512 * (f + 1)], start=True, stop=True).then_inc(s_flip, 1)
            pe.wait_ge(s_flipped, NF)
            pe.wait_ge(s_nlo, 2 * NT)
            pe.wait_ge(s_stT, 2)

            def block(n, m, slot):
                pe.wait_ge(s_wlo, n + 3)
                pe.wait_ge(s_ev[m % 2], slot + 1)
                bk = pj[3 * (m % 2):3 * (m % 2) + 3]
                for k in range(KC):
                    for a, (ws, xs) in enumerate(((w_hi, (n_hi, n_lo)), (w_lo, (n_hi,)))):
                        for x in xs:
                            for c, (t0, tn) in enumerate(CHUNKS):
                                ins = pe.matmul(bk[c][:, 0:tn], ws[:, m % 2, P * k:P * (k + 1)], x[:, k, t0:t0 + tn],
                                                start=(k == 0 and x is n_hi and a == 0), stop=(k == KC - 1 and a == 1))
                ins.then_inc(s_mm, 1)

            def to_rows(src, e):
                for q, (t0, t1) in enumerate(((0, 4), (4, 8), (8, 9))):
                    pe.wait_ge(s_trev, 3 * e + (1 if q == 0 else q))
                    for t in range(t0, t1):
                        M = ROWS[t]
                        ins = pe.transpose(tp[q % 2][0:M, P * (t - t0):P * (t - t0 + 1)], src[:, P * t:P * t + M], ident)
                    ins.then_inc(s_tr, 1)

            for half in range(2):
                with pe.Fori(0, 2) as g:
                    for m in range(6):
                        block(12 * half + 6 * g + m, m, 6 * half + 3 * g + m // 2)
                        h = 2 * g + m // 3
                        if not half and m % 3 == 1:
                            pe.wait_ge(s_vev, h + 1)
                            to_rows(v_cur, 2 * h)
                        if not half and m % 3 == 2:
                            pe.wait_ge(s_kev, h + 1)
                            to_rows(k_cur, 2 * h + 1)

        s_vev = sem("s_vev")

        def pe_c(pe):
            pe.wait_ge(s_ev[0], 1 + 12)
            pe.wait_ge(s_y, 1)
            for i in range(NT):
                M = ROWS[i]
                ins = pe.matmul(pj[0][0:M, i:i + 1], c_ssum[:, cols(i)], C("ones")[:, 0:1], start=True, stop=True)
            ins.then_inc(s_cssq, 1)
            for j in range(CJ):
                ins = pe.transpose(tp[0][0:10, P * j:P * (j + 1)], utail[:, j, :], C("ident"))
            ins.then_inc(s_utr, 1)
            pe_queries(pe)
            pe.wait_ge(s_clo, CJ)
            for i in range(NT):
                M = ROWS[i]
                if i >= 2:
                    pe.wait_ge(s_hp, i - 1)
                bk = pj[2 + 2 * (i % 2):4 + 2 * (i % 2)]
                for k in range(CJ):
                    if i == 0:
                        pe.wait_ge(s_wlo, 2 + NB + k + 1)
                    for a, (c, w) in enumerate(((c_hi, wc_hi), (c_hi, wc_lo), (c_lo, wc_hi))):
                        for b in range(2):
                            ins = pe.matmul(bk[b][0:M, :], c[:, k, cols(i)], w[:, k, 512 * b:512 * (b + 1)],
                                            start=(k == 0 and a == 0), stop=(k == CJ - 1 and a == 2))
                ins.then_inc(s_c, 1)

        def dve_ab(dve, did):
            def settle():
                dve.wait_ge(s_step, did.n[0])
            dve.sem_inc(s_ev[0], 1)
            dve.sem_inc(s_ev[1], 1)
            did(dve.memset(rel33[NE:NE + 1, :], -BIG))
            dve.wait_ge(s_step, did.n[0])
            dve.memset(cssq[:], 1.0).then_inc(s_zero, 1)
            dve.wait_ge(s_const, 32)

            def norm(i):
                M = ROWS[i]
                dve.wait_ge(s_rstd, i + 1)
                if i >= 2:
                    dve.wait_ge(s_trA, 2 * (i - 1))
                dve.scalar_tensor_tensor(xn[0:M, i % 2, :], xt[0:M, i % 3, :], rstd[0:M, i:i + 1], g_in[0:M, :], ALU.mult, ALU.mult).then_inc(s_xn, 1)

            norm(0)
            norm(1)
            dve.wait_ge(s_early, 16 * 12)
            did(dve.tensor_scalar(subln[:], subln[:], 1.0 - LAM_INIT, None, ALU.mult))
            did(dve.memset(logits[:], 0.0))
            dve.wait_ge(s_step, did.n[0])
            for m in range(2):
                dve.tensor_tensor_reduce(out=lj[:], in0=lq[:, 2 * m, :], in1=lq[:, 2 * m + 1, :], scale=1.0, scalar=0.0,
                                         op0=ALU.mult, op1=ALU.add, accum_out=lamw[:, m:m + 1]).then_inc(s_lam, 1)
                dve.wait_ge(s_lam, m + 1)
            for i in range(NT):
                M = ROWS[i]
                if 1 < i + 1 < NT:
                    norm(i + 1)
                for b in range(2):
                    dve.wait_ge(s_nhi, 2 * i + b + 1)
                    dve.tensor_tensor(n_lo[:, 4 * b:4 * b + 4, cols(i)], tp[b][:].rearrange("p (c t) -> p c t", c=4)[:, :, 0:M],
                                      n_hi[:, 4 * b:4 * b + 4, cols(i)].bitcast(F32), ALU.subtract).then_inc(s_nlo, 1)
            for f in range(NF):
                dve.wait_ge(s_flip, f + 1)
                dve.tensor_copy(strip_in[:, 512 * f:512 * (f + 1)], pj[f % 3][:]).then_inc(s_flipped, 1)
            dve.wait_ge(s_lexp, 1)
            dve.scalar_tensor_tensor(lamw[:, 4:5], lamw[:, 3:4], -LAM_INIT, lamw[:, 2:3], ALU.add, ALU.subtract).then_inc(s_lam, 1)

            with dve.Fori(0, 2) as g:
                for m in range(6):
                    n = 6 * g + m
                    h = 2 * g + m // 3
                    dve.wait_ge(s_mm, n + 3)
                    if m % 3 < 2:
                        dve.wait_ge(s_trev, 6 * h + 1)
                    if m % 3 == 1:
                        dve.wait_ge(s_kcp, h + 1)
                    for c, (t0, tn) in enumerate(CHUNKS):
                        src = pj[3 * (m % 2) + c][:, 0:tn]
                        if m % 3 == 2:
                            ins = dve.tensor_scalar(qT[:, bass.ds(h, 1), t0:t0 + tn], src.rearrange("p (a t) -> p a t", a=1), DH ** -0.5, None, ALU.mult)
                        else:
                            ins = dve.tensor_copy((v_cur, k_cur)[m % 3][:, t0:t0 + tn], src)
                        if c < 2:
                            did(ins)
                    ins.then_inc(s_ev[m % 2], 1)
                    if m % 3 < 2:
                        dve.wait_ge(s_ev[m % 2], 3 * g + m // 2 + 2)
                        dve.wait_ge(s_step, 3 + 12 * g + 2 * m + 2)
                        dve.sem_inc((s_vev, s_kev)[m % 3], 1)
            did.n[0] = 3 + 24
            settle()
            dve.wait_ge(s_trev, 1 + 6 * H)
            dve.wait_ge(s_kcp, 1 + H)
            dve.wait_ge(s_nlo, 2 * NT)
            did(dve.memset(u_ext[:, 0:2], 0.0))
            did(dve.memset(c_ssum[:], 0.0))
            settle()
            N0 = did.n[0]
            with dve.Fori(0, 2) as g:
                did.n[0] = N0 + 2 * PER_J * g
                for jj in range(2):
                    j = 2 * g + jj
                    n0 = did.n[0]
                    evac_conv(dve, did, settle, g, jj, j)
            did.n[0] = N0 + 4 * PER_J
            settle()
            dve.sem_inc(s_y, 1)

        PER_J = 15

        def evac_conv(dve, did, settle, g, jj, j):
            m = 3 * jj
            par = m % 2
            count = [0]

            def step(ins):
                did(ins)
                count[0] += 1
            dve.wait_ge(s_mm, 12 + 6 * g + m + 3)
            for c, (t0, tn) in enumerate(CHUNKS):
                ins = dve.tensor_copy(h_cur[:, t0:t0 + tn], pj[3 * par + c][:, 0:tn])
                step(ins) if c < 2 else ins.then_inc(s_ev[par], 1)
            settle()
            dve.wait_ge(s_ev[par], 6 + 3 * g + m // 2 + 2)
            m += 1
            par = m % 2
            dve.wait_ge(s_mm, 12 + 6 * g + m + 3)
            for c, (t0, tn) in enumerate(CHUNKS):
                ins = dve.tensor_tensor(u_ext[:, 2 + t0:2 + t0 + tn], pj[3 * par + c][:, 0:tn], h_cur[:, t0:t0 + tn], ALU.mult)
                step(ins) if c < 2 else ins.then_inc(s_ev[par], 1)
            settle()
            dve.wait_ge(s_ev[par], 6 + 3 * g + m // 2 + 2)
            w = [conv_w[:, bass.ds(j, 1), t] for t in range(3)]
            S0 = PROMPT
            st = stT[:, bass.ds(j, 1), :].rearrange("p a (b s) -> p (a b) s", s=2)
            step(dve.tensor_scalar(cv[:, 0:S0], u_ext[:, 0:S0], w[0], None, ALU.mult))
            step(dve.tensor_scalar(cv[:, S0:TOK], st[:, :, 0], w[0], None, ALU.mult))
            step(dve.tensor_copy(utail[:, bass.ds(j, 1), :], u_ext[:, 2 + S0 - 2:2 + TOK].rearrange("p (a t) -> p a t", a=1)))
            settle()
            step(dve.scalar_tensor_tensor(cv[:, 0:S0], u_ext[:, 1:1 + S0], w[1], cv[:, 0:S0], ALU.mult, ALU.add))
            step(dve.scalar_tensor_tensor(cv[:, S0:TOK], st[:, :, 1], w[1], cv[:, S0:TOK], ALU.mult, ALU.add))
            settle()
            step(dve.scalar_tensor_tensor(cv[:, 0:TOK], u_ext[:, 2:2 + TOK], w[2], cv[:, 0:TOK], ALU.mult, ALU.add))
            settle()
            m += 1
            par = m % 2
            dve.wait_ge(s_mm, 12 + 6 * g + m + 3)
            for c, (t0, tn) in enumerate(CHUNKS):
                ins = dve.tensor_tensor(y_cur[:, t0:t0 + tn], pj[3 * par + c][:, 0:tn], cv[:, t0:t0 + tn], ALU.mult)
                step(ins) if c < 2 else ins.then_inc(s_ev[par], 1)
            settle()
            dve.wait_ge(s_ev[par], 6 + 3 * g + m // 2 + 2)
            dve.wait_ge(s_kout, 48)
            step(dve.tensor_scalar(c_hi[:, bass.ds(j, 1), :], y_cur[:].rearrange("p (a t) -> p a t", a=1), conv_g[:, bass.ds(j, 1)], None, ALU.mult))
            step(dve.tensor_tensor(y_sq[:], y_cur[:], y_cur[:], ALU.mult))
            settle()
            step(dve.tensor_tensor(c_ssum[:], c_ssum[:], y_sq[:], ALU.add))
            dve.scalar_tensor_tensor(c_lo[:, bass.ds(j, 1), :], y_cur[:].rearrange("p (a t) -> p a t", a=1), conv_g[:, bass.ds(j, 1)],
                                     c_hi[:, bass.ds(j, 1), :].bitcast(F32), ALU.mult, ALU.subtract).then_inc(s_clo, 1)
            dve.wait_ge(s_clo, j + 1)
            assert count[0] == PER_J, count

        PAGES_AT = (0, 1, 2, 2, 3, 3, 3, 2, 0)

        def dve_c(dve, did):
            dve.wait_ge(s_cssq, 1)
            dve.wait_ge(s_zero, 1)
            did(dve.tensor_copy(cssq[:, 0:NT - 1], pj[0][:, 0:NT - 1]))
            did(dve.tensor_copy(cssq[0:LAST, NT - 1:NT], pj[0][0:LAST, NT - 1:NT]))
            dve.wait_ge(s_step, did.n[0])
            dve.sem_inc(s_cssq, 1)
            dve.wait_ge(s_utr, 1)
            dve.tensor_copy(out10[:], tp[0][0:10, :]).then_inc(s_out10, 1)
            dve_queries(dve, did)
            dve.wait_ge(s_crstd, 1)
            for i in range(NT):
                M = ROWS[i]
                dve.wait_ge(s_c, i + 1)
                dve.wait_ge(s_xr[i % 2], xr_count(i))
                if i >= 2:
                    dve.wait_ge(s_hpout[i % 2], 16 * (i // 2))
                for b in range(2):
                    part = slice(512 * b, 512 * (b + 1))
                    ins = dve.scalar_tensor_tensor(hp[0:M, i % 2, part], pj[2 + 2 * (i % 2) + b][0:M, :], crstd[0:M, i:i + 1],
                                                   xr[0:M, i % 2, part], ALU.mult, ALU.add)
                    if b == 0:
                        did(ins)
                ins.then_inc(s_hp, 1)
                for n in range(sum(PAGES_AT[:i]), sum(PAGES_AT[:i + 1])):
                    dve_page(dve, did, n)

        NS = DEC * H * 2
        k_page = at("k_page", [P, 4, QKW], F32, r_w)
        q_all = at("q_all", [P, 2, QKW], F32, r_w + 8192)
        prod = at("prod", [P, QKW], F32, r_w + 12288)
        qs_rows = at("qs_rows", [DEC, QKW], F32, r_t + 18944)
        s_keys = keep("s_keys", [P, PAGES, NS])
        pages_sb = keep("pages_sb", [1, DEC * PAGES], I32)
        sp_o = [r_s]

        def tiny(name, shape, dt=F32):
            o = sp_o[0]
            sp_o[0] += 4 * int(np.prod(shape[1:])) + (-4 * int(np.prod(shape[1:]))) % 32
            assert sp_o[0] <= r_s + 4 * TOK
            return at(name, shape, dt, o)

        q64 = tiny("q64", [NS, DH])
        k64 = tiny("k64", [NS, DH])
        bias64 = tiny("bias64", [NS, PAST + 1])
        p64 = tiny("p64", [NS, PAST + 1])
        st64 = tiny("st64", [NS, 12])
        a_keys = tiny("a_keys", [P, PAGES, DEC * H])
        o_T = tiny("o_T", [P, DEC * H])
        v32 = tiny("v32", [DEC * H, P])
        o32 = tiny("o32", [DEC * H, P])
        st32 = tiny("st32", [DEC * H, 8])
        v_page = [at(f"v_page{i}", [P, QKW], F32, r_w + 18432 + 2048 * i) for i in range(3)] + [at("v_page3", [P, QKW], F32, r_t + 19072)]

        s_pt = sem("s_pt")
        s_k4 = [sem("s_k4_0"), sem("s_k4_1")]
        s_v4 = [sem("s_v4_0"), sem("s_v4_1")]
        s_qstr = sem("s_qstr")
        s_qsr = sem("s_qsr")
        s_qsd = sem("s_qsd")
        s_qall = [sem("s_qall0"), sem("s_qall1")]
        s_s64 = sem("s_s64")
        s_pair = sem("s_pair")
        s_p64 = sem("s_p64")
        s_e64 = sem("s_e64")
        s_ak = sem("s_ak")
        s_pvs = sem("s_pvs")
        s_oT = sem("s_oT")
        s_o32 = sem("s_o32")
        s_r32 = sem("s_r32")
        s_q32 = sem("s_q32")
        s_osd = sem("s_osd")
        s_strip = [sem(f"s_strip{h}") for h in range(H)]

        kp_rows = I["cache_k"][0].rearrange("n s a b c -> n s (a b c)")
        vp_rows = I["cache_v"][0].rearrange("n s a b -> n s (a b)")

        def act_pages(act):
            act.dma_start(pages_sb[:], I["page_table"].rearrange("(o b) n -> o (b n)", o=1)).then_inc(s_pt, 16)
            act.wait_ge(s_qsr, 1)
            act.dma_start(qs_dram, qs_rows[:]).then_inc(s_qsd, 16)
            act.wait_ge(s_pt, 16)
            act.wait_ge(s_wlo, 2 + NB + 8)
            act.wait_ge(s_qsd, 16)
            for n in range(DEC * PAGES):
                b = n // PAGES
                page = act.value_load(pages_sb[0:1, n:n + 1], min_val=0, max_val=I["cache_k"].shape[1] - 1)
                if n >= 4:
                    act.wait_ge(s_pair, n - 3)
                if n % PAGES == 0:
                    if n >= 4:
                        act.wait_ge(s_pair, n - 2)
                    act.dma_start(q_all[:, b % 2, :], bass.AP(tensor=qs_dram.tensor, offset=QKW * b, ap=[[0, P], [1, QKW]])).then_inc(s_qall[b % 2], 16)
                act.dma_start(k_page[:, n % 4, :], kp_rows[bass.ds(page, 1)].rearrange("a s c -> (a s) c")).then_inc(s_k4[b % 2], 16)

        def sync_sample(sp):
            sp.wait_ge(s_cssq, 1)
            for b in range(DEC):
                src = bass.AP(tensor=g_dram.tensor, offset=STRIP - 1 - PAST, ap=[[GW, H], [0, 2], [1, PAST + 1]])
                sp.dma_start(bias64[8 * b:8 * b + 8, :], src).then_inc(s_s64, 16)
            sp.wait_ge(s_qsd, 16)
            sp.wait_ge(s_kout, 48)
            sp.wait_ge(s_vout, 48)
            sp.dma_start(q64[:], qs_dram.rearrange("b (g d) -> (b g) d", d=DH)).then_inc(s_s64, 16)
            sp.dma_start(k64[:], O["k_sample"][0, :, 0].rearrange("b h c d -> (b h c) d")).then_inc(s_s64, 16)
            sp.dma_start(v32[:], O["v_sample"][0, :, 0].rearrange("b h d -> (b h) d")).then_inc(s_s64, 16)

        S64 = 16 * (DEC + 3)

        def sync_values(sp, b):
            for n in (PAGES * b, PAGES * b + 1):
                page = sp.value_load(pages_sb[0:1, n:n + 1], min_val=0, max_val=I["cache_v"].shape[1] - 1)
                if n >= 4:
                    sp.wait_ge(s_pvs, n - 3)
                sp.dma_start(v_page[n % 4][:], vp_rows[bass.ds(page, 1)].rearrange("a s c -> (a s) c")).then_inc(s_v4[b % 2], 16)

        def pe_queries(pe):
            for h in range(H):
                ins = pe.transpose(tp[1][0:DEC, P * h:P * (h + 1)], qT[:, h, PROMPT:TOK], C("ident"))
            ins.then_inc(s_qstr, 1)

        def dve_queries(dve, did):
            dve.wait_ge(s_qstr, 1)
            dve.tensor_copy(qs_rows[:], tp[1][0:DEC, :]).then_inc(s_qsr, 1)

        def dve_page(dve, did, n):
            b, g = n // PAGES, n % PAGES
            dve.wait_ge(s_k4[b % 2], 32 * (b // 2 + 1))
            dve.wait_ge(s_qall[b % 2], 16 * (b // 2 + 1))
            did(dve.tensor_tensor(prod[:], k_page[:, n % 4, :], q_all[:, b % 2, :], ALU.mult))
            dve.wait_ge(s_step, did.n[0])
            dve.tensor_reduce(s_keys[:, g, 8 * b:8 * b + 8], prod[:].rearrange("p (g d) -> p g d", d=DH), AX.X, ALU.add).then_inc(s_pair, 1)
            dve.wait_ge(s_pair, n + 1)

        S_SCORES, S_WEIGHTS, S_VALUES, S_OUT = 0, 2, 3, 3 + DEC + 1

        def sample_step(s):
            return s in (S_SCORES, S_WEIGHTS, S_OUT) or S_VALUES <= s < S_VALUES + DEC

        def pe_sample(pe, s, bk):
            if s == S_SCORES:
                pe.wait_ge(s_pair, DEC * PAGES)
                for g in range(PAGES):
                    ins = pe.transpose(bk[0:NS, P * g:P * (g + 1)], s_keys[:, g, :], C("ident"))
            elif s == S_WEIGHTS:
                pe.wait_ge(s_p64, 2)
                for g in range(PAGES):
                    pe.transpose(bk[:, NS * g:NS * (g + 1)], p64[:, P * g:P * (g + 1)], C("ident", NS)[:, 0:NS])
                ins = pe.matmul(bk[0:DEC * H, 256:257], C("pair", NS), p64[:, PAST:PAST + 1], start=True, stop=True)
            elif s == S_OUT:
                pe.wait_ge(s_oT, DEC)
                ins = pe.transpose(bk[0:DEC * H, 0:P], o_T[:], C("ident"))
            else:
                b = s - S_VALUES
                if b == 0:
                    pe.wait_ge(s_ak, 1)
                pe.wait_ge(s_v4[b % 2], 32 * (b // 2 + 1))
                for h in range(H):
                    for g in range(PAGES):
                        ins = pe.matmul(bk[:, h:h + 1], v_page[(PAGES * b + g) % 4][:, P * h:P * (h + 1)], a_keys[:, g, H * b + h:H * b + h + 1],
                                        start=(g == 0), stop=(g == PAGES - 1))
                ins.then_inc(s_sc, 1)
                pe.wait_ge(s_sc, SCU[("S", s, 0)] + 1)
                pe.sem_inc(s_pvs, 2)
                return
            ins.then_inc(s_sc, 1)

        def dve_sample(dve, did, s, bk):
            def settle():
                dve.wait_ge(s_step, did.n[0])
            if s == S_SCORES:
                dve.wait_ge(s_s64, S64)
                did(dve.tensor_tensor_reduce(out=q64[:], in0=q64[:], in1=k64[:], scale=1.0, scalar=0.0, op0=ALU.mult, op1=ALU.add, accum_out=st64[:, 0:1]))
                dve.tensor_tensor_reduce(out=p64[:, 0:PAST], in0=bk[0:NS, 0:PAST], in1=bias64[:, 0:PAST], scale=1.0, scalar=-3.0e38,
                                         op0=ALU.add, op1=ALU.max, accum_out=st64[:, 1:2]).then_inc(s_sb, 1)
                settle()
                did(dve.tensor_tensor(p64[:, PAST:PAST + 1], st64[:, 0:1], bias64[:, PAST:PAST + 1], ALU.add))
                dve.wait_ge(s_sb, SCU[("S", s, 0)] + 1)
                settle()
                did(dve.tensor_tensor(st64[:, 2:3], p64[:, PAST:PAST + 1], st64[:, 1:2], ALU.max))
                settle()
                dve.tensor_scalar(st64[:, 3:4], st64[:, 2:3], -1.0, None, ALU.mult).then_inc(s_p64, 1)
            elif s == S_WEIGHTS:
                did(dve.tensor_reduce(a_keys[:].rearrange("p g r -> p (g r)"), bk[:, 0:2 * NS].rearrange("p (r c) -> p r c", c=2), AX.X, ALU.add))
                dve.tensor_copy(st32[:, 0:1], bk[0:DEC * H, 256:257]).then_inc(s_sb, 1)
                settle()
                dve.sem_inc(s_ak, 1)
            elif s == S_OUT:
                dve.scalar_tensor_tensor(o32[:], v32[:], st32[:, 0:1], bk[0:DEC * H, 0:P], ALU.mult, ALU.add).then_inc(s_sb, 1)
                dve.wait_ge(s_sb, SCU[("S", s, 0)] + 1)
                dve.tensor_tensor_reduce(out=v32[:], in0=o32[:], in1=o32[:], scale=1.0, scalar=0.0, op0=ALU.mult, op1=ALU.add,
                                         accum_out=st32[:, 1:2]).then_inc(s_q32, 1)
            else:
                b = s - S_VALUES
                dve.tensor_copy(o_T[:, H * b:H * (b + 1)], bk[:, 0:H]).then_inc(s_sb, 1)
                dve.wait_ge(s_sb, SCU[("S", s, 0)] + 1)
                dve.sem_inc(s_oT, 1)

        def dve_sample_weights(dve, did):
            dve.wait_ge(s_e64, 1)
            did(dve.reciprocal(st64[:, 5:6], st64[:, 4:5]))
            did(dve.scalar_tensor_tensor(st64[:, 6:7], C("odd", NS), lamw[0:NS, 4:5], C("even", NS), ALU.mult, ALU.add))
            dve.wait_ge(s_step, did.n[0])
            did(dve.tensor_tensor(st64[:, 7:8], st64[:, 5:6], st64[:, 6:7], ALU.mult))
            dve.wait_ge(s_step, did.n[0])
            dve.tensor_scalar(p64[:], p64[:], st64[:, 7:8], None, ALU.mult).then_inc(s_p64, 1)

        def dve_sample_last(dve):
            dve.wait_ge(s_r32, 1)
            dve.scalar_tensor_tensor(o32[:], o32[:], st32[:, 3:4], subln[0:DEC * H, :], ALU.mult, ALU.mult).then_inc(s_o32, 1)

        def act_sample(act):
            act.wait_ge(s_p64, 1)
            act.activation(p64[:], p64[:], ACT.Exp, bias=st64[:, 3:4], accum_out=st64[:, 4:5]).then_inc(s_e64, 1)

        def pool_sample_root(pool, did):
            pool.wait_ge(s_q32, 1)
            did(pool.tensor_scalar(st32[:, 2:3], st32[:, 1:2], 1.0 / P, EPS, ALU.mult, ALU.add))
            pool.wait_ge(s_pool, did.n[0])
            pool.tensor_tensor(st32[:, 3:4], st32[:, 2:3], C("mhalf", DEC * H)[:, 0:1], ALU.pow).then_inc(s_r32, 1)

        def pool_sample_store(pool):
            pool.wait_ge(s_o32, 1)
            pool.dma_start(os_dram, o32[:]).then_inc(s_osd, 16)

        strip = at("strip", [P, H, STRIP], F32, r_w)
        SW = PROMPT
        SB = 3
        sc = at("sc", [P, SB, 2, SW], F32, r_nhi)
        o_sb = at("o_sb", [P, 2, H * P], F32, r_nhi + 8 * SB * SW)
        oT = at("oT", [P, H, P], F32, r_nhi + 8 * SB * SW + 4096)
        aT = at("aT", [P, 2, NT, P], F32, r_t + 9856)
        hp_in = at("hp_in", [P, 2, D], F32, r_chi)
        h_sb = at("h_sb", [P, 2, D], F32, r_chi + 8192)
        hn = at("hn", [P, 2, D], F32, r_chi + 16384)
        oT_hi = at("oT_hi", [P, H, P], F32R, r_chi + 24576)
        oT_lo = at("oT_lo", [P, H, P], F32R, r_chi + 26624)
        hnT = at("hnT", [P, KC, P], F32, r_chi + 28672)
        g_ffn = at("g_ffn", [P, D], F32, r_t)
        router = at("router", [P, KC, NG + NE], F32, r_t + 4096)
        junk = at("junk", [P, D], F32, r_t + 5248)
        junk_o = at("junk_o", [P, P], F32, r_t + 9344)
        UB = 5
        ust = keep("ust", [P, UB, 16])
        ost = keep("ost", [P, 2, 12])
        hst = keep("hst", [P, 2, 4])

        UNITS = [(i, h) for i in range(NT) for h in range(H)]
        NU = len(UNITS)

        def keys(i):
            return min(P * (i + 1), PROMPT)

        def q_rows(i):
            return TAIL if i == NT - 1 else P

        def pieces(i):
            n = keys(i)
            return [(c, k0, min(512, n - k0)) for c in range(2) for k0 in range(0, n, 512)]

        def groups(i):
            return [(b, min(b + 4, i + 1)) for b in range(0, i + 1, 4)]

        piece0 = [sum(len(pieces(i)) for i, _ in UNITS[:u]) for u in range(NU + 1)]

        bank_uses = []

        n_before_d = [0]
        s_sc = sem("s_sc")
        s_sb = sem("s_sb")
        s_nmx = sem("s_nmx")
        s_exp = sem("s_exp")
        s_a = sem("s_a")
        s_b = sem("s_b")
        s_be = sem("s_be")
        s_blo = sem("s_blo")
        s_o = sem("s_o")
        s_oe = sem("s_oe")
        s_ossq = sem("s_ossq")
        s_orstd = sem("s_orstd")
        s_on = sem("s_on")
        s_osin = sem("s_osin")
        s_hpi = [sem("s_hpi0"), sem("s_hpi1")]
        s_h = sem("s_h")
        s_hsq = sem("s_hsq")
        s_hrstd = sem("s_hrstd")
        s_hn = sem("s_hn")
        s_hst = [sem("s_hst0"), sem("s_hst1")]
        s_hnst = [sem("s_hnst0"), sem("s_hnst1")]
        s_lge = sem("s_lge")
        s_dconst = sem("s_dconst")

        L_T, L_PV, L_OE = 2, 3, 4
        L_ON, L_OT, L_H, L_HN, L_HT, L_LG = 5, 6, 7, 9, 10, 11

        def unit_at(s, lag):
            return s - lag if 0 <= s - lag < NU else None

        def tile_at(s, lag):
            i = (s - lag - 3) // H
            return i if (s - lag - 3) % H == 0 and 0 <= i < NT else None

        SLOTS = NU + L_LG + 1

        for s in range(SLOTS):
            if (u := unit_at(s, L_T)) is not None:
                for q in range(len(groups(UNITS[u][0]))):
                    bank_uses.append(("a", u, q))
            if (i := tile_at(s, L_OT)) is not None:
                bank_uses.append(("o", i, 0))
            if (i := tile_at(s, L_HT)) is not None:
                bank_uses += [("h", i, 0), ("h", i, 1)]
        USE = {u: n for n, u in enumerate(bank_uses)}
        SC_USES = []
        for s in range(SLOTS):
            if s < NU:
                SC_USES += [("s", s, n) for n in range(len(pieces(UNITS[s][0])))]
            if sample_step(s):
                SC_USES.append(("S", s, 0))
            if (i := tile_at(s, L_H)) is not None:
                SC_USES += [("w", i, 0), ("w", i, 1)]
            if (i := tile_at(s, L_LG)) is not None:
                SC_USES.append(("r", i, 0))
        SCU = {u: n for n, u in enumerate(SC_USES)}
        NR = 4
        ring = [pj[0], pj[1], pj[2], pj[5]]
        o_bank = [pj[3], pj[4]]

        def sync_d(sp):
            sp.wait_ge(s_wlo, 2 + NB + 8)
            sp.wait_ge(s_gd, 16)
            sp.wait_ge(s_pair, DEC * PAGES)
            sp.wait_ge(s_stripd, 16)
            for h in range(H):
                sp.dma_start(strip[:, h, :], strip_dram[:, STRIP * h:STRIP * (h + 1)]).then_inc(s_strip[h], 16)
            sp.wait_ge(s_hp, NT)
            sp.wait_ge(s_hpout[0], 16 * 5)
            sp.wait_ge(s_hpout[1], 16 * 4)
            sp.dma_start(g_ffn[:], bass.AP(tensor=I["norm_ffn"].tensor, offset=0, ap=[[0, P], [1, D]])).then_inc(s_dconst, 16)
            sp.dma_start(router[:, :, 0:NG], I["router_group"][0].rearrange("(k p) c -> p k c", p=P)).then_inc(s_dconst, 16)
            sp.dma_start(router[:, :, NG:NG + NE], I["router_expert"][0].rearrange("(k p) c -> p k c", p=P)).then_inc(s_dconst, 16)
            for i in range(NT):
                M = ROWS[i]
                if i >= 2:
                    sp.wait_ge(s_h, i - 1)
                sp.dma_start(hp_in[0:M, i % 2, :], hp_dram[cols(i)]).then_inc(s_hpi[i % 2], 16)
                if i == 1:
                    for b in range(2, DEC):
                        sync_values(sp, b)
                if i == NT - 1:
                    sample_rows(sp)
                    sp.wait_ge(s_o, NU)
                    first_experts(sp)
                if i >= 1:
                    store_tile(sp, i - 1)
            store_tile(sp, NT - 1)
            sp.wait_ge(s_lge, NT)
            sp.dma_start(c_pre[:], c_prefix.rearrange("p (a b) -> p a b", a=NE)).then_inc(s_dconst, 16)

        def sample_rows(sp):
            sp.wait_ge(s_fill, 16 * XB)
            sp.wait_ge(s_osd, 16)
            sp.wait_ge(s_b, USE[("o", NT - 3, 0)] + 1)
            sp.dma_start(o_sb[TAIL:TAIL + DEC, (NT - 1) % 2, :], os_dram.rearrange("(b h) d -> b (h d)", h=H)).then_inc(s_osin, 16)

        def store_tile(sp, i):
            M = ROWS[i]
            sp.wait_ge(s_h, i + 1)
            sp.dma_start(h_dram[cols(i)], h_sb[0:M, i % 2, :]).then_inc(s_hst[i % 2], 16)
            sp.wait_ge(s_hn, i + 1)
            sp.dma_start(hn_dram[cols(i)], hn[0:M, i % 2, :]).then_inc(s_hnst[i % 2], 16)

        def hp_stored(eng):
            eng.wait_ge(s_hpout[0], 16 * 5)
            eng.wait_ge(s_hpout[1], 16 * 4)

        def pe_d(pe):
            ident = C("ident")
            pe.wait_ge(s_be, 1)
            pe.wait_ge(s_hp, NT)
            pe.wait_ge(s_step, n_before_d[0])
            for s in range(SLOTS):
                if s < NU:
                    i, h = UNITS[s]
                    M = q_rows(i)
                    for n, (c, k0, kn) in enumerate(pieces(i)):
                        u = SCU[("s", s, n)]
                        if u >= NR:
                            pe.wait_ge(s_sb, u - NR + 1)
                        pe.matmul(ring[u % NR][0:M, 0:kn], qT[DH * c:DH * (c + 1), h, P * i:P * i + M],
                                  kT[DH * c:DH * (c + 1), h, k0:k0 + kn], start=True, stop=True).then_inc(s_sc, 1)
                if (t := unit_at(s, L_T)) is not None:
                    i, h = UNITS[t]
                    M = q_rows(i)
                    for q, (b0, b1) in enumerate(groups(i)):
                        u = USE[("a", t, q)]
                        if q == 0:
                            pe.wait_ge(s_a, t + 1)
                        if u >= 2:
                            pe.wait_ge(s_be, u)
                        for b in range(b0, b1):
                            kw = min(P, PROMPT - P * b)
                            ins = pe.transpose(tp[u % 2][0:kw, P * (b - b0):P * (b - b0) + M], sc[0:M, t % SB, 0, P * b:P * b + kw], ident[0:M, 0:M])
                        ins.then_inc(s_b, 1)
                if (t := unit_at(s, L_PV)) is not None:
                    i, h = UNITS[t]
                    M = q_rows(i)
                    pe.wait_ge(s_be, USE[("a", t, len(groups(i)) - 1)] + 2)
                    if t >= 2:
                        pe.wait_ge(s_oe, t - 1)
                    for b in range(i + 1):
                        kw = min(P, PROMPT - P * b)
                        ins = pe.matmul(o_bank[t % 2][0:M, 0:P], aT[0:kw, t % 2, b, 0:M], v_tok[0:kw, b, P * h:P * (h + 1)],
                                        start=(b == 0), stop=(b == i))
                    ins.then_inc(s_o, 1)
                if sample_step(s):
                    u = SCU[("S", s, 0)]
                    if u >= NR:
                        pe.wait_ge(s_sb, u - NR + 1)
                    pe_sample(pe, s, ring[u % NR])
                if (i := tile_at(s, L_OT)) is not None:
                    M = ROWS[i]
                    u = USE[("o", i, 0)]
                    pe.wait_ge(s_on, i + 1)
                    if i == NT - 1:
                        pe.wait_ge(s_osin, 16)
                    pe.wait_ge(s_be, u)
                    for h in range(H):
                        ins = pe.transpose(tp[u % 2][:, P * h:P * h + M], o_sb[0:M, i % 2, P * h:P * (h + 1)], ident[0:M, 0:M])
                    ins.then_inc(s_b, 1)
                if (i := tile_at(s, L_H)) is not None:
                    M = ROWS[i]
                    pe.wait_ge(s_blo, i + 1)
                    u0 = SCU[("w", i, 0)]
                    pe.wait_ge(s_sb, u0 + 1 - NR + 1)
                    for k in range(H):
                        for a, (c, w) in enumerate(((oT_hi, wa_hi), (oT_hi, wa_lo), (oT_lo, wa_hi))):
                            for b in range(2):
                                ins = pe.matmul(ring[(u0 + b) % NR][0:M, :], c[:, k, 0:M], w[:, k, 512 * b:512 * (b + 1)],
                                                start=(k == 0 and a == 0), stop=(k == H - 1 and a == 2))
                                if k == H - 1 and a == 2:
                                    ins.then_inc(s_sc, 1)
                if (i := tile_at(s, L_HT)) is not None:
                    M = ROWS[i]
                    pe.wait_ge(s_hn, i + 1)
                    for q in range(2):
                        u = USE[("h", i, q)]
                        pe.wait_ge(s_be, u)
                        for c in range(4):
                            k = 4 * q + c
                            ins = pe.transpose(tp[u % 2][:, P * c:P * c + M], hn[0:M, i % 2, P * k:P * (k + 1)], ident[0:M, 0:M])
                        ins.then_inc(s_b, 1)
                if (i := tile_at(s, L_LG)) is not None:
                    M = ROWS[i]
                    u = SCU[("r", i, 0)]
                    pe.wait_ge(s_be, USE[("h", i, 1)] + 2)
                    pe.wait_ge(s_sb, u - NR + 1)
                    if i == 0:
                        pe.wait_ge(s_dconst, 48)
                    for k in range(KC):
                        ins = pe.matmul(ring[u % NR][0:M, 0:NG + NE], hnT[:, k, 0:M], router[:, k, :], start=(k == 0), stop=(k == KC - 1))
                    ins.then_inc(s_sc, 1)

        def act_d(act):
            for s in range(SLOTS):
                if s == S_SCORES + 1:
                    act_sample(act)
                if (t := unit_at(s, L_T)) is not None:
                    i, h = UNITS[t]
                    M = q_rows(i)
                    if t == 0:
                        hp_stored(act)
                    if t >= 2:
                        act.wait_ge(s_o, t - 1)
                    for q, (b0, b1) in enumerate(groups(i)):
                        u = USE[("a", t, q)]
                        act.wait_ge(s_b, u + 1)
                        kw = min(P, PROMPT - P * (b1 - 1))
                        act.activation(aT[0:kw, t % 2, b0:b1, 0:M], tp[u % 2][0:kw, :].rearrange("p (b t) -> p b t", t=P)[:, 0:b1 - b0, 0:M], ACT.Copy).then_inc(s_be, 1)
                        assert kw == P or b1 == b0 + 1
                if s < NU:
                    i, h = UNITS[s]
                    M = q_rows(i)
                    act.wait_ge(s_nmx, s + 1)
                    for c in range(2):
                        act.activation(sc[0:M, s % SB, c, 0:keys(i)], sc[0:M, s % SB, c, 0:keys(i)], ACT.Exp, bias=ust[0:M, s % UB, 8 + c:9 + c],
                                       accum_out=ust[0:M, s % UB, 10 + c:11 + c]).then_inc(s_exp, 1)
                if (i := tile_at(s, L_OT)) is not None:
                    M = ROWS[i]
                    u = USE[("o", i, 0)]
                    act.wait_ge(s_b, u + 1)
                    if i >= 1:
                        act.wait_ge(s_sc, SCU[("w", i - 1, 1)] + 1)
                        act.wait_ge(s_blo, i)
                    src = tp[u % 2][:].rearrange("p (h t) -> p h t", h=H)[:, :, 0:M]
                    act.activation(oT_hi[:, :, 0:M], src, ACT.Copy).then_inc(s_othi, 1)
                    act.activation(oT[:, :, 0:M], src, ACT.Copy).then_inc(s_be, 1)
                if (i := tile_at(s, L_H + 1)) is not None:
                    M = ROWS[i]
                    act.wait_ge(s_h, i + 1)
                    if i == 0:
                        act.wait_ge(s_dconst, 48)
                    if i >= 1:
                        act.wait_ge(s_hsq, i)
                    act.activation(junk[0:M, :], h_sb[0:M, i % 2, :], ACT.Square, accum_out=hst[0:M, i % 2, 0:1]).then_inc(s_hsq, 1)
                if (i := tile_at(s, L_HT)) is not None:
                    M = ROWS[i]
                    if i >= 1:
                        act.wait_ge(s_sc, SCU[("r", i - 1, 0)] + 1)
                    for q in range(2):
                        u = USE[("h", i, q)]
                        act.wait_ge(s_b, u + 1)
                        act.activation(hnT[:, 4 * q:4 * q + 4, 0:M], tp[u % 2][:].rearrange("p (c t) -> p c t", c=4)[:, :, 0:M], ACT.Copy).then_inc(s_be, 1)

        s_othi = sem("s_othi")

        def pool_d(pool, did):
            for s in range(SLOTS):
                if s == S_OUT + 1:
                    pool_sample_root(pool, did)
                if s == S_OUT + 2:
                    pool_sample_store(pool)
                if (i := tile_at(s, L_OE)) is not None:
                    M = q_rows(i)
                    pool.wait_ge(s_ossq, H * (i + 1))
                    did(pool.tensor_scalar(ost[0:M, i % 2, 4:8], ost[0:M, i % 2, 0:4], 1.0 / P, EPS, ALU.mult, ALU.add))
                    pool.wait_ge(s_pool, did.n[0])
                    pool.tensor_tensor(ost[0:M, i % 2, 8:12], ost[0:M, i % 2, 4:8], C("mhalf", M)[:, 0:4], ALU.pow).then_inc(s_orstd, 1)
                if (i := tile_at(s, L_OT)) is not None:
                    M = ROWS[i]
                    pool.wait_ge(s_othi, i + 1)
                    pool.wait_ge(s_be, USE[("o", i, 0)] + 2)
                    pool.tensor_tensor(oT_lo[:, :, 0:M], oT[:, :, 0:M], oT_hi[:, :, 0:M].bitcast(F32), ALU.subtract).then_inc(s_blo, 1)
                if (i := tile_at(s, L_H + 1)) is not None:
                    M = ROWS[i]
                    pool.wait_ge(s_hsq, i + 1)
                    did(pool.tensor_scalar(hst[0:M, i % 2, 1:2], hst[0:M, i % 2, 0:1], 1.0 / D, EPS, ALU.mult, ALU.add))
                    pool.wait_ge(s_pool, did.n[0])
                    pool.tensor_tensor(hst[0:M, i % 2, 2:3], hst[0:M, i % 2, 1:2], C("mhalf", M)[:, 0:1], ALU.pow).then_inc(s_hrstd, 1)

        def dve_d(dve, did):
            n_before_d[0] = did.n[0]
            def settle():
                dve.wait_ge(s_step, did.n[0])
            dve.wait_ge(s_fill, 16 * XB)
            for s in range(SLOTS + 1):
                if s - 1 >= 0 and sample_step(s - 1):
                    u = SCU[("S", s - 1, 0)]
                    dve.wait_ge(s_sc, u + 1)
                    dve_sample(dve, did, s - 1, ring[u % NR])
                if s == S_WEIGHTS:
                    dve_sample_weights(dve, did)
                if s == S_OUT + 2:
                    dve_sample_last(dve)
                if (i := tile_at(s, L_H + 1)) is not None:
                    M = ROWS[i]
                    u0 = SCU[("w", i, 0)]
                    dve.wait_ge(s_sc, u0 + 2)
                    dve.wait_ge(s_hpi[i % 2], 16 * (i // 2 + 1))
                    if i >= 2:
                        dve.wait_ge(s_hst[i % 2], 16 * (i // 2))
                    for b in range(2):
                        part = slice(512 * b, 512 * (b + 1))
                        dve.tensor_tensor(h_sb[0:M, i % 2, part], ring[(u0 + b) % NR][0:M, :], hp_in[0:M, i % 2, part], ALU.add).then_inc(s_sb, 1)
                if (i := tile_at(s, L_LG + 1)) is not None:
                    M = ROWS[i]
                    u = SCU[("r", i, 0)]
                    dve.wait_ge(s_sc, u + 1)
                    dve.tensor_copy(logits[0:M, i, :], ring[u % NR][0:M, 0:NG + NE]).then_inc(s_sb, 1)
                if (t := unit_at(s, L_T)) is not None:
                    i, h = UNITS[t]
                    M, x = q_rows(i), t % UB
                    dve.wait_ge(s_exp, 2 * t + 2)
                    did(dve.reciprocal(ust[0:M, x, 12:14], ust[0:M, x, 10:12]))
                    settle()
                    did(dve.scalar_tensor_tensor(ust[0:M, x, 14:15], ust[0:M, x, 10:11], lamw[0:M, 4:5], ust[0:M, x, 13:14], ALU.mult, ALU.mult))
                    settle()
                    dve.scalar_tensor_tensor(sc[0:M, t % SB, 0, 0:keys(i)], sc[0:M, t % SB, 1, 0:keys(i)], ust[0:M, x, 14:15], sc[0:M, t % SB, 0, 0:keys(i)],
                                             ALU.mult, ALU.add).then_inc(s_a, 1)
                if (i := tile_at(s, L_H + 1)) is not None:
                    dve.wait_ge(s_sb, SCU[("w", i, 1)] + 1)
                    dve.sem_inc(s_h, 1)
                if (i := tile_at(s, L_LG + 1)) is not None:
                    dve.wait_ge(s_sb, SCU[("r", i, 0)] + 1)
                    dve.sem_inc(s_lge, 1)
                if s < NU:
                    i, h = UNITS[s]
                    M, x = q_rows(i), s % UB
                    ps = pieces(i)
                    half = len(ps) // 2
                    if i == 0:
                        dve.wait_ge(s_strip[h], 16)
                    if s >= SB:
                        i2 = UNITS[s - SB][0]
                        dve.wait_ge(s_b, USE[("a", s - SB, len(groups(i2)) - 1)] + 1)
                    for n, (c, k0, kn) in enumerate(ps):
                        u = SCU[("s", s, n)]
                        dve.wait_ge(s_sc, u + 1)
                        m0 = P * (NT - 1) - P * i + k0
                        col = c * half + (n - c * half)
                        dve.tensor_tensor_reduce(out=sc[0:M, s % SB, c, k0:k0 + kn], in0=ring[u % NR][0:M, 0:kn], in1=strip[0:M, h, m0:m0 + kn],
                                                 scale=1.0, scalar=-3.0e38, op0=ALU.add, op1=ALU.max, accum_out=ust[0:M, x, col:col + 1]).then_inc(s_sb, 1)
                    dve.wait_ge(s_sb, SCU[("s", s, len(ps) - 1)] + 1)
                    did(dve.tensor_reduce(ust[0:M, x, 6:8], ust[0:M, x, 0:2 * half].rearrange("p (c n) -> p c n", c=2), AX.X, ALU.max))
                    settle()
                    dve.tensor_scalar(ust[0:M, x, 8:10], ust[0:M, x, 6:8], -1.0, None, ALU.mult).then_inc(s_nmx, 1)
                if (t := unit_at(s, L_OE)) is not None:
                    i, h = UNITS[t]
                    M, x = q_rows(i), t % UB
                    if h == 0 and i >= 2:
                        dve.wait_ge(s_b, USE[("o", i - 2, 0)] + 1)
                    dve.wait_ge(s_o, t + 1)
                    dve.tensor_scalar(o_sb[0:M, i % 2, P * h:P * (h + 1)], o_bank[t % 2][0:M, 0:P], ust[0:M, x, 12:13], None, ALU.mult).then_inc(s_oe, 1)
                    dve.wait_ge(s_oe, t + 1)
                    if t >= 1:
                        dve.wait_ge(s_ossq, t)
                    else:
                        hp_stored(dve)
                    dve.tensor_tensor_reduce(out=junk_o[0:M, :], in0=o_sb[0:M, i % 2, P * h:P * (h + 1)], in1=o_sb[0:M, i % 2, P * h:P * (h + 1)],
                                             scale=1.0, scalar=0.0, op0=ALU.mult, op1=ALU.add, accum_out=ost[0:M, i % 2, h:h + 1]).then_inc(s_ossq, 1)
                if (i := tile_at(s, L_ON)) is not None:
                    M = q_rows(i)
                    dve.wait_ge(s_orstd, i + 1)
                    for h in range(H):
                        ins = dve.scalar_tensor_tensor(o_sb[0:M, i % 2, P * h:P * (h + 1)], o_sb[0:M, i % 2, P * h:P * (h + 1)], ost[0:M, i % 2, 8 + h:9 + h],
                                                       subln[0:M, :], ALU.mult, ALU.mult)
                        did(ins)
                    settle()
                    dve.sem_inc(s_on, 1)
                if (i := tile_at(s, L_HN)) is not None:
                    M = ROWS[i]
                    dve.wait_ge(s_hrstd, i + 1)
                    if i == 0:
                        dve.wait_ge(s_dconst, 48)
                    if i >= 2:
                        dve.wait_ge(s_hnst[i % 2], 16 * (i // 2))
                    dve.scalar_tensor_tensor(hn[0:M, i % 2, :], h_sb[0:M, i % 2, :], hst[0:M, i % 2, 2:3], g_ffn[0:M, :], ALU.mult, ALU.mult).then_inc(s_hn, 1)

        XMEM = r_chi + 4 * 4 * 6144
        SZ = 4 * 6144
        e_raw = at("e_raw", [P, 6, 2048], F32, r_q)
        e_hi = at("e_hi", [P, 2, 3, 2048], F32R, r_chi)
        e_lo = at("e_lo", [P, 2, 3, 2048], F32R, r_chi + 2 * SZ)
        xg = at("xg", [P, 2, D], F32, XMEM)
        xT_hi = at("xT_hi", [P, KC, P], F32R, XMEM + 8192)
        xT_lo = at("xT_lo", [P, KC, P], F32R, XMEM + 12288)
        yo = at("yo", [P, 2, D], F32, XMEM + 16384)
        sg = at("sg", [P, FF], F32, XMEM + 24576)
        hh = at("hh", [P, FF], F32, XMEM + 25600)
        hT_hi = at("hT_hi", [P, 2, P], F32R, XMEM + 26624)
        hT_lo = at("hT_lo", [P, 2, P], F32R, XMEM + 27648)
        rcur = [XMEM + 16384]

        def rt(name, shape, dt=F32):
            o = rcur[0]
            n = 4 * int(np.prod(shape[1:]))
            rcur[0] = o + n + (-n) % 32
            assert rcur[0] <= r_s + 4 * TOK, rcur[0] - r_s
            return at(name, shape, dt, o)

        A = NE * NT
        c_pre = rt("c_pre", [P, NE, NE])
        pre_nx = rt("pre_nx", [P, NE, NE])
        lem = rt("lem", [P, NT, NE])
        eq = rt("eq", [P, NT, NE])
        hot2 = rt("hot2", [P, 2, NT, NE])
        mark = rt("mark", [P, NT + 2, NE], F32R)
        grp = rt("grp", [P, 4, NT, NG])
        gs = rt("gs", [P, 8, NT])
        ms = rt("ms", [P, 2, NT])
        ei = rt("ei", [P, 2, NT])
        rk = rt("rk", [P, 8, 2, NT])
        beforeR = rt("beforeR", [P, P], F32R)
        onesR = rt("onesR", [P, P], F32R)
        big2 = at("big2", [P, 2, NT, NE], F32, XMEM + 8192)
        over2 = at("over2", [P, 2 * NT, 8], F32, XMEM + 12288)
        ranks = at("ranks", [P, NT + 1, NE], F32, XMEM + 13312)
        place_hot = at("place_hot", [P, 2 * NT, P], F32R, XMEM)
        block_tok = at("block_tok", [P, 2 * NT, MAXB], F32R, XMEM + 9216)
        block_hot = at("block_hot", [P, 2 * NT, MAXB], F32, XMEM + 12672)
        nxs = rt("nxs", [P, 4, NE])
        xl = at("xl", [P, XB, NE], F32, XMEM + 12672)
        xlf = rt("xlf", [P, XB + 1])
        gate_w = keep("gate_w", [P, 2, NT])
        addr = keep("addr", [P, 2 * NT], I32)
        slot_tok = keep("slot_tok", [P, MAXB], I32)
        xlist = keep("xlist", [P, XB + 1], I32)
        idx_cur = keep("idx_cur", [P, 2], I32)

        s_rx = sem("s_rx")
        s_re = sem("s_re")
        s_mark = sem("s_mark")
        s_rank = sem("s_rank")
        s_ph = sem("s_ph")
        s_phr = sem("s_phr")
        UC = 3
        slot_f = at("slot_f", [P, MAXB], F32, XMEM + 12672)
        s_pm = sem("s_pm")
        s_slots = sem("s_slots")

        def spread(ap, dims):
            return bass.AP(tensor=ap.tensor, offset=ap.offset, ap=[list(ap.ap[0])] + dims)

        def each(ap, n, inner):
            return spread(ap, [[1, n], [0, inner]])

        def over_rows(ap, outer, n):
            return spread(ap, [[0, outer], [1, n]])

        def dve_r(dve, did):
            def settle():
                dve.wait_ge(s_step, did.n[0])

            def do(ins):
                did(ins)
                settle()
            dve.wait_ge(s_hsq, NT)
            g, e = logits[:, :, 0:NG], logits[:, :, NG:NG + NE]
            iota32 = C("iota32")

            def first_max(vals, n, m, idx, tmp):
                do(dve.tensor_reduce(m, vals, AX.X, ALU.max))
                do(dve.tensor_tensor(tmp, vals, each(m, NT, n), ALU.is_equal))
                do(dve.scalar_tensor_tensor(tmp, tmp, -64.0, over_rows(iota32, NT, n), ALU.mult, ALU.add))
                do(dve.tensor_reduce(idx, tmp, AX.X, ALU.min))
                do(dve.tensor_scalar(idx, idx, 64.0, None, ALU.add))

            first_max(g, NG, gs[:, 0, :], gs[:, 1, :], grp[:, 0])
            dve.tensor_tensor(grp[:, 1], g, each(gs[:, 0, :], NT, NG), ALU.subtract).then_inc(s_rx, 1)
            do(dve.tensor_tensor(eq[:], over_rows(C("iotag"), NT, NE), each(gs[:, 1, :], NT, NE), ALU.is_equal))
            do(dve.tensor_scalar(eq[:], eq[:], -1.0, BIG, ALU.add, ALU.mult))
            do(dve.tensor_tensor(lem[:], eq[:], e, ALU.add))
            for c in range(2):
                first_max(lem[:], NE, ms[:, c, :], ei[:, c, :], eq[:])
                do(dve.tensor_tensor(hot2[:, c], over_rows(iota32, NT, NE), each(ei[:, c, :], NT, NE), ALU.is_equal))
                if c == 0:
                    do(dve.scalar_tensor_tensor(lem[:], hot2[:, 0], -3.0 * BIG, lem[:], ALU.mult, ALU.add))
            dve.tensor_tensor(gs[:, 2, :], ms[:, 1, :], ms[:, 0, :], ALU.subtract).then_inc(s_rx, 1)
            did(dve.memset(mark[:].bitcast(F32), 0.0))
            do(dve.tensor_tensor(eq[:], hot2[:, 0], hot2[:, 1], ALU.add))
            dve.tensor_tensor(mark[:, 1:NT + 1, :], eq[:], each(C("valid"), NT, NE), ALU.mult).then_inc(s_mark, 1)
            dve.wait_ge(s_re, 4)
            do(dve.tensor_reduce(gs[:, 3, :], grp[:, 2], AX.X, ALU.add))
            do(dve.tensor_scalar(gs[:, 5, :], gs[:, 4, :], 1.0, None, ALU.add))
            do(dve.tensor_tensor(gs[:, 3, :], gs[:, 3, :], gs[:, 5, :], ALU.mult))
            do(dve.reciprocal(gate_w[:, 0, :], gs[:, 3, :]))
            do(dve.tensor_tensor(gate_w[:, 1, :], gate_w[:, 0, :], gs[:, 4, :], ALU.mult))
            dve.wait_ge(s_rank, 1)
            do(dve.tensor_copy(ranks[:], pj[0][:, 0:(NT + 1) * NE].rearrange("p (t e) -> p t e", e=NE)))
            ov = C("over")
            do(dve.tensor_tensor(big2[:, 0, 0:8, :].rearrange("p a b -> p (a b)").rearrange("p (e j) -> p e j", j=8), each(ranks[:, NT, :], NE, 8), over_rows(ov, NE, 8), ALU.is_gt))
            do(dve.tensor_reduce(nxs[:, 0, :], big2[:, 0, 0:8, :].rearrange("p a b -> p (a b)").rearrange("p (e j) -> p e j", j=8), AX.X, ALU.add))
            dve.wait_ge(s_dconst, 64)
            do(dve.tensor_tensor(pre_nx[:], c_pre[:], over_rows(nxs[:, 0, :], NE, NE), ALU.mult))
            do(dve.tensor_reduce(nxs[:, 1, :], pre_nx[:], AX.X, ALU.add))
            do(dve.tensor_tensor(nxs[:, 2, :], nxs[:, 0, :], nxs[:, 1, :], ALU.add))
            for c in range(2):
                did(dve.tensor_tensor(big2[:, c], hot2[:, c], ranks[:, 0:NT, :], ALU.mult))
            settle()
            do(dve.tensor_reduce(rk[:, 0], big2[:], AX.X, ALU.add))
            for c in range(2):
                did(dve.tensor_tensor(big2[:, c], hot2[:, c], over_rows(nxs[:, 1, :], NT, NE), ALU.mult))
            settle()
            do(dve.tensor_reduce(rk[:, 1], big2[:], AX.X, ALU.add))
            flat = [rk[:, i].rearrange("p a b -> p (a b)") for i in range(8)]
            eif = ei[:].rearrange("p a b -> p (a b)")
            N2 = 2 * NT
            do(dve.tensor_tensor(over2[:], each(flat[0], N2, 8), over_rows(ov, N2, 8), ALU.is_ge))
            do(dve.tensor_reduce(flat[2], over2[:], AX.X, ALU.add))
            do(dve.scalar_tensor_tensor(flat[3], flat[2], -float(P), flat[0], ALU.mult, ALU.add))
            do(dve.tensor_tensor(flat[4], flat[1], flat[2], ALU.add))
            do(dve.scalar_tensor_tensor(flat[4], flat[4], float(NE - 1), eif, ALU.add, ALU.subtract))
            do(dve.tensor_scalar(flat[5], flat[2], 1.0, None, ALU.min))
            do(dve.tensor_tensor(flat[4], flat[4], flat[5], ALU.mult))
            do(dve.tensor_tensor(flat[6], flat[4], eif, ALU.add))
            do(dve.scalar_tensor_tensor(flat[7], flat[3], float(MAXB), flat[6], ALU.mult, ALU.add))
            for u in range(0, N2, UC):
                iota = C("iota128")
                do(dve.tensor_tensor(block_hot[:, u:u + UC], over_rows(iota[:, 0:MAXB], UC, MAXB), each(flat[6][:, u:u + UC], UC, MAXB), ALU.is_equal))
                did(dve.tensor_tensor(block_tok[:, u:u + UC], block_hot[:, u:u + UC], each(C("token1")[:, u % NT:u % NT + UC], UC, MAXB), ALU.mult))
                dve.tensor_tensor(place_hot[:, u:u + UC], over_rows(iota, UC, P), each(flat[3][:, u:u + UC], UC, P), ALU.is_equal).then_inc(s_ph, 1)
                dve.wait_ge(s_ph, u // UC + 1)
                settle()
                dve.sem_inc(s_phr, 1)
            dve.wait_ge(s_pm, 1)
            do(dve.tensor_scalar(slot_f[:], pj[1][:, 0:MAXB], 0.0, 4096.0, ALU.is_equal, ALU.mult))
            do(dve.scalar_tensor_tensor(slot_f[:], pj[1][:, 0:MAXB], -1.0, slot_f[:], ALU.add, ALU.add))
            did(dve.tensor_copy(slot_tok[:], slot_f[:]))
            settle()
            dve.sem_inc(s_slots, 1)
            did(dve.tensor_copy(addr[:], flat[7]))
            do(dve.tensor_tensor(xl[:], each(C("iotax"), XB, NE), over_rows(nxs[:, 2, :], XB, NE), ALU.is_ge))
            do(dve.tensor_reduce(xlf[:, 0:XB], xl[:], AX.X, ALU.add))
            do(dve.tensor_scalar(xlf[:, 0:XB], xlf[:, 0:XB], float(NE - 1), None, ALU.min))
            do(dve.tensor_copy(xlf[:, XB:XB + 1], nxs[:, 2, NE - 1:NE]))
            did(dve.tensor_copy(xlist[:], xlf[:]))
            settle()
            dve.sem_inc(s_slots, 1)

        def act_r(act):
            act.wait_ge(s_lge, NT)
            act.activation(beforeR[:], C("before"), ACT.Copy).then_inc(s_re, 1)
            act.activation(onesR[:], C("ones"), ACT.Copy).then_inc(s_re, 1)
            act.wait_ge(s_rx, 1)
            act.activation(grp[:, 2], grp[:, 1], ACT.Exp).then_inc(s_re, 1)
            act_first(act, 0)
            act.wait_ge(s_rx, 2)
            act.activation(gs[:, 4, :], gs[:, 2, :], ACT.Exp).then_inc(s_re, 1)

        def pe_r(pe):
            pe.wait_ge(s_mark, 1)
            pe.wait_ge(s_lge, NT)
            pe.wait_ge(s_re, 2)
            out = pj[0][:, 0:(NT + 1) * NE]
            pe.matmul(out, onesR[:], mark[:, 0:NT + 1, :].rearrange("p t e -> p (t e)"), start=True, stop=False)
            for t in range(NT - 1):
                pe.matmul(out[:, NE * (t + 2):], onesR[:], spread(mark[:, t + 1, :], [[0, NT - 1 - t], [1, NE]]),
                          start=False, stop=False, skip_group_check=True)
            pe.matmul(out, beforeR[:], mark[:, 1:NT + 2, :].rearrange("p t e -> p (t e)"), start=False, stop=True).then_inc(s_rank, 1)
            for u in range(2 * NT):
                if u % UC == 0:
                    pe.wait_ge(s_phr, u // UC + 1)
                ins = pe.matmul(pj[1][:, 0:MAXB], place_hot[:, u, :], block_tok[:, u, :], start=(u == 0), stop=(u == 2 * NT - 1))
            ins.then_inc(s_pm, 1)

        s_er = [sem(f"s_er{i}") for i in range(6)]
        s_hi = [sem(f"s_hi{q}") for q in range(3)]
        s_lo = [sem(f"s_lo{q}") for q in range(3)]
        s_idx = sem("s_idx")
        s_xg = [sem("s_xg0"), sem("s_xg1")]
        s_xt = sem("s_xt")
        s_xthi = sem("s_xthi")
        s_xtlo = sem("s_xtlo")
        s_gu = sem("s_gu")
        s_silu = sem("s_silu")
        s_hh = sem("s_hh")
        s_ht = sem("s_ht")
        s_hthi = sem("s_hthi")
        s_htlo = sem("s_htlo")
        s_dn = sem("s_dn")
        s_y0 = sem("s_y0")
        s_y1 = sem("s_y1")
        s_yst = [sem("s_yst0"), sem("s_yst1")]
        s_ally = sem("s_ally")
        s_turn = sem("s_turn")

        xb = [tp[0], tp[1]]
        gu_bank, ht_bank, dn = pj[2], pj[3], [pj[4], pj[5]]
        y_rows = y_dram.rearrange("(p b) c -> p b c", b=MAXB)

        def later(n, lag):
            return not isinstance(n, int) or n >= lag

        def load_piece(sp, n, m, par, q, expert):
            if later(n, 2):
                sp.wait_ge(s_lo[q], n - 1)
            w = I[("w_gate", "w_up", "w_down")[q]][0]
            if q < 2:
                src = w[bass.ds(expert, 1)].rearrange("a (p k) f -> p (a k f)", p=P)
                dst = e_raw[:, 3 * par + q, :]
            else:
                src = w[bass.ds(expert, 1)].rearrange("a (f p) c -> p (a f) c", p=P)
                dst = e_raw[:, 3 * par + q, :].rearrange("p (f c) -> p f c", f=2)
            sp.dma_start(dst, src).then_inc(s_er[3 * par + q], 16)

        def store_block(sp, n, m, par):
            sp.wait_ge(s_y0, n + 1)
            sp.wait_ge(s_y1, n + 1)
            sp.dma_start(y_rows[:, bass.ds(n, 1), :], yo[:, par:par + 1, :]).then_inc(s_yst[par], 16)

        def gather(pool, n, m, par):
            if later(n, 2):
                pool.wait_ge(s_xt, 2 * n - 2)
            pool.tensor_copy(idx_cur[:, par:par + 1], slot_tok[:, bass.ds(n, 1)]).then_inc(s_idx, 1)
            pool.wait_ge(s_idx, n + 1)
            pool.sem_inc(s_turn, 1)
            pool.indirect_dma_start(xg[:, par, :], None, hn_dram, bass.IndirectOffsetOnAxis(ap=idx_cur[:, par:par + 1], axis=0),
                                    bounds_check=TOK - 1, oob_is_err=False).then_inc(s_xg[par], 16)

        def high(act, n, m, par, q):
            act.wait_ge(s_er[3 * par + q], 16 * (m + 1))
            if later(n, 2):
                act.wait_ge(s_dn if q == 2 else s_gu, n - 1)
            act.activation(e_hi[:, par, q, :], e_raw[:, 3 * par + q, :], ACT.Copy).then_inc(s_hi[q], 1)

        def low(eng, n, m, par, q):
            eng.wait_ge(s_hi[q], n + 1)
            eng.tensor_tensor(e_lo[:, par, q, :], e_raw[:, 3 * par + q, :], e_hi[:, par, q, :].bitcast(F32), ALU.subtract).then_inc(s_lo[q], 1)

        def pe_xt(pe, n, m, par):
            pe.wait_ge(s_xg[par], 16 * (m + 1))
            rows = xg[:, par, :].rearrange("s (p k) -> s k p", k=KC)
            for q in range(2):
                if later(n, 1):
                    pe.wait_ge(s_xtlo, 2 * n + q - 1)
                for c in range(4):
                    ins = pe.transpose(xb[q][:, P * c:P * (c + 1)], rows[:, 4 * q + c, :], C("ident"))
                ins.then_inc(s_xt, 1)

        def act_xt(act, n, m, par):
            for q in range(2):
                act.wait_ge(s_xt, 2 * n + q + 1)
                if later(n, 1) and q == 0:
                    act.wait_ge(s_gu, n)
                act.activation(xT_hi[:, 4 * q:4 * q + 4, :].rearrange("p c t -> p (c t)"), xb[q][:], ACT.Copy).then_inc(s_xthi, 1)

        def dve_xt(dve, n, m, par):
            for q in range(2):
                dve.wait_ge(s_xthi, 2 * n + q + 1)
                dve.tensor_tensor(xT_lo[:, 4 * q:4 * q + 4, :].rearrange("p c t -> p (c t)"), xb[q][:],
                                  xT_hi[:, 4 * q:4 * q + 4, :].rearrange("p c t -> p (c t)").bitcast(F32), ALU.subtract).then_inc(s_xtlo, 1)

        def pe_gu(pe, n, m, par):
            pe.wait_ge(s_xtlo, 2 * n + 2)
            pe.wait_ge(s_lo[0], n + 1)
            pe.wait_ge(s_lo[1], n + 1)
            if later(n, 1):
                pe.wait_ge(s_hh, n)
            for k in range(KC):
                for a, (x, w) in enumerate(((xT_hi, e_hi), (xT_hi, e_lo), (xT_lo, e_hi))):
                    ins = pe.matmul(gu_bank[:].rearrange("p (q f) -> p q f", q=2), x[:, k, :], w[:, par, 0:2, FF * k:FF * (k + 1)],
                                    start=(k == 0 and a == 0), stop=(k == KC - 1 and a == 2))
            ins.then_inc(s_gu, 1)

        def act_silu(act, n, m, par):
            act.wait_ge(s_gu, n + 1)
            if later(n, 1):
                act.wait_ge(s_hh, n)
            act.activation(sg[:], gu_bank[:, 0:FF], ACT.Silu).then_inc(s_silu, 1)

        def dve_mult(dve, n, m, par):
            dve.wait_ge(s_silu, n + 1)
            if later(n, 1):
                dve.wait_ge(s_ht, n)
            dve.tensor_tensor(hh[:], gu_bank[:, FF:2 * FF], sg[:], ALU.mult).then_inc(s_hh, 1)

        def pe_ht(pe, n, m, par):
            pe.wait_ge(s_hh, n + 1)
            if later(n, 1):
                pe.wait_ge(s_htlo, n)
            for f in range(2):
                ins = pe.transpose(ht_bank[:, P * f:P * (f + 1)], hh[:, P * f:P * (f + 1)], C("ident"))
            ins.then_inc(s_ht, 1)

        def act_ht(act, n, m, par):
            act.wait_ge(s_ht, n + 1)
            if later(n, 1):
                act.wait_ge(s_dn, n)
            act.activation(hT_hi[:].rearrange("p f t -> p (f t)"), ht_bank[:, 0:2 * P], ACT.Copy).then_inc(s_hthi, 1)

        def dve_ht(dve, n, m, par):
            dve.wait_ge(s_hthi, n + 1)
            dve.tensor_tensor(hT_lo[:].rearrange("p f t -> p (f t)"), ht_bank[:, 0:2 * P], hT_hi[:].rearrange("p f t -> p (f t)").bitcast(F32),
                              ALU.subtract).then_inc(s_htlo, 1)

        def pe_dn(pe, n, m, par):
            pe.wait_ge(s_htlo, n + 1)
            pe.wait_ge(s_lo[2], n + 1)
            if later(n, 1):
                pe.wait_ge(s_y0, n)
                pe.wait_ge(s_y1, n)
            for f in range(2):
                for a, (x, w) in enumerate(((hT_hi, e_hi), (hT_hi, e_lo), (hT_lo, e_hi))):
                    for b in range(2):
                        o = D * f + 512 * b
                        ins = pe.matmul(dn[b][:], x[:, f, :], w[:, par, 2, o:o + 512], start=(f == 0 and a == 0), stop=(f == 1 and a == 2))
            ins.then_inc(s_dn, 1)

        def y_half(eng, n, m, par, b):
            eng.wait_ge(s_dn, n + 1)
            eng.wait_ge(s_yst[par], 16 * m + 16)
            part = slice(512 * b, 512 * (b + 1))
            if b == 0:
                eng.activation(yo[:, par, part], dn[b][:], ACT.Copy).then_inc(s_y0, 1)
            else:
                eng.tensor_copy(yo[:, par, part], dn[b][:]).then_inc(s_y1, 1)

        def sp_step(sp, B):
            if (b := B(2)):
                load_piece(sp, *b, 0, b[0])
                load_piece(sp, *b, 1, b[0])
            if (b := B(-2)):
                store_block(sp, *b)
            if (b := B(2)):
                load_piece(sp, *b, 2, b[0])

        def pool_step(pool, B):
            if (b := B(1)) and later(b[0], 2):
                low(pool, *b, 1)
            if (b := B(2)):
                gather(pool, *b)

        def act_step(act, B):
            if (b := B(-1)):
                act_ht(act, *b)
            if (b := B(-2)):
                y_half(act, *b, 0)
            if (b := B(0)) and later(b[0], 2):
                high(act, *b, 2)
            if (b := B(1)) and later(b[0], 2):
                high(act, *b, 0)
                high(act, *b, 1)
            if (b := B(0)):
                act_silu(act, *b)
            if (b := B(1)):
                act_xt(act, *b)

        def dve_step(dve, B):
            if (b := B(-1)):
                dve_ht(dve, *b)
            if (b := B(-2)):
                y_half(dve, *b, 1)
            if (b := B(0)) and later(b[0], 1):
                low(dve, *b, 2)
            if (b := B(1)) and later(b[0], 1):
                low(dve, *b, 0)
            if (b := B(0)):
                dve_mult(dve, *b)
            if (b := B(1)):
                dve_xt(dve, *b)

        def pe_step(pe, B):
            if (b := B(0)):
                pe_gu(pe, *b)
            if (b := B(1)):
                pe_xt(pe, *b)
            if (b := B(-1)):
                pe_dn(pe, *b)
            if (b := B(0)):
                pe_ht(pe, *b)

        def run_blocks(eng, step, first):
            def at_block(n):
                return lambda d: (n + d, (n + d) // 2, (n + d) % 2) if 0 <= n + d < NE else None
            for n in range(first, 2):
                step(eng, at_block(n))
            with eng.Fori(1, NE // 2 - 1) as g:
                for par in range(2):
                    step(eng, lambda d: (2 * g + (par + d), g + (par + d) // 2, (par + d) % 2))
            for n in range(NE - 2, NE + 2):
                step(eng, at_block(n))

        def overflow(eng, body):
            eng.wait_ge(s_slots, 2)
            extra = eng.value_load(xlist[0:1, XB:XB + 1], min_val=0, max_val=XB)
            with eng.Fori(0, XB // 2) as g:
                for par in range(2):
                    with eng.If(2 * g + par < extra):
                        body((NE + 2 * g + par, NE // 2 + g, par), g)

        def first_experts(sp):
            for n in range(2):
                for q in range(3):
                    load_piece(sp, n, 0, n, q, n)

        def act_first(act, n):
            if n == 0:
                for w in range(2):
                    act.wait_ge(s_hst[w], 16 * (5 - w))
                    act.wait_ge(s_hnst[w], 16 * (5 - w))
            for q in range(3):
                high(act, n, 0, n, q)

        def pool_first(pool):
            for n, q in ((0, 0), (0, 1), (0, 2), (1, 1)):
                low(pool, n, 0, n, q)

        def sp_m(sp):
            for w in range(2):
                sp.sem_inc(s_yst[w], 16)
            run_blocks(sp, sp_step, 0)

            def body(b, g):
                n, m, par = b
                expert = sp.value_load(xlist[0:1, bass.ds(2 * g + par, 1)], min_val=0, max_val=NE - 1)
                for q in range(3):
                    load_piece(sp, n, m, par, q, expert)
                store_block(sp, n, m, par)
                sp.wait_ge(s_yst[par], 16 * (m + 2))
                sp.sem_inc(s_turn, 1)
            overflow(sp, body)
            for q in range(3):
                sp.wait_ge(s_lo[q], NE)
            final_loads(sp)
            for w in range(2):
                sp.wait_ge(s_yst[w], 16 * (NE // 2 + 1))
            sp.sem_inc(s_ally, 1)

        def pool_m(pool, did):
            pool_first(pool)
            pool.wait_ge(s_pm, 1)
            did(pool.memset(xg[:], 0.0))
            pool.wait_ge(s_slots, 1)
            for w in range(2):
                pool.wait_ge(s_hnst[w], 16 * (5 - w))
            pool.wait_ge(s_pool, did.n[0])
            run_blocks(pool, pool_step, -2)

            def body(b, g):
                gather(pool, *b)
                low(pool, *b, 1)
            overflow(pool, body)

        def act_m(act):
            act_first(act, 1)
            run_blocks(act, act_step, -1)

            def body(b, g):
                for q in range(3):
                    high(act, *b, q)
                act_xt(act, *b)
                act_silu(act, *b)
                act_ht(act, *b)
                y_half(act, *b, 0)
            overflow(act, body)

        def dve_m(dve):
            for q in (0, 2):
                dve.wait_ge(s_lo[q], 1)
            run_blocks(dve, dve_step, -1)

            def body(b, g):
                low(dve, *b, 0)
                low(dve, *b, 2)
                dve_xt(dve, *b)
                dve_mult(dve, *b)
                dve_ht(dve, *b)
                y_half(dve, *b, 1)
            overflow(dve, body)

        def pe_m(pe):
            run_blocks(pe, pe_step, -1)

            def body(b, g):
                pe_xt(pe, *b)
                pe_gu(pe, *b)
                pe_ht(pe, *b)
                pe_dn(pe, *b)
            overflow(pe, body)

        RF = 4
        f_h = at("f_h", [P, RF, D], F32, r_q)
        f_y = at("f_y", [P, RF, 2, D], F32, r_chi)
        f_o = at("f_o", [P, RF, D], F32, r_chi + 4096 * 2 * RF)
        f_junk = at("f_junk", [P, D], F32, r_chi + 4096 * 3 * RF)
        g_fin = at("g_fin", [P, D], F32, r_q + 4096 * RF)
        fst = keep("fst", [P, RF, 4])
        s_fh = [sem(f"s_fh{i}") for i in range(RF)]
        s_fy = [sem(f"s_fy{i}") for i in range(RF)]
        s_fs = sem("s_fs")
        s_fq = sem("s_fq")
        s_fr = sem("s_fr")
        s_fn = sem("s_fn")
        s_fout = s_strip

        def final_loads(sp):
            sp.dma_start(g_fin[:], bass.AP(tensor=I["norm_final"].tensor, offset=0, ap=[[0, P], [1, D]])).then_inc(s_dconst, 16)
            for i in range(RF):
                load_h(sp, i)

        def load_h(sp, i):
            sp.dma_start(f_h[0:ROWS[i], i % RF, :], h_dram[cols(i)]).then_inc(s_fh[i % RF], 16)

        def sp_f(sp):

            def out(i):
                sp.wait_ge(s_fn, i + 1)
                r = i % RF
                y = O["y_prompt"][0]
                if i == 0:
                    sp.dma_start(y[0:P - META], f_o[META:P, r, :]).then_inc(s_fout[r], 16)
                elif i < NT - 1:
                    sp.dma_start(y[P * i - META:P * (i + 1) - META], f_o[:, r, :]).then_inc(s_fout[r], 16)
                else:
                    sp.dma_start(y[P * i - META:SEQ], f_o[0:TAIL, r, :]).then_inc(s_fout[r], 16)
                    sp.dma_start(O["y_sample"].rearrange("b t d -> (b t) d"), f_o[TAIL:TAIL + DEC, r, :]).then_inc(s_fout[r], 16)

            for i in range(NT):
                out(i)
                if i + RF < NT:
                    load_h(sp, i + RF)
            for r in range(RF):
                tiles = len(range(r, NT, RF))
                sp.wait_ge(s_fout[r], 16 * (1 + tiles + (r == (NT - 1) % RF)))
            for s, v in ((s_kout, 48), (s_vout, 48), (s_cout, 48)):
                sp.wait_ge(s, v)

        def pool_f(pool, did):
            pool.wait_ge(s_ally, 1)

            def root(i):
                M = ROWS[i]
                pool.wait_ge(s_fq, i + 1)
                did(pool.tensor_scalar(fst[0:M, i % RF, 1:2], fst[0:M, i % RF, 0:1], 1.0 / D, EPS, ALU.mult, ALU.add))
                pool.wait_ge(s_pool, did.n[0])
                pool.tensor_tensor(fst[0:M, i % RF, 2:3], fst[0:M, i % RF, 1:2], C("mhalf", M)[:, 0:1], ALU.pow).then_inc(s_fr, 1)

            for i in range(NT):
                M = ROWS[i]
                if i >= RF:
                    pool.wait_ge(s_fs, 2 * (i - RF + 1))
                for c in range(2):
                    pool.indirect_dma_start(f_y[0:M, i % RF, c, :], None, y_dram,
                                            bass.IndirectOffsetOnAxis(ap=addr[0:M, NT * c + i:NT * c + i + 1], axis=0)).then_inc(s_fy[i % RF], 16)
                if i >= RF:
                    root(i - RF)
            for i in range(NT - RF, NT):
                root(i)

        def act_f(act):
            act.wait_ge(s_ally, 1)
            for i in range(NT):
                M = ROWS[i]
                act.wait_ge(s_fs, 2 * i + 2)
                if i >= 1:
                    act.wait_ge(s_fq, i)
                act.activation(f_junk[0:M, :], f_o[0:M, i % RF, :], ACT.Square, accum_out=fst[0:M, i % RF, 0:1]).then_inc(s_fq, 1)

        def dve_f(dve, did):
            dve.wait_ge(s_ally, 1)
            dve.wait_ge(s_dconst, 80)

            def norm(i):
                M, r = ROWS[i], i % RF
                dve.wait_ge(s_fr, i + 1)
                dve.scalar_tensor_tensor(f_o[0:M, r, :], f_o[0:M, r, :], fst[0:M, r, 2:3], g_fin[0:M, :], ALU.mult, ALU.mult).then_inc(s_fn, 1)

            for i in range(NT):
                M, r = ROWS[i], i % RF
                dve.wait_ge(s_fh[r], 16 * (i // RF + 1))
                dve.wait_ge(s_fy[r], 32 * (i // RF + 1))
                if i >= RF:
                    dve.wait_ge(s_fout[r], 16 * (i // RF + 1))
                for c in range(2):
                    dve.scalar_tensor_tensor(f_o[0:M, r, :], f_y[0:M, r, c, :], gate_w[0:M, c, i:i + 1], (f_h[0:M, r, :], f_o[0:M, r, :])[c],
                                             ALU.mult, ALU.add).then_inc(s_fs, 1)
                    if c == 0:
                        dve.wait_ge(s_fs, 2 * i + 1)
                if i >= 1:
                    norm(i - 1)
            norm(NT - 1)

        block = ctx.enter_context(nc.Block())

        @block.sync
        def _(sp):
            sync_ab(sp)
            sync_c(sp)
            sync_d(sp)
            sp_m(sp)
            sp_f(sp)

        @block.gpsimd
        def _(pool):
            did = tally(s_pool)
            pool_ab(pool, did)
            pool_d(pool, did)
            pool_m(pool, did)
            pool_f(pool, did)

        @block.scalar
        def _(act):
            act_ab(act)
            act_pages(act)
            act_d(act)
            act_r(act)
            act_m(act)
            act_f(act)

        @block.vector
        def _(dve):
            did = tally(s_step)
            dve_ab(dve, did)
            dve_c(dve, did)
            dve.sem_inc(s_be, 1)
            dve_d(dve, did)
            dve_r(dve, did)
            dve_m(dve)
            dve_f(dve, did)

        @block.tensor
        def _(pe):
            pe_ab(pe)
            pe_c(pe)
            pe_d(pe)
            pe_r(pe)
            pe_m(pe)


_OUTS = {"y_prompt": (1, SEQ, D), "y_sample": (DEC, 1, D), "k_prompt": (1, 1, PROMPT, H, 2, DH), "v_prompt": (1, 1, PROMPT, H, P),
         "conv_prompt": (1, 1, 2, WC), "k_sample": (1, DEC, 1, H, 2, DH), "v_sample": (1, DEC, 1, H, P), "conv_sample": (1, DEC, 2, WC)}


def kernel(**inputs):
    import concourse.bacc as bacc
    from concourse.bass_utils import run_bass_kernel_spmd

    nc = bacc.Bacc("TRN2", target_bir_lowering=False, num_devices=1)
    arrays = {f"in_{k}": np.ascontiguousarray(a) for k, a in inputs.items()}
    ins = {k: nc.dram_tensor(f"in_{k}", arrays[f"in_{k}"].shape, mybir.dt.from_np(arrays[f"in_{k}"].dtype), kind="ExternalInput").ap()
           for k in inputs}
    outs = {k: nc.dram_tensor(f"out_{k}", shape, F32, kind="ExternalOutput").ap() for k, shape in _OUTS.items()}
    step_kernel(nc, ins, outs)
    got = run_bass_kernel_spmd(nc, [arrays], core_ids=[0]).results[0]
    return tuple(got[f"out_{k}"] for k in _OUTS)
```
